# Optimizing a Trainium2 kernel written in Bass

```python
import jax, jax.numpy as jnp
from jax import lax
import numpy as np

D_MODEL = 1024
BATCH = 1
SEQ = 1024
DEPTH = 1

GRID_W = 64
CTX_LEN = 256
MLA_HEADS = 8
QK_NOPE = 128
QK_ROPE = 64
V_DIM = 128
Q_LORA = 384
KV_LORA = 256
ROPE_BASE = 10000.0
ROPE_PAIRS = QK_ROPE // 4
Q_BLOCK = 128
ATTN_SCALE = (QK_NOPE + QK_ROPE) ** -0.5
MLA_WIDTH = MLA_HEADS * V_DIM
ML_HEADS = 4
ML_INNER = 1024
ML_HEAD_DIM = ML_INNER // ML_HEADS
QKV_BLOCK = 4
QKV_NBLK = ML_INNER // QKV_BLOCK
CONV_W = 5
CHUNK = 128
N_EXPERTS = 16
EXPERT_FF = 1024
CAP_FACTOR = 2
EPS = 1e-6
IN_SIZES = (Q_LORA, KV_LORA, QK_ROPE, ML_INNER, ML_INNER, D_MODEL, D_MODEL)
IN_DIM = Q_LORA + KV_LORA + QK_ROPE + 2 * ML_INNER + 2 * D_MODEL


def rmsnorm(x, g):
    xf = x.astype(jnp.float32)
    y = xf * lax.rsqrt(jnp.mean(xf * xf, axis=-1, keepdims=True) + EPS)
    return (y * g.astype(jnp.float32)).astype(x.dtype)

def modulate(h, shift, scale):
    return h * (1 + scale[:, None, :]) + shift[:, None, :]

def axial_angles(T):
    rows = T // GRID_W
    row = jnp.repeat(jnp.arange(rows, dtype=jnp.float32), GRID_W)
    col = jnp.tile(jnp.arange(GRID_W, dtype=jnp.float32), rows)
    inv = ROPE_BASE ** (-jnp.arange(ROPE_PAIRS, dtype=jnp.float32) / ROPE_PAIRS)
    return row[:, None] * inv, col[:, None] * inv

def rotate(x, ang):
    cos = jnp.cos(ang)[None, :, None, :]
    sin = jnp.sin(ang)[None, :, None, :]
    xf = x.astype(jnp.float32)
    x1, x2 = xf[..., :ROPE_PAIRS], xf[..., ROPE_PAIRS:]
    return jnp.concatenate([x1 * cos - x2 * sin, x2 * cos + x1 * sin], -1).astype(x.dtype)

def rope_2d(x, ang_row, ang_col):
    half = QK_ROPE // 2
    return jnp.concatenate([rotate(x[..., :half], ang_row), rotate(x[..., half:], ang_col)], -1)

def mla_qkv(q_lat, kv_lat, k_rope, q_norm, w_uq, kv_norm, w_ukv, angles):
    B, T, _ = q_lat.shape
    q = (rmsnorm(q_lat, q_norm) @ w_uq).reshape(B, T, MLA_HEADS, QK_NOPE + QK_ROPE)
    kv = (rmsnorm(kv_lat, kv_norm) @ w_ukv).reshape(B, T, MLA_HEADS, QK_NOPE + V_DIM)
    q_nope, q_pe = q[..., :QK_NOPE], q[..., QK_NOPE:]
    k_nope, v = kv[..., :QK_NOPE], kv[..., QK_NOPE:]
    k_pe = k_rope[:, :, None, :]
    if angles is not None:
        q_pe = rope_2d(q_pe, *angles)
        k_pe = rope_2d(k_pe, *angles)
    k_pe = jnp.broadcast_to(k_pe, (B, T, MLA_HEADS, QK_ROPE))
    return (jnp.concatenate([q_nope, q_pe], -1), jnp.concatenate([k_nope, k_pe], -1), v)

def attend(q, k, v):
    B, Tq, H, Dk = q.shape
    nb = Tq // Q_BLOCK
    qb = q.reshape(B, nb, Q_BLOCK, H, Dk).transpose(1, 0, 2, 3, 4)

    def one_block(qi):
        s = jnp.einsum('bqhd,bkhd->bhqk', qi, k).astype(jnp.float32) * ATTN_SCALE
        p = jax.nn.softmax(s, axis=-1).astype(v.dtype)
        return jnp.einsum('bhqk,bkhd->bqhd', p, v)

    o = lax.map(one_block, qb)
    return o.transpose(1, 0, 2, 3, 4).reshape(B, Tq, H * v.shape[-1])

def dwconv(x, w, b):
    out = lax.conv_general_dilated(x, w[:, None, :].astype(x.dtype), (1,), [(CONV_W // 2, CONV_W // 2)],
                                   dimension_numbers=('NWC', 'WIO', 'NWC'), feature_group_count=x.shape[-1])
    return out + b

def blockdiag(x, w):
    B, T, _ = x.shape
    y = jnp.einsum('btnj,njk->btnk', x.reshape(B, T, QKV_NBLK, QKV_BLOCK), w)
    return y.reshape(B, T, ML_INNER)

def mlstm_features(x_m, conv_w, conv_b, w_qblk, w_kblk, w_vblk, w_gate, b_gate):
    B, T, _ = x_m.shape
    x_c = jax.nn.silu(dwconv(x_m, conv_w, conv_b))
    q = blockdiag(x_c, w_qblk)
    k = blockdiag(x_c, w_kblk)
    v = blockdiag(x_m, w_vblk)
    gates = (jnp.concatenate([q, k, v], -1) @ w_gate + b_gate).reshape(B, T, 2, 2, ML_HEADS)
    gates = gates.astype(jnp.float32).transpose(2, 3, 0, 4, 1)
    heads = lambda a: a.reshape(B, T, ML_HEADS, ML_HEAD_DIM).transpose(0, 2, 1, 3).astype(jnp.float32)
    return heads(q), heads(k) * (ML_HEAD_DIM ** -0.5), heads(v), gates, x_c

def mlstm_chunkwise(q, k, v, ig, lf, state):
    B, H, T, dh = q.shape
    nc = T // CHUNK
    ch = lambda a: jnp.moveaxis(a.reshape(B, H, nc, CHUNK, *a.shape[3:]), 2, 0)
    mask = jnp.tril(jnp.ones((CHUNK, CHUNK), dtype=bool))

    def step(carry, xs):
        C, n, m = carry
        qc, kc, vc, ic, fc = xs
        b = jnp.cumsum(fc, axis=-1)
        dmat = jnp.where(mask, b[..., :, None] - b[..., None, :] + ic[..., None, :], -jnp.inf)
        inter = b + m[..., None]
        m_t = jnp.maximum(inter, jnp.max(dmat, axis=-1))
        w_inter = jnp.exp(inter - m_t)
        s = jnp.einsum('bhtd,bhsd->bhts', qc, kc) * jnp.exp(dmat - m_t[..., None])
        num = jnp.einsum('bhts,bhsd->bhtd', s, vc) + w_inter[..., None] * jnp.einsum('bhvd,bhtd->bhtv', C, qc)
        den = jnp.sum(s, axis=-1) + w_inter * jnp.einsum('bhd,bhtd->bht', n, qc)
        h = num / jnp.maximum(jnp.abs(den), jnp.exp(-m_t))[..., None]
        b_last = b[..., -1]
        dec = b_last[..., None] - b + ic
        m_new = jnp.maximum(b_last + m, jnp.max(dec, axis=-1))
        wk = jnp.exp(dec - m_new[..., None])
        keep = jnp.exp(b_last + m - m_new)
        C_new = keep[..., None, None] * C + jnp.einsum('bhsv,bhsd->bhvd', vc * wk[..., None], kc)
        n_new = keep[..., None] * n + jnp.einsum('bhs,bhsd->bhd', wk, kc)
        return (C_new, n_new, m_new), h

    state, hs = lax.scan(step, state, (ch(q), ch(k), ch(v), ch(ig), ch(lf)))
    return jnp.moveaxis(hs, 0, 2).reshape(B, H, T, dh), state

def mlstm_bidir(feat_c, feat_l):
    qc, kc, vc, gc = feat_c
    ql, kl, vl, gl = feat_l
    B, H, _, dh = qc.shape
    zero = (jnp.zeros((B, H, dh, dh), jnp.float32), jnp.zeros((B, H, dh), jnp.float32),
            jnp.zeros((B, H), jnp.float32))
    lsig = jax.nn.log_sigmoid
    flip = lambda a: jnp.flip(a, axis=2)
    hc_f, st_f = mlstm_chunkwise(qc, kc, vc, gc[0, 0], lsig(gc[0, 1]), zero)
    hl_f, _ = mlstm_chunkwise(ql, kl, vl, gl[0, 0], lsig(gl[0, 1]), st_f)
    hc_b, st_b = mlstm_chunkwise(flip(qc), flip(kc), flip(vc), flip(gc[1, 0]), lsig(flip(gc[1, 1])), zero)
    hl_b, _ = mlstm_chunkwise(flip(ql), flip(kl), flip(vl), flip(gl[1, 0]), lsig(flip(gl[1, 1])), st_b)
    return hc_f + flip(hc_b), hl_f + flip(hl_b)

def mlstm_readout(h, z, x_c, ml_norm, ml_skip):
    B, H, T, dh = h.shape
    hf = h.transpose(0, 2, 1, 3)
    hn = hf * lax.rsqrt(jnp.mean(hf * hf, axis=-1, keepdims=True) + EPS)
    hn = hn.reshape(B, T, ML_INNER).astype(z.dtype) * ml_norm
    return jax.nn.sigmoid(z) * (hn + ml_skip * x_c)

def merge(y_mla, y_ml, g_mla, g_ml, w_out):
    return (jax.nn.sigmoid(g_mla) * y_mla + jax.nn.sigmoid(g_ml) * y_ml) @ w_out

def mixer(h_c, h_l, angles, last, w_in, q_norm, w_uq, kv_norm, w_ukv, conv_w, conv_b,
          w_qblk, w_kblk, w_vblk, w_gate, b_gate, ml_norm, ml_skip, w_out):
    splits = [int(s) for s in np.cumsum(IN_SIZES)[:-1]]
    qlat_c, kvlat_c, krope_c, xm_c, z_c, gmla_c, gml_c = jnp.split(h_c @ w_in, splits, axis=-1)
    qlat_l, kvlat_l, krope_l, xm_l, z_l, gmla_l, gml_l = jnp.split(h_l @ w_in, splits, axis=-1)
    q_c, k_c, v_c = mla_qkv(qlat_c, kvlat_c, krope_c, q_norm, w_uq, kv_norm, w_ukv, None)
    q_l, k_l, v_l = mla_qkv(qlat_l, kvlat_l, krope_l, q_norm, w_uq, kv_norm, w_ukv, angles)
    y_mla_l = attend(q_l, jnp.concatenate([k_c, k_l], 1), jnp.concatenate([v_c, v_l], 1))
    fc = mlstm_features(xm_c, conv_w, conv_b, w_qblk, w_kblk, w_vblk, w_gate, b_gate)
    fl = mlstm_features(xm_l, conv_w, conv_b, w_qblk, w_kblk, w_vblk, w_gate, b_gate)
    hc, hl = mlstm_bidir(fc[:4], fl[:4])
    out_l = merge(y_mla_l, mlstm_readout(hl, z_l, fl[4], ml_norm, ml_skip), gmla_l, gml_l, w_out)
    if last:
        return None, out_l
    y_mla_c = attend(q_c, k_c, v_c)
    out_c = merge(y_mla_c, mlstm_readout(hc, z_c, fc[4], ml_norm, ml_skip), gmla_c, gml_c, w_out)
    return out_c, out_l

def ec_moe(x, w_router, w_e_gate, w_e_up, w_e_down):
    B, T, D = x.shape
    cap = CAP_FACTOR * T // N_EXPERTS
    aff = jax.nn.softmax((x @ w_router).astype(jnp.float32), axis=-1)
    g, idx = lax.top_k(aff.transpose(0, 2, 1), cap)
    xs = jax.vmap(lambda xb, ib: xb[ib])(x, idx)
    a = jnp.einsum('becd,edf->becf', xs, w_e_gate)
    u = jnp.einsum('becd,edf->becf', xs, w_e_up)
    y = jnp.einsum('becf,efd->becd', jax.nn.silu(a) * u, w_e_down) * g[..., None].astype(x.dtype)
    return jax.vmap(lambda yb, ib: jnp.zeros((T, D), x.dtype).at[ib.reshape(-1)].add(yb.reshape(-1, D)))(y, idx)

def first_inputs(seed: int = 0) -> dict:
    key = jax.random.key(seed)
    ks = jax.random.split(key, 32)
    f32 = jnp.float32
    nrm = lambda k, shape, fan: jax.random.normal(k, shape, f32) * (fan ** -0.5)
    gain = lambda k, shape: 1.0 + 0.02 * jax.random.normal(k, shape, f32)
    L, D = DEPTH, D_MODEL
    b_gate = (0.1 * jax.random.normal(ks[16], (L, 2, 2, ML_HEADS), f32)
              + jnp.array([0.0, 3.0], f32)[None, None, :, None]).reshape(L, 4 * ML_HEADS)
    return {
        "x": jax.random.normal(ks[0], (BATCH, SEQ, D), f32),
        "c": jax.random.normal(ks[1], (BATCH, D), f32),
        "ctx": jax.random.normal(ks[2], (BATCH, CTX_LEN, D), f32),
        "c_ctx": jax.random.normal(ks[3], (D,), f32),
        "w_mod": nrm(ks[4], (L, D, 6 * D), D) * 0.5,
        "b_mod": 0.02 * jax.random.normal(ks[5], (L, 6 * D), f32),
        "norm1": gain(ks[6], (L, D)),
        "w_in": nrm(ks[7], (L, D, IN_DIM), D),
        "q_norm": gain(ks[8], (L, Q_LORA)),
        "w_uq": nrm(ks[9], (L, Q_LORA, MLA_HEADS * (QK_NOPE + QK_ROPE)), Q_LORA),
        "kv_norm": gain(ks[10], (L, KV_LORA)),
        "w_ukv": nrm(ks[11], (L, KV_LORA, MLA_HEADS * (QK_NOPE + V_DIM)), KV_LORA),
        "conv_w": nrm(ks[12], (L, CONV_W, ML_INNER), CONV_W),
        "conv_b": 0.02 * jax.random.normal(ks[13], (L, ML_INNER), f32),
        "w_qblk": nrm(ks[14], (L, QKV_NBLK, QKV_BLOCK, QKV_BLOCK), QKV_BLOCK),
        "w_kblk": nrm(ks[15], (L, QKV_NBLK, QKV_BLOCK, QKV_BLOCK), QKV_BLOCK),
        "w_vblk": nrm(ks[17], (L, QKV_NBLK, QKV_BLOCK, QKV_BLOCK), QKV_BLOCK),
        "w_gate": nrm(ks[18], (L, 3 * ML_INNER, 4 * ML_HEADS), 3 * ML_INNER) * 0.5,
        "b_gate": b_gate,
        "ml_norm": gain(ks[19], (L, ML_INNER)),
        "ml_skip": gain(ks[20], (L, ML_INNER)),
        "w_out": nrm(ks[21], (L, D, D), D),
        "norm2": gain(ks[22], (L, D)),
        "w_router": nrm(ks[23], (L, D, N_EXPERTS), D),
        "w_e_gate": nrm(ks[24], (L, N_EXPERTS, D, EXPERT_FF), D),
        "w_e_up": nrm(ks[25], (L, N_EXPERTS, D, EXPERT_FF), D),
        "w_e_down": nrm(ks[26], (L, N_EXPERTS, EXPERT_FF, D), EXPERT_FF),
        "final_norm": gain(ks[27], (D,)),
    }

def first_block(x, c, ctx, c_ctx, w_mod, b_mod, norm1, w_in, q_norm, w_uq, kv_norm, w_ukv, conv_w, conv_b,
              w_qblk, w_kblk, w_vblk, w_gate, b_gate, ml_norm, ml_skip, w_out, norm2, w_router,
              w_e_gate, w_e_up, w_e_down, final_norm):
    angles = axial_angles(x.shape[1])
    for l in range(DEPTH):
        last = l == DEPTH - 1
        mod_l = jax.nn.silu(c) @ w_mod[l] + b_mod[l]
        mod_c = jax.nn.silu(c_ctx)[None, :] @ w_mod[l] + b_mod[l]
        sh1, sc1, g1, sh2, sc2, g2 = jnp.split(mod_l, 6, axis=-1)
        sh1c, sc1c, g1c, sh2c, sc2c, g2c = jnp.split(mod_c, 6, axis=-1)
        h_l = modulate(rmsnorm(x, norm1[l]), sh1, sc1)
        h_c = modulate(rmsnorm(ctx, norm1[l]), sh1c, sc1c)
        out_c, out_l = mixer(h_c, h_l, angles, last, w_in[l], q_norm[l], w_uq[l], kv_norm[l], w_ukv[l],
                             conv_w[l], conv_b[l], w_qblk[l], w_kblk[l], w_vblk[l], w_gate[l], b_gate[l],
                             ml_norm[l], ml_skip[l], w_out[l])
        x = x + g1[:, None, :] * out_l
        h_l = modulate(rmsnorm(x, norm2[l]), sh2, sc2)
        x = x + g2[:, None, :] * ec_moe(h_l, w_router[l], w_e_gate[l], w_e_up[l], w_e_down[l])
        if not last:
            ctx = ctx + g1c[:, None, :] * out_c
            h_c = modulate(rmsnorm(ctx, norm2[l]), sh2c, sc2c)
            ctx = ctx + g2c[:, None, :] * ec_moe(h_c, w_router[l], w_e_gate[l], w_e_up[l], w_e_down[l])
    return rmsnorm(x, final_norm)


DEPTH_2 = 2

D_MIX = D_MODEL
W_F = D_MIX // 4
W_ATT = D_MIX // 4
W_CONV = D_MIX // 4
W_POOL = D_MIX // 4
HEAD_DIM = 64
N_HEADS = W_ATT // HEAD_DIM
N_KV_HEADS = N_HEADS // 2
GQA = N_HEADS // N_KV_HEADS
KV_DIM = N_KV_HEADS * HEAD_DIM
ATT_SCALE = HEAD_DIM ** -0.5
ROPE_FREQS = HEAD_DIM // 4
ROPE_THETA = 10000.0
F_HEADS = 4
F_DIM = W_F // F_HEADS
CONV_W_2 = 3
POOL_WINDOWS = (2, 4, 8, 16)
POOL_DIM = W_POOL // len(POOL_WINDOWS)
SPLIT_WIDTHS = (W_ATT, KV_DIM, KV_DIM, W_ATT, W_F, W_F, W_CONV, W_CONV, W_CONV, W_CONV, W_POOL, W_POOL)
D_IN = sum(SPLIT_WIDTHS)


def _split_cols(p):
    return jnp.split(p, np.cumsum(SPLIT_WIDTHS)[:-1].tolist(), axis=-1)

def _rmsnorm(x, g):
    xf = x.astype(jnp.float32)
    y = xf * lax.rsqrt(jnp.mean(xf * xf, axis=-1, keepdims=True) + EPS)
    return (y * g.astype(jnp.float32)).astype(x.dtype)

def _axial_angles(n):
    n_rows = n // GRID_W
    row = jnp.repeat(jnp.arange(n_rows), GRID_W).astype(jnp.float32)
    col = jnp.tile(jnp.arange(GRID_W), n_rows).astype(jnp.float32)
    inv = ROPE_THETA ** (-jnp.arange(ROPE_FREQS, dtype=jnp.float32) / ROPE_FREQS)
    return row[:, None] * inv, col[:, None] * inv

def _rotate(x, ang):
    f = ang.shape[-1]
    cos = jnp.cos(ang)[None, :, None, :].astype(x.dtype)
    sin = jnp.sin(ang)[None, :, None, :].astype(x.dtype)
    x1, x2 = x[..., :f], x[..., f:]
    return jnp.concatenate([x1 * cos - x2 * sin, x2 * cos + x1 * sin], axis=-1)

def _axial_rope(x, ang_row, ang_col):
    half = HEAD_DIM // 2
    return jnp.concatenate([_rotate(x[..., :half], ang_row), _rotate(x[..., half:], ang_col)], axis=-1)

def _latent_attention(q, k, v, kc, vc):
    b, s = q.shape[0], q.shape[1]
    nblk = s // Q_BLOCK
    k_all = jnp.concatenate([kc, k], axis=1)
    v_all = jnp.concatenate([vc, v], axis=1)
    qb = q.reshape(b, nblk, Q_BLOCK, N_KV_HEADS, GQA, HEAD_DIM).transpose(1, 0, 2, 3, 4, 5)

    def one_block(qi):
        sc = jnp.einsum('bqkgd,bskd->bkgqs', qi, k_all, preferred_element_type=jnp.float32)
        p = jax.nn.softmax(sc, axis=-1).astype(v_all.dtype)
        return jnp.einsum('bkgqs,bskd->bqkgd', p, v_all)

    o = lax.map(one_block, qb)
    return o.transpose(1, 0, 2, 3, 4, 5).reshape(b, s, W_ATT)

def _context_attention(qc, kc, vc):
    b, n = qc.shape[0], qc.shape[1]
    qg = qc.reshape(b, n, N_KV_HEADS, GQA, HEAD_DIM)
    sc = jnp.einsum('bqkgd,bskd->bkgqs', qg, kc, preferred_element_type=jnp.float32)
    p = jax.nn.softmax(sc, axis=-1).astype(vc.dtype)
    return jnp.einsum('bkgqs,bskd->bqkgd', p, vc).reshape(b, n, W_ATT)

def _fourier_branch(u, z, w_fourier):
    b, n, _ = u.shape
    uf = u.astype(jnp.float32).reshape(b, n, F_HEADS, F_DIM)
    y = jnp.fft.fftn(uf, axes=(1, 3), norm='ortho').real.reshape(b, n, W_F).astype(u.dtype)
    return jax.nn.silu(z) * (y @ w_fourier)

def _conv_branch(bg, cg, hv, z, conv_w, conv_b):
    t = cg * hv
    tp = jnp.pad(t, ((0, 0), (1, 1), (0, 0)))
    y = tp[:, :-2] * conv_w[0] + tp[:, 1:-1] * conv_w[1] + tp[:, 2:] * conv_w[2] + conv_b
    return jax.nn.silu(z) * (bg * y)

def _pool_branch(u, z, pool_w, pool_scale):
    b, n, _ = u.shape
    cs = jnp.cumsum(u.astype(jnp.float32), axis=1)
    cs = jnp.concatenate([jnp.zeros((b, 1, W_POOL), jnp.float32), cs], axis=1)
    pos = jnp.arange(n)
    outs = []
    for i, w in enumerate(POOL_WINDOWS):
        left = w // 2
        right = w - 1 - left
        lo = jnp.clip(pos - left, 0, n)
        hi = jnp.clip(pos + right + 1, 0, n)
        sl = slice(i * POOL_DIM, (i + 1) * POOL_DIM)
        mean = (cs[:, hi, sl] - cs[:, lo, sl]) / (hi - lo).astype(jnp.float32)[None, :, None]
        d = (mean - u[..., sl].astype(jnp.float32)).astype(u.dtype)
        outs.append(d @ pool_w[i])
    y = jnp.concatenate(outs, axis=-1) * pool_scale
    return jax.nn.silu(z) * y

def _local_branches(parts, w_fourier, conv_w, conv_b, pool_w, pool_scale):
    _, _, _, _, u_f, z_f, b_c, c_c, h_c, z_c, u_p, z_p = parts
    o_f = _fourier_branch(u_f, z_f, w_fourier)
    o_c = _conv_branch(b_c, c_c, h_c, z_c, conv_w, conv_b)
    o_p = _pool_branch(u_p, z_p, pool_w, pool_scale)
    return o_f, o_c, o_p

def _layer(x, xc, c, c_ctx, ang_row, ang_col, w_mod, b_mod, norm_g, w_in, q_gain, k_gain,
           w_fourier, conv_w, conv_b, pool_w, pool_scale, w_out, ctx_out):
    b, s, _ = x.shape
    n_ctx = xc.shape[1]
    shift, scale, gate = jnp.split(jax.nn.silu(c) @ w_mod + b_mod, 3, axis=-1)
    shift_c, scale_c, gate_c = jnp.split(jax.nn.silu(c_ctx) @ w_mod + b_mod, 3, axis=-1)
    h = _rmsnorm(x, norm_g) * (1.0 + scale[:, None]) + shift[:, None]
    hc = _rmsnorm(xc, norm_g) * (1.0 + scale_c) + shift_c

    parts = _split_cols(h @ w_in)
    if ctx_out:
        parts_c = _split_cols(hc @ w_in)
        kc_raw, vc_raw = parts_c[1], parts_c[2]
    else:
        kc_raw, vc_raw = jnp.split(hc @ w_in[:, W_ATT:W_ATT + 2 * KV_DIM], 2, axis=-1)
    kc = _rmsnorm(kc_raw.reshape(b, n_ctx, N_KV_HEADS, HEAD_DIM), k_gain)
    vc = vc_raw.reshape(b, n_ctx, N_KV_HEADS, HEAD_DIM)

    q = _rmsnorm(parts[0].reshape(b, s, N_HEADS, HEAD_DIM), q_gain)
    k = _rmsnorm(parts[1].reshape(b, s, N_KV_HEADS, HEAD_DIM), k_gain)
    v = parts[2].reshape(b, s, N_KV_HEADS, HEAD_DIM)
    q = _axial_rope(q, ang_row, ang_col) * ATT_SCALE
    k = _axial_rope(k, ang_row, ang_col)
    o_att = jax.nn.silu(parts[3]) * _latent_attention(q, k, v, kc, vc)
    o_f, o_c, o_p = _local_branches(parts, w_fourier, conv_w, conv_b, pool_w, pool_scale)
    out = jnp.concatenate([o_f, o_att, o_c, o_p], axis=-1) @ w_out
    x_new = x + gate[:, None] * out

    if ctx_out:
        qc = _rmsnorm(parts_c[0].reshape(b, n_ctx, N_HEADS, HEAD_DIM), q_gain) * ATT_SCALE
        oc_att = jax.nn.silu(parts_c[3]) * _context_attention(qc, kc, vc)
        oc_f, oc_c, oc_p = _local_branches(parts_c, w_fourier, conv_w, conv_b, pool_w, pool_scale)
        out_c = jnp.concatenate([oc_f, oc_att, oc_c, oc_p], axis=-1) @ w_out
        xc = xc + gate_c * out_c
    return x_new, xc

def second_inputs(seed: int = 0) -> dict:
    key = jax.random.key(seed)
    ks = jax.random.split(key, 20)
    f32 = jnp.float32
    nrm = lambda k, shape: jax.random.normal(k, shape, f32)
    return {
        "x": nrm(ks[0], (BATCH, SEQ, D_MODEL)),
        "c": nrm(ks[1], (BATCH, D_MODEL)),
        "ctx": nrm(ks[2], (BATCH, CTX_LEN, D_MODEL)),
        "c_ctx": nrm(ks[3], (D_MODEL,)),
        "w_mod": nrm(ks[4], (DEPTH_2, D_MODEL, 3 * D_MODEL)) * (0.5 * D_MODEL ** -0.5),
        "b_mod": nrm(ks[5], (DEPTH_2, 3 * D_MODEL)) * 0.02,
        "norm_g": 1.0 + 0.05 * nrm(ks[6], (DEPTH_2, D_MODEL)),
        "w_in": nrm(ks[7], (DEPTH_2, D_MODEL, D_IN)) * D_MODEL ** -0.5,
        "q_gain": 1.0 + 0.05 * nrm(ks[8], (DEPTH_2, HEAD_DIM)),
        "k_gain": 1.0 + 0.05 * nrm(ks[9], (DEPTH_2, HEAD_DIM)),
        "w_fourier": nrm(ks[10], (DEPTH_2, W_F, W_F)) * W_F ** -0.5,
        "conv_w": nrm(ks[11], (DEPTH_2, CONV_W_2, W_CONV)) * CONV_W_2 ** -0.5,
        "conv_b": nrm(ks[12], (DEPTH_2, W_CONV)) * 0.02,
        "pool_w": nrm(ks[13], (DEPTH_2, len(POOL_WINDOWS), POOL_DIM, POOL_DIM)) * POOL_DIM ** -0.5,
        "pool_scale": 1.0 + 0.1 * nrm(ks[14], (DEPTH_2, W_POOL)),
        "w_out": nrm(ks[15], (DEPTH_2, D_MIX, D_MODEL)) * D_MIX ** -0.5,
    }

def second_block(x, c, ctx, c_ctx, w_mod, b_mod, norm_g, w_in, q_gain, k_gain,
              w_fourier, conv_w, conv_b, pool_w, pool_scale, w_out):
    ang_row, ang_col = _axial_angles(x.shape[1])
    xc = ctx
    for l in range(DEPTH_2):
        x, xc = _layer(x, xc, c, c_ctx, ang_row, ang_col, w_mod[l], b_mod[l], norm_g[l], w_in[l],
                       q_gain[l], k_gain[l], w_fourier[l], conv_w[l], conv_b[l], pool_w[l],
                       pool_scale[l], w_out[l], ctx_out=(l < DEPTH_2 - 1))
    return x


def setup_inputs(seed=0):
    out = dict(first_inputs(seed))
    for name, value in second_inputs(seed + 1).items():
        if name != "x":
            out[name + "_2"] = value
    return out


def reference(
    x, c, ctx, c_ctx, w_mod, b_mod, norm1, w_in, q_norm, w_uq, kv_norm, w_ukv, conv_w, conv_b,
    w_qblk, w_kblk, w_vblk, w_gate, b_gate, ml_norm, ml_skip, w_out, norm2, w_router, w_e_gate,
    w_e_up, w_e_down, final_norm, c_2, ctx_2, c_ctx_2, w_mod_2, b_mod_2, norm_g_2, w_in_2,
    q_gain_2, k_gain_2, w_fourier_2, conv_w_2, conv_b_2, pool_w_2, pool_scale_2, w_out_2,
):
    x = first_block(
        x, c, ctx, c_ctx, w_mod, b_mod, norm1, w_in, q_norm, w_uq, kv_norm, w_ukv, conv_w,
        conv_b, w_qblk, w_kblk, w_vblk, w_gate, b_gate, ml_norm, ml_skip, w_out, norm2,
        w_router, w_e_gate, w_e_up, w_e_down, final_norm,
    )
    return second_block(
        x, c_2, ctx_2, c_ctx_2, w_mod_2, b_mod_2, norm_g_2, w_in_2, q_gain_2, k_gain_2,
        w_fourier_2, conv_w_2, conv_b_2, pool_w_2, pool_scale_2, w_out_2,
    )


_drawn_inputs = setup_inputs


def setup_inputs(seed=0):
    import zlib

    import numpy as np

    out = dict(_drawn_inputs(seed))
    spreads = {}
    factors = {'ctx': 5.923,
     'c_ctx': 4.805,
     'b_mod': 3.984,
     'norm1': 8.0,
     'q_norm': 8.0,
     'w_uq': 4.228,
     'kv_norm': 8.0,
     'conv_b': 8.0,
     'ml_norm': 8.0,
     'ml_skip': 8.0,
     'norm2': 8.0,
     'final_norm': 2.93,
     'ctx_2': 8.0,
     'c_ctx_2': 6.458,
     'b_mod_2': 2.769,
     'q_gain_2': 23.506,
     'k_gain_2': 23.594,
     'conv_b_2': 42.648,
     'pool_scale_2': 10.571}
    for name, (base, spread) in spreads.items():
        noise = np.random.default_rng([zlib.crc32(name.encode()), seed]).standard_normal(out[name].shape)
        drawn = base * np.exp(spread * noise) if base else spread * noise
        out[name] = __import__('jax').numpy.asarray(drawn.astype(out[name].dtype))
    for name, factor in factors.items():
        out[name] = (out[name] * factor).astype(out[name].dtype)
    return out
```

```python
from contextlib import ExitStack

import numpy as np

import concourse.bass as bass
from concourse import mybir

F32 = mybir.dt.float32
FR = mybir.dt.float32r
I32 = mybir.dt.int32
U32 = mybir.dt.uint32
ALU = mybir.AluOpType
ACT = mybir.ActivationFunctionType
AX = mybir.AxisListType
ds = bass.ds

P = 128
BANK = 512
D = 1024
KD = D // P
N_LAT, N_CTX = 1024, 256
N_ALL = N_CTX + N_LAT
LT, CT = N_LAT // P, N_CTX // P
NT = LT + CT
EPS = 1e-6
LAT_CHUNKS = [(256, 512), (768, 512)]
ALL_CHUNKS = LAT_CHUNKS + [(0, 256)]

HEADS, NOPE, ROPE, VD = 8, 128, 64, 128
QL, KL = 384 // P, 256 // P
QK = NOPE + ROPE
ATT_SCALE = QK ** -0.5
COL_KV, COL_KR, COL_XM = 384, 640, 704
COL_Z, COL_GMLA, COL_GML = 1728, 2752, 3776
ML_HEADS, DH = 4, 256
TAPS = 5
N_EXP, FF = 16, 1024
CAP = 2 * N_LAT // N_EXP
FT = FF // P

PA_NORM1, PA_QN, PA_KVN, PA_CB, PA_MLN, PA_SKIP, PA_CW = 0, 8, 11, 13, 21, 29, 37
PB_C, PB_NORM, PB_PS, PB_CB, PB_CW, PB_QG, PB_KG = 0, 32, 48, 52, 56, 68, 70

D_IN2 = 2816
H2, KVH, HD = 4, 2, 64
ATT2_SCALE = HD ** -0.5
T_Q, T_K, T_V, T_ZA, T_UF, T_ZF, T_B, T_C, T_H, T_ZC, T_UP, T_ZP = 0, 2, 3, 4, 6, 8, 10, 12, 14, 16, 18, 20


def tables():
    f = np.float32
    out = {"ident": np.eye(P, dtype=f), "rev": np.ascontiguousarray(np.eye(P, dtype=f)[::-1])}
    s, t = np.arange(P)[:, None], np.arange(P)[None, :]
    out["causal"] = np.stack([np.where(s <= t, 0, 1e30), np.where(s >= t, 0, 1e30)]).astype(f)
    out["block4"] = (s // 4 == t // 4).astype(f)
    out["block64"] = (s // 64 == t // 64).astype(f)
    rot = np.zeros((P, P), f)
    for j in range(P):
        if j % 32 < 16:
            rot[j + 16, j] = -1
        else:
            rot[j - 16, j] = 1
    out["rot"] = rot
    pos = np.arange(N_LAT)
    inv = (10000.0 ** (-np.arange(16, dtype=f) / f(16))).astype(f)
    ang = np.zeros((P, N_LAT), f)
    for j in range(P):
        base = (pos // 64 if (j % 64) < 32 else pos % 64).astype(f)
        ang[j] = base * inv[j % 16]
    out["cos"], out["sin"] = np.cos(ang).astype(f), np.sin(ang).astype(f)
    for n, name in ((N_LAT, "lat"), (N_CTX, "ctx")):
        k = (np.arange(n)[:, None] * np.arange(n)[None, :]) % n
        out["dft_" + name] = np.stack([np.cos(2 * np.pi * k / n), np.sin(2 * np.pi * k / n)]).astype(f)
        d = (np.arange(64)[:, None] * np.arange(64)[None, :]) % 64
        norm = 1.0 / np.sqrt(n * 64.0)
        small = np.zeros((2, P, P))
        for b in (0, 64):
            small[0, b:b + 64, b:b + 64] = np.cos(2 * np.pi * d / 64) * norm
            small[1, b:b + 64, b:b + 64] = -np.sin(2 * np.pi * d / 64) * norm
        out["dftd_" + name] = small.astype(f)
        cnt = np.zeros((2, P, n), f)
        for i, w in enumerate((2, 4, 8, 16)):
            left, right = w // 2, w - 1 - w // 2
            p = np.arange(n)
            c = np.clip(p + right + 1, 0, n) - np.clip(p - left, 0, n)
            cnt[i // 2, (i % 2) * 64:(i % 2) * 64 + 64] = 1.0 / c
        out["rcnt_" + name] = cnt
    reset = np.ones((36, NT, P), f)
    reset[:, :, 0] = 0
    out["reset"] = reset.reshape(36, N_ALL)
    return out


class Phase(ExitStack):

    def __init__(self, nc, tag):
        super().__init__()
        self.nc, self.tag, self.sems = nc, tag, []

    def sb(self, name, shape, dt=F32):
        return self.enter_context(self.nc.sbuf_tensor(f"{self.tag}_{name}", shape, dt))

    def ps(self, name, shape, dt=F32):
        return self.enter_context(self.nc.psum_tensor(f"{self.tag}_{name}", shape, dt))

    def sem(self, name):
        self.sems.append(self.nc.alloc_semaphore(f"{self.tag}_{name}"))
        return self.sems[-1]

    def __exit__(self, *exc):
        if exc[0] is None:
            self.nc.clear_and_free_semaphores(self.sems)
            self.nc.all_engine_barrier(sem_only=True)
        return super().__exit__(*exc)


class Steps:

    def __init__(self, eng, sem):
        self.eng, self.sem, self.n, self.base = eng, sem, 0, 0

    def __call__(self, ins):
        self.n += 1
        ins.then_inc(self.sem, 1)
        self.eng.wait_ge(self.sem, self.base + self.n)


def accumulate(nc, out, pairs):
    last = len(pairs) - 1
    for n, (lhsT, rhs) in enumerate(pairs):
        mm = nc.tensor.matmul(out, lhsT, rhs, start=n == 0, stop=n == last)
    return mm


def rows(ap):
    return ap.rearrange("(r p) -> r p", p=P)


def spread(ap, parts=P):
    return bass.AP(tensor=ap.tensor, offset=ap.offset, ap=[[0, parts]] + [list(x) for x in ap.ap])


def modulation(nc, g):
    io = g.io
    RING = 6
    MOD_N = 2 * 6 * D
    with Phase(nc, "mod") as ph:
        raw = ph.sb("raw", [P, 2, P])
        w = [ph.sb(f"w{j}", [P, KD, BANK]) for j in range(RING)]
        c4 = ph.sb("c4", [P, 4, KD])
        c2 = ph.sb("c2", [P, 2, KD, 2])
        row = ph.sb("row", [2, MOD_N])
        back = ph.sb("back", [96, 2, P])
        tp = ph.ps("tp", [P, 2, BANK])
        acc = ph.ps("acc", [2, 2, BANK])
        par_in, par_t, par_c = ph.sem("par_in"), ph.sem("par_t"), ph.sem("par_c")
        zero = ph.sem("zero")
        act_c, dve_c = ph.sem("act_c"), ph.sem("dve_c")
        w_in = [ph.sem(f"w_in{j}") for j in range(RING)]
        mm_done, mod_done = ph.sem("mm_done"), ph.sem("mod_done")
        bias_in, row_out, back_in, turned = ph.sem("bias_in"), ph.sem("row_out"), ph.sem("back_in"), ph.sem("turned")
        srcs = [(io["w_mod"], 12), (io["w_mod_2"][0], 6), (io["w_mod_2"][1], 6)]
        n_par = [0]
        first = [(io["norm1"], 8), (io["q_norm"], 3), (io["kv_norm"], 2), (io["conv_b"], 8), (io["ml_norm"], 8),
                 (io["ml_skip"], 8), (io["conv_w"], 40)]
        second = [(io["c"], 8), (io["c_ctx"], 8), (io["c_2"], 8), (io["c_ctx_2"], 8),
                  (io["norm_g_2"], 16), (io["pool_scale_2"], 4), (io["conv_b_2"], 4), (io["conv_w_2"], 12)]

        with nc.Block() as block:
            @block.gpsimd
            def _(pool):
                pool.memset(raw[:], 0.0).then_inc(zero, 1)
                pool.memset(g.ones[:], 1.0).then_inc(zero, 1)

            @block.sync
            def _(sp):
                for dst, name in ((g.ident, "ident"), (g.rev, "rev"), (g.block64, "block64"), (g.rot, "rot")):
                    sp.dma_start(dst[:], io["t_" + name]).then_inc(par_in, 16)
                    n_par[0] += 1
                sp.dma_start(g.causal[:], io["t_causal"].rearrange("d s t -> s d t")).then_inc(par_in, 16)
                n_par[0] += 1
                sp.wait_ge(zero, 1)
                for side, group in enumerate((first, second)):
                    at = 0
                    for ap, n in group:
                        sp.dma_start(raw[at:at + n, side, :], rows(ap)).then_inc(par_in, 16)
                        at += n
                        n_par[0] += 1
                for l in range(2):
                    for half in (0, HD):
                        for at, gain in ((PB_QG, io["q_gain_2"]), (PB_KG, io["k_gain_2"])):
                            sp.dma_start(raw[at + l:at + l + 1, 1, half:half + HD],
                                         gain[l:l + 1, :]).then_inc(par_in, 16)
                            n_par[0] += 1
                for s in range(2):
                    sp.dma_start(row[s:s + 1, 0:6 * D], io["b_mod"].rearrange("(o n) -> o n", o=1)).then_inc(bias_in, 16)
                    sp.dma_start(row[s:s + 1, 6 * D:], io["b_mod_2"].rearrange("(o n) -> o n", o=1)
                                 ).then_inc(bias_in, 16)
                base = 0
                for src, n in srcs:
                    wv = src.rearrange("(k p) n -> p k n", p=P)
                    with sp.Fori(0, n // RING) as i:
                        for j in range(RING):
                            sp.wait_ge(mm_done, base + RING * i + j + 1)
                            sp.dma_start(w[j][:], wv[:, :, ds((RING * i + j) * BANK, BANK)]).then_inc(w_in[j], 16)
                    base += n
                sp.wait_ge(mod_done, 2 + base)
                sp.dma_start(g.modrow, row[:]).then_inc(row_out, 16)
                sp.wait_ge(row_out, 16)
                for s in range(2):
                    sp.dma_start(back[:, s, :], rows(g.modrow[s])).then_inc(back_in, 16)

            @block.tensor
            def _(pe):
                pe.wait_ge(par_in, 16 * n_par[0])
                for side in range(2):
                    pe.transpose(tp[:, side, 0:P], raw[:, side, :], g.ident[:]).then_inc(par_t, 1)
                pe.wait_ge(dve_c, 4)
                pe.sem_inc(mm_done, RING)
                base = 0
                for blk, (_, n) in enumerate(srcs):
                    with pe.Fori(0, n // RING) as i:
                        for j in range(RING):
                            pe.wait_ge(w_in[j], 16 * (base // RING + i + 1))
                            pe.wait_ge(mod_done, base + RING * i + j + 1)
                            accumulate(nc, acc[:, j % 2, :], [(c2[:, min(blk, 1), k, :], w[j][:, k, :])
                                                              for k in range(KD)]).then_inc(mm_done, 1)
                    base += n
                pe.wait_ge(back_in, 32)
                for s in range(2):
                    pe.transpose(tp[:, s, 0:96], back[:, s, :], g.ident[0:96, 0:96]).then_inc(turned, 1)

            @block.scalar
            def _(act):
                act.wait_ge(par_c, 2)
                act.activation(c4[:].rearrange("p a k -> p (a k)"), g.pb[:, PB_C:PB_C + 32], ACT.Silu).then_inc(act_c, 1)

            @block.vector
            def _(dve):
                for side, dst in enumerate((g.pa, g.pb)):
                    dve.wait_ge(par_t, side + 1)
                    dve.tensor_copy(dst[:], tp[:, side, 0:P]).then_inc(par_c, 1)
                dve.wait_ge(act_c, 1)
                for blk in range(2):
                    for s in range(2):
                        dve.tensor_copy(c2[:, blk, :, s], c4[:, 2 * blk + s, :]).then_inc(dve_c, 1)
                dve.sem_inc(mod_done, 2)
                dve.wait_ge(bias_in, 64)
                base = 0
                for _, n in srcs:
                    with dve.Fori(0, n // RING) as i:
                        for j in range(RING):
                            dve.wait_ge(mm_done, base + RING * i + j + RING + 1)
                            cols = ds((base + RING * i + j) * BANK, BANK)
                            dve.tensor_tensor(row[:, cols], row[:, cols], acc[:, j % 2, :], ALU.add).then_inc(mod_done, 1)
                    base += n
                for s in range(2):
                    dve.wait_ge(turned, s + 1)
                    dve.tensor_copy(g.mod1[:, s, :], tp[:, s, 0:48])
                    dve.tensor_copy(g.mod2[:, s, :], tp[:, s, 48:96])


def normed_transposed(nc, g, tag, segments, norm, mod, at_shift, at_scale, hT):
    with Phase(nc, tag) as ph:
        x = ph.sb("x", [P, 2, D])
        xn = ph.sb("xn", [P, 2, D])
        junk = ph.sb("junk", [P, D])
        st = ph.sb("st", [P, 2, 4])
        gain = ph.sb("gain", [P, 2, KD])
        tp = ph.ps("tp", [P, 2, 2, BANK])
        x_in = [ph.sem(f"x_in{j}") for j in range(2)]
        gain_done, squared, var_done = ph.sem("gain_done"), ph.sem("squared"), ph.sem("var_done")
        root_done, inv_done, xn_done = ph.sem("root_done"), ph.sem("inv_done"), ph.sem("xn_done")
        turned, out_a, out_b = ph.sem("turned"), ph.sem("out_a"), ph.sem("out_b")

        with nc.Block() as block:
            @block.sync
            def _(sp):
                base = 0
                for src, pairs, _, _ in segments:
                    with sp.Fori(0, pairs) as i:
                        for j in range(2):
                            sp.wait_ge(xn_done, base + 2 * i + j + 1)
                            sp.dma_start(x[:, j, :], src[ds((2 * i + j) * P, P), :]).then_inc(x_in[j], 16)
                    base += 2 * pairs

            @block.scalar
            def _(act):
                act.sem_inc(out_a, 1)
                base = 0
                for _, pairs, s, col in segments:
                    with act.Fori(0, pairs) as i:
                        for j in range(2):
                            n = base + 2 * i + j
                            act.wait_ge(x_in[j], 16 * (base // 2 + i + 1))
                            act.wait_ge(inv_done, n + 1)
                            act.activation(junk[:], x[:, j, :], ACT.Square,
                                           accum_out=st[:, j, 0:1]).then_inc(squared, 1)
                            act.wait_ge(var_done, n + 1)
                            act.activation(st[:, j, 2:3], st[:, j, 1:2], ACT.Sqrt).then_inc(root_done, 1)
                            act.wait_ge(turned, n + 2)
                            act.wait_ge(gain_done, 2)
                            for k in range(4):
                                ins = act.activation(hT[:, k, ds(col + (2 * i + j) * P, P)],
                                                     tp[:, j, 0, k * P:(k + 1) * P], ACT.Identity,
                                                     bias=mod[:, s, at_shift + k:at_shift + k + 1],
                                                     scale=gain[:, s, k:k + 1])
                            ins.then_inc(out_a, 1)
                    base += 2 * pairs

            @block.vector
            def _(dve):
                for s in range(2):
                    dve.scalar_tensor_tensor(gain[:, s, :], mod[:, s, at_scale:at_scale + KD], 1.0, norm,
                                             ALU.add, ALU.mult).then_inc(gain_done, 1)
                dve.sem_inc(xn_done, 2)
                dve.sem_inc(inv_done, 2)
                dve.sem_inc(out_b, 1)
                dve.wait_ge(gain_done, 2)
                base = 0
                for _, pairs, s, col in segments:
                    with dve.Fori(0, pairs) as i:
                        for j in range(2):
                            n = base + 2 * i + j
                            dve.wait_ge(squared, n + 1)
                            dve.tensor_scalar(st[:, j, 1:2], st[:, j, 0:1], 1.0 / D, EPS, ALU.mult,
                                              ALU.add).then_inc(var_done, 1)
                            dve.wait_ge(root_done, n + 1)
                            dve.reciprocal(st[:, j, 3:4], st[:, j, 2:3]).then_inc(inv_done, 1)
                            dve.wait_ge(inv_done, n + 3)
                            dve.wait_ge(turned, n + 1)
                            dve.tensor_scalar(xn[:, j, :], x[:, j, :], st[:, j, 3:4], None,
                                              ALU.mult).then_inc(xn_done, 1)
                            dve.wait_ge(turned, n + 2)
                            for k in range(4):
                                ins = dve.tensor_scalar(hT[:, 4 + k, ds(col + (2 * i + j) * P, P)],
                                                        tp[:, j, 1, k * P:(k + 1) * P], gain[:, s, 4 + k:5 + k],
                                                        mod[:, s, at_shift + 4 + k:at_shift + 5 + k],
                                                        ALU.mult, ALU.add)
                            ins.then_inc(out_b, 1)
                    base += 2 * pairs

            @block.tensor
            def _(pe):
                pe.sem_inc(turned, 1)
                base = 0
                for _, pairs, _, _ in segments:
                    with pe.Fori(0, pairs) as i:
                        for j in range(2):
                            n = base + 2 * i + j
                            pe.wait_ge(xn_done, n + 3)
                            pe.wait_ge(out_a, n + 1)
                            pe.wait_ge(out_b, n + 1)
                            for k in range(KD):
                                mm = pe.transpose(tp[:, j, k // 4, (k % 4) * P:(k % 4 + 1) * P],
                                                  xn[:, j, k * P:(k + 1) * P], g.ident[:])
                            mm.then_inc(turned, 1)
                    base += 2 * pairs


def latents(nc, g):
    io = g.io
    with Phase(nc, "lat") as ph:
        w = ph.sb("w", [P, KD, COL_XM + ROPE])
        sq = ph.sb("sq", [P, 5, N_ALL])
        kr = ph.sb("kr", [P, N_ALL])
        kpe = ph.sb("kpe", [P, N_ALL])
        rstd = ph.sb("rstd", [P, 2, N_ALL])
        t1 = ph.sb("t1", [P, N_LAT])
        ps = ph.ps("ps", [P, 2, BANK])
        w_in, cs_in = ph.sem("w_in"), ph.sem("cs_in")
        full = [ph.sem(f"full{b}") for b in range(2)]
        free = [ph.sem(f"free{b}") for b in range(2)]
        act_step, dve_step, sq_done = ph.sem("act_step"), ph.sem("dve_step"), ph.sem("sq_done")
        root_ready, kpe_ready, kpe_high = ph.sem("root_ready"), ph.sem("kpe_ready"), ph.sem("kpe_high")
        uses = [(m, c) for m in range(3) for c in LAT_CHUNKS] + [(m, c) for m in range(3, 6) for c in ALL_CHUNKS]
        sums = [(0, c) for c in LAT_CHUNKS] + [(1, c) for c in ALL_CHUNKS]
        n1, n2 = len(uses), len(uses) + len(sums)

        with nc.Block() as block:
            @block.sync
            def _(sp):
                view = io["w_in"].rearrange("(k p) n -> p k n", p=P)
                sp.dma_start(w[:, :, 0:COL_XM], view[:, :, 0:COL_XM]).then_inc(w_in, 16)
                sp.dma_start(w[:, :, COL_XM:], view[:, :, COL_KR:COL_XM]).then_inc(w_in, 16)
                sp.dma_start(g.cos[:], io["t_cos"]).then_inc(cs_in, 16)
                sp.dma_start(g.sin[:], io["t_sin"]).then_inc(cs_in, 16)

            @block.tensor
            def _(pe):
                pe.wait_ge(w_in, 32)
                for n, (m, (c0, cn)) in enumerate(uses):
                    b, M = n % 2, P
                    if n >= 2:
                        pe.wait_ge(free[b], n // 2)
                    accumulate(nc, ps[0:M, b, 0:cn], [(w[:, k, m * P:m * P + M], g.hT[:, k, c0:c0 + cn])
                                                      for k in range(KD)]).then_inc(full[b], 1)
                pe.wait_ge(sq_done, n1 - 3)
                for n, (q, (c0, cn)) in enumerate(sums, n1):
                    b = n % 2
                    pe.wait_ge(free[b], n // 2)
                    src = range(3) if q == 0 else range(3, 5)
                    accumulate(nc, ps[:, b, 0:cn], [(g.ones[:], sq[:, k, c0:c0 + cn]) for k in src]).then_inc(full[b], 1)
                for n, (c0, cn) in enumerate(LAT_CHUNKS, n2):
                    b = n % 2
                    pe.wait_ge(free[b], n // 2)
                    accumulate(nc, ps[:, b, 0:cn], [(g.rot[:], kr[:, c0:c0 + cn])]).then_inc(full[b], 1)

            @block.vector
            def _(dve):
                step = Steps(dve, dve_step)
                for n, (m, (c0, cn)) in enumerate(uses):
                    b = n % 2
                    dst = g.ql[:, m, c0 - N_CTX:c0 - N_CTX + cn] if m < 3 else g.kl[:, m - 3, c0:c0 + cn] if m < 5 \
                        else kr[:, c0:c0 + cn]
                    dve.wait_ge(full[b], n // 2 + 1)
                    dve.tensor_copy(dst, ps[0:dst.shape[0], b, 0:cn]).then_inc(free[b], 1)
                for n, (q, (c0, cn)) in enumerate(sums, n1):
                    b = n % 2
                    dve.wait_ge(full[b], n // 2 + 1)
                    dve.tensor_scalar(rstd[:, q, c0:c0 + cn], ps[:, b, 0:cn], 1.0 / ((QL, KL)[q] * P), EPS,
                                      ALU.mult, ALU.add).then_inc(free[b], 1)
                dve.wait_ge(root_ready, 2)
                step(dve.reciprocal(rstd[:, 0, N_CTX:], rstd[:, 0, N_CTX:]))
                step(dve.reciprocal(rstd[:, 1, :], rstd[:, 1, :]))
                for m in range(QL):
                    step(dve.scalar_tensor_tensor(g.ql[:, m, :], g.ql[:, m, :], g.pa[:, PA_QN + m:PA_QN + m + 1],
                                                  rstd[:, 0, N_CTX:], ALU.mult, ALU.mult))
                for m in range(KL):
                    step(dve.scalar_tensor_tensor(g.kl[:, m, :], g.kl[:, m, :], g.pa[:, PA_KVN + m:PA_KVN + m + 1],
                                                  rstd[:, 1, :], ALU.mult, ALU.mult))
                dve.wait_ge(cs_in, 32)
                for n, (c0, cn) in enumerate(LAT_CHUNKS, n2):
                    b = n % 2
                    dve.wait_ge(full[b], n // 2 + 1)
                    dve.tensor_tensor(t1[:, c0 - N_CTX:c0 - N_CTX + cn], ps[:, b, 0:cn],
                                      g.sin[:, c0 - N_CTX:c0 - N_CTX + cn], ALU.mult).then_inc(free[b], 1)
                for b in range(2):
                    dve.wait_ge(free[b], (n2 + 3 - b) // 2)
                dve.tensor_copy(kpe[:, 0:N_CTX], kr[:, 0:N_CTX])
                step(dve.tensor_tensor(kpe[:, N_CTX:], kr[:, N_CTX:], g.cos[:], ALU.mult))
                dve.tensor_tensor(kpe[:, N_CTX:], kpe[:, N_CTX:], t1[:], ALU.add).then_inc(kpe_ready, 1)
                dve.wait_ge(kpe_high, 1)
                dve.tensor_tensor(g.kpe_lo[:], kpe[0:ROPE, :], g.kpe_hi[0:ROPE, :].bitcast(F32), ALU.subtract)

            @block.scalar
            def _(act):
                for n, (m, (c0, cn)) in enumerate(uses):
                    if m == 5:
                        continue
                    b = n % 2
                    src = g.ql[:, m, c0 - N_CTX:c0 - N_CTX + cn] if m < 3 else g.kl[:, m - 3, c0:c0 + cn]
                    act.wait_ge(free[b], n // 2 + 1)
                    act.activation(sq[:, m, c0:c0 + cn], src, ACT.Square).then_inc(sq_done, 1)
                for b in range(2):
                    act.wait_ge(free[b], (n2 + 1 - b) // 2)
                act.activation(rstd[:, 0, N_CTX:], rstd[:, 0, N_CTX:], ACT.Sqrt).then_inc(root_ready, 1)
                act.activation(rstd[:, 1, :], rstd[:, 1, :], ACT.Sqrt).then_inc(root_ready, 1)
                act.wait_ge(kpe_ready, 1)
                act.activation(g.kpe_hi[:], kpe[:], ACT.Copy).then_inc(kpe_high, 1)


def wait_count(eng, sem, count):
    if not isinstance(count, int) or count > 0:
        eng.wait_ge(sem, count)


def attention(nc, g):
    io = g.io
    with Phase(nc, "att") as ph:
        wq = ph.sb("wq", [P, QL, QK + ROPE])
        wkv = ph.sb("wkv", [P, KL, NOPE + VD])
        qh, qlo = ph.sb("qh", [P, 2, N_LAT], FR), ph.sb("qlo", [P, 2, N_LAT], FR)
        kh, klo = ph.sb("kh", [P, 2, N_ALL], FR), ph.sb("klo", [P, 2, N_ALL], FR)
        qraw = ph.sb("qraw", [P, N_LAT])
        qsum = ph.sb("qsum", [P, N_LAT])
        qp = ph.sb("qp", [P, 2, N_LAT], FR)
        v = ph.sb("v", [P, 2, NT, VD])
        p = ph.sb("p", [P, 2, N_ALL])
        pT = ph.sb("pT", [P, 2, NT, P])
        st = ph.sb("st", [P, 2, 4])
        sc = ph.ps("sc", [P, 2, 3, BANK])
        tb = ph.ps("tb", [P, 2, BANK])
        wt_in = ph.sem("wt_in")
        full = [ph.sem(f"full{b}") for b in range(2)]
        free = [ph.sem(f"free{b}") for b in range(2)]
        high, sum_ready, qp_high, qp_ready = ph.sem("high"), ph.sem("sum_ready"), ph.sem("qp_high"), ph.sem("qp_ready")
        cos_done = ph.sem("cos_done")
        scored, maxed, bias_ready, exped = ph.sem("scored"), ph.sem("maxed"), ph.sem("bias_ready"), ph.sem("exped")
        inv_ready, p_ready = ph.sem("inv_ready"), ph.sem("p_ready")
        ROPE_USE, NOPE_USE, ROT_USE, KEY_USE, VAL_USE, PROJ, TURN = 0, 2, 4, 6, 9, 12, 3
        USES = PROJ + TURN * LT
        GROUPS = [(0, 4), (4, 4), (8, 2)]
        HALVES = [slice(c * BANK, (c + 1) * BANK) for c in range(2)]

        def use(head, n):
            m = n if isinstance(head, int) and head == 0 and n < PROJ else n - TURN
            return m % 2, head * (USES // 2) + m // 2

        def turn_use(head, t, c):
            if t < LT - 1 or isinstance(head, int) and head == HEADS - 1:
                return use(head, PROJ + TURN * (t + 1) + c)
            return use(head + 1, PROJ + c)

        def steps(head, first):
            if not first:
                yield head - 1, LT - 1, (head, 0)
            for t in range(LT - 1):
                yield head, t, (head, t + 1)

        def before(head, t):
            return (head, t - 1) if t else (head - 1, LT - 1)

        def over_heads(eng, body):
            for j in range(2):
                body(j, j, j == 0)
            with eng.Fori(0, HEADS // 2 - 1) as i:
                for j in range(2):
                    body(2 * i + 2 + j, j, False)

        with nc.Block() as block:
            @block.sync
            def _(sp):
                def load(head, j, first):
                    if not first:
                        b, earlier = use(head - 1, PROJ - 1)
                        sp.wait_ge(full[b], earlier + 1)
                    q_cols = io["w_uq"].rearrange("(k p) n -> p k n", p=P)
                    kv_cols = io["w_ukv"].rearrange("(k p) n -> p k n", p=P)
                    sp.dma_start(wq[:, :, 0:QK], q_cols[:, :, ds(head * QK, QK)]).then_inc(wt_in, 16)
                    sp.dma_start(wq[:, :, QK:], q_cols[:, :, ds(head * QK + NOPE, ROPE)]).then_inc(wt_in, 16)
                    sp.dma_start(wkv[:], kv_cols[:, :, ds(head * (NOPE + VD), NOPE + VD)]).then_inc(wt_in, 16)
                over_heads(sp, load)

            @block.tensor
            def _(pe):
                def into_bank(head, n, make):
                    b, earlier = use(head, n)
                    wait_count(pe, free[b], earlier)
                    make(b).then_inc(full[b], 1)

                def project(head, j):
                    pe.wait_ge(wt_in, 48 * (head + 1))
                    for c in range(2):
                        into_bank(head, ROPE_USE + c, lambda b: accumulate(nc, tb[:, b, :], [
                            (wq[:, k, NOPE:], g.ql[:, k, HALVES[c]]) for k in range(QL)]))
                    for c in range(2):
                        into_bank(head, NOPE_USE + c, lambda b: accumulate(nc, tb[:, b, :], [
                            (wq[:, k, 0:NOPE], g.ql[:, k, HALVES[c]]) for k in range(QL)]))
                    for c in range(2):
                        into_bank(head, ROT_USE + c, lambda b: accumulate(nc, tb[:, b, :], [
                            (g.rot[:], qraw[:, HALVES[c]])]))
                    for c, (c0, cn) in enumerate(ALL_CHUNKS):
                        into_bank(head, KEY_USE + c, lambda b: accumulate(nc, tb[:, b, 0:cn], [
                            (wkv[:, k, 0:NOPE], g.kl[:, k, c0:c0 + cn]) for k in range(KL)]))
                    for c, (t0, tn) in enumerate(GROUPS):
                        def values(b):
                            for t in range(tn):
                                mm = accumulate(nc, tb[:, b, t * P:(t + 1) * P], [
                                    (g.kl[:, k, (t0 + t) * P:(t0 + t + 1) * P], wkv[:, k, NOPE:])
                                    for k in range(KL)])
                            return mm
                        into_bank(head, VAL_USE + c, values)

                def scores(head, t, j):
                    n = head * LT + t
                    if t == 0:
                        for c in (1, 2):
                            b, earlier = use(head, PROJ - c)
                            pe.wait_ge(free[b], earlier + 1)
                        pe.wait_ge(qp_ready, head + 1)
                    wait_count(pe, exped, n - 1)
                    tile = slice(t * P, (t + 1) * P)
                    for c0, cn in [(0, BANK), (BANK, BANK), (2 * BANK, N_ALL - 2 * BANK)]:
                        cols = slice(c0, c0 + cn)
                        mm = accumulate(nc, sc[:, t % 2, c0 // BANK, 0:cn], [
                            (qh[:, j, tile], kh[:, j, cols]), (qh[:, j, tile], klo[:, j, cols]),
                            (qlo[:, j, tile], kh[:, j, cols]), (qp[:, j, tile], g.kpe_hi[:, cols]),
                            (qp[0:ROPE, j, tile], g.kpe_lo[:, cols])])
                    mm.then_inc(scored, 1)

                def turn(head, t, c, more=None):
                    def make(b):
                        t0, tn = GROUPS[c]
                        for k in range(tn):
                            mm = pe.transpose(tb[:, b, k * P:(k + 1) * P],
                                              p[:, t % 2, (t0 + k) * P:(t0 + k + 1) * P], g.ident[:])
                        return more(b) if more else mm
                    b, earlier = turn_use(head, t, c)
                    wait_count(pe, free[b], earlier)
                    make(b).then_inc(full[b], 1)

                def output(t, j):
                    return lambda b: accumulate(nc, tb[:, b, 2 * P:3 * P], [
                        (v[:, j, k, :], pT[:, t % 2, k, :]) for k in range(NT)])

                def wait_turned(head, t):
                    for c in (1, 2):
                        b, earlier = turn_use(head, t, c)
                        pe.wait_ge(free[b], earlier + 1)

                def one(head, j, first):
                    project(head, j)
                    if first:
                        scores(head, 0, j)
                    for (h, t, nxt) in steps(head, first):
                        scores(*nxt, j)
                        pe.wait_ge(p_ready, h * LT + t + 1)
                        turn(h, t, 0)
                        turn(h, t, 1)
                        if first and t == 0:
                            turn(h, t, 2)
                        else:
                            pj = j if h is head and t > 0 else 1 - j
                            turn(h, t, 2, output(before(h, t)[1], pj))

                over_heads(pe, one)
                last, n = HEADS - 1, HEADS * LT
                pe.wait_ge(p_ready, n)
                turn(last, LT - 1, 0)
                turn(last, LT - 1, 1)
                turn(last, LT - 1, 2, output(LT - 2, 1))
                wait_turned(last, LT - 1)
                b, earlier = use(last, USES + TURN)
                output(LT - 1, 1)(b).then_inc(full[b], 1)

            @block.scalar
            def _(act):
                def out_of_bank(b, earlier, dst, src, sem):
                    act.wait_ge(full[b], earlier + 1)
                    act.activation(dst, src, ACT.Copy).then_inc(sem, 1)

                def exp(head, t):
                    act.wait_ge(bias_ready, head * LT + t + 1)
                    act.activation(p[:, t % 2, :], sc[:, t % 2].rearrange("p b n -> p (b n)")[:, 0:N_ALL], ACT.Exp,
                                   bias=st[:, t % 2, 1:2], scale=ATT_SCALE,
                                   accum_out=st[:, t % 2, 2:3]).then_inc(exped, 1)

                def copy_projections(head, j):
                    for c in range(2):
                        b, earlier = use(head, ROPE_USE + c)
                        out_of_bank(b, earlier, qraw[:, HALVES[c]], tb[:, b, :], free[b])
                    for c in range(2):
                        b, earlier = use(head, NOPE_USE + c)
                        out_of_bank(b, earlier, qh[:, j, HALVES[c]], tb[:, b, :], high)
                    for c, (c0, cn) in enumerate(ALL_CHUNKS):
                        b, earlier = use(head, KEY_USE + c)
                        out_of_bank(b, earlier, kh[:, j, c0:c0 + cn], tb[:, b, 0:cn], high)
                    act.wait_ge(sum_ready, head + 1)
                    act.activation(qp[:, j, :], qsum[:], ACT.Copy).then_inc(qp_high, 1)
                    for c, (t0, tn) in enumerate(GROUPS):
                        b, earlier = use(head, VAL_USE + c)
                        out_of_bank(b, earlier, v[:, j, t0:t0 + tn, :].rearrange("p t d -> p (t d)"),
                                    tb[:, b, 0:tn * P], free[b])

                def copy_turned(head, t, c, output_of=None):
                    t0, tn = GROUPS[c]
                    b, earlier = turn_use(head, t, c)
                    act.wait_ge(full[b], earlier + 1)
                    ins = act.activation(pT[:, t % 2, t0:t0 + tn, :].rearrange("p t d -> p (t d)"),
                                         tb[:, b, 0:tn * P], ACT.Copy)
                    if output_of:
                        ins = copy_output(b, *output_of)
                    ins.then_inc(free[b], 1)

                def copy_output(b, head, t):
                    return act.activation(g.yT[:, ds(head, 1), t * P:(t + 1) * P].rearrange("p o n -> p (o n)"),
                                          tb[:, b, 2 * P:3 * P], ACT.Copy)

                def one(head, j, first):
                    copy_projections(head, j)
                    if first:
                        exp(head, 0)
                    for (h, t, nxt) in steps(head, first):
                        copy_turned(h, t, 0)
                        copy_turned(h, t, 1)
                        exp(*nxt)
                        copy_turned(h, t, 2, None if first and t == 0 else before(h, t))

                over_heads(act, one)
                last = HEADS - 1
                for c in range(TURN):
                    copy_turned(last, LT - 1, c, (last, LT - 2) if c == TURN - 1 else None)
                b, earlier = use(last, USES + TURN)
                act.wait_ge(full[b], earlier + 1)
                copy_output(b, last, LT - 1)

            @block.vector
            def _(dve):
                def maximum(head, t):
                    n = head * LT + t
                    dve.wait_ge(scored, n + 1)
                    dve.tensor_reduce(st[:, t % 2, 0:1], sc[:, t % 2].rearrange("p b n -> p (b n)")[:, 0:N_ALL],
                                      AX.X, ALU.max).then_inc(maxed, 1)
                    dve.wait_ge(maxed, n + 1)
                    dve.tensor_scalar(st[:, t % 2, 1:2], st[:, t % 2, 0:1], -ATT_SCALE, None,
                                      ALU.mult).then_inc(bias_ready, 1)

                def normalise(head, t):
                    n = head * LT + t
                    dve.wait_ge(exped, n + 1)
                    dve.reciprocal(st[:, t % 2, 3:4], st[:, t % 2, 2:3]).then_inc(inv_ready, 1)
                    dve.wait_ge(inv_ready, n + 1)
                    dve.tensor_scalar(p[:, t % 2, :], p[:, t % 2, :], st[:, t % 2, 3:4], None,
                                      ALU.mult).then_inc(p_ready, 1)

                def low(head, n, order, lo, hi):
                    b, _ = use(head, n)
                    dve.wait_ge(high, 5 * head + order + 1)
                    dve.tensor_tensor(lo, tb[:, b, 0:lo.shape[1]], hi.bitcast(F32), ALU.subtract).then_inc(free[b], 1)

                def split(head, j):
                    for c in range(2):
                        low(head, NOPE_USE + c, c, qlo[:, j, HALVES[c]], qh[:, j, HALVES[c]])
                    for c in range(2):
                        b, earlier = use(head, ROT_USE + c)
                        dve.wait_ge(full[b], earlier + 1)
                        dve.tensor_tensor(qsum[:, HALVES[c]], tb[:, b, :], g.sin[:, HALVES[c]],
                                          ALU.mult).then_inc(free[b], 1)
                    dve.tensor_tensor(qraw[:], qraw[:], g.cos[:], ALU.mult).then_inc(cos_done, 1)
                    dve.wait_ge(cos_done, head + 1)
                    dve.tensor_tensor(qsum[:], qsum[:], qraw[:], ALU.add).then_inc(sum_ready, 1)
                    for c, (c0, cn) in enumerate(ALL_CHUNKS):
                        low(head, KEY_USE + c, 2 + c, klo[:, j, c0:c0 + cn], kh[:, j, c0:c0 + cn])
                    dve.wait_ge(qp_high, head + 1)
                    dve.tensor_tensor(qp[ROPE:, j, :], qsum[ROPE:, :], qp[ROPE:, j, :].bitcast(F32),
                                      ALU.subtract).then_inc(qp_ready, 1)

                def one(head, j, first):
                    split(head, j)
                    for t in range(LT):
                        maximum(head, t)
                        normalise(head, t)

                over_heads(dve, one)


def credit(eng, sem, n):
    eng.sem_inc(sem, n)


def stream_weights(sp, view, w, w_in, tile_done, segs, width=P):
    base = 0
    for col, pairs, _ in segs:
        with sp.Fori(0, pairs) as i:
            for j in range(2):
                sp.wait_ge(tile_done, base + 2 * i + j + 1)
                sp.dma_start(w[:, j], view[:, :, ds(col + (2 * i + j) * width, width)]).then_inc(w_in[j], 16)
        base += 2 * pairs


def project_tiles(nc, pe, w, w_in, tile_done, read_out, ps, hT, segs):
    credit(pe, tile_done, 2)
    base = 0
    for _, pairs, chunks in segs:
        with pe.Fori(0, pairs) as i:
            for j in range(2):
                pe.wait_ge(w_in[j], 16 * (base // 2 + i + 1))
                pe.wait_ge(read_out, base + 2 * i + j + 1)
                for c, (c0, cn) in enumerate(chunks):
                    mm = accumulate(nc, ps[:, j, c, 0:cn], [(w[:, j, k, :], hT[:, k, c0:c0 + cn])
                                                            for k in range(KD)])
                mm.then_inc(tile_done, 1)
        base += 2 * pairs


def gate_attention(nc, g):
    io = g.io
    with Phase(nc, "gat") as ph:
        w = ph.sb("w", [P, 2, KD, P])
        sig = ph.sb("sig", [P, 2, N_LAT])
        ps = ph.ps("ps", [P, 2, 2, BANK])
        w_in = [ph.sem(f"w_in{j}") for j in range(2)]
        tile_done, read_out, gated, stored = ph.sem("tile_done"), ph.sem("read_out"), ph.sem("gated"), ph.sem("stored")
        segs = [(COL_GMLA, KD // 2, LAT_CHUNKS)]
        with nc.Block() as block:
            @block.sync
            def _(sp):
                stream_weights(sp, io["w_in"].rearrange("(k p) n -> p k n", p=P), w, w_in, tile_done, segs)

            @block.tensor
            def _(pe):
                project_tiles(nc, pe, w, w_in, tile_done, read_out, ps, g.hT, segs)

            @block.scalar
            def _(act):
                credit(act, read_out, 2)
                with act.Fori(0, KD // 2) as i:
                    for j in range(2):
                        act.wait_ge(tile_done, 2 * i + j + 3)
                        act.wait_ge(gated, 2 * i + j + 1)
                        act.activation(sig[:, j, :], ps[:, j].rearrange("p c n -> p (c n)"),
                                       ACT.Sigmoid).then_inc(read_out, 1)

            @block.vector
            def _(dve):
                credit(dve, gated, 2)
                with dve.Fori(0, KD // 2) as i:
                    for j in range(2):
                        dve.wait_ge(read_out, 2 * i + j + 3)
                        y = g.yT[:, ds(2 * i + j, 1), :]
                        dve.tensor_tensor(y, y, sig[:, j:j + 1, :], ALU.mult).then_inc(gated, 1)

            @block.gpsimd
            def _(pool):
                pool.wait_ge(gated, KD + 2)
                pool.dma_start(g.y_dram.rearrange("k p n -> p k n"), g.yT[:]).then_inc(stored, 16)
                pool.wait_ge(stored, 16)


PAD = TAPS // 2
W_PAD = N_ALL + 3 * PAD
OFF_CTX, OFF_LAT = PAD, 2 * PAD + N_CTX


def padded(c):
    return OFF_CTX + c * P if c < CT else OFF_LAT + (c - CT) * P


def inner(nc, g):
    io = g.io
    with Phase(nc, "inn") as ph:
        w = ph.sb("w", [P, 2, KD, P])
        cv = ph.sb("cv", [P, 2, W_PAD])
        ps = ph.ps("ps", [P, 2, 3, BANK])
        w_in = [ph.sem(f"w_in{j}") for j in range(2)]
        tile_done, read_out, conv_done = ph.sem("tile_done"), ph.sem("read_out"), ph.sem("conv_done")
        tap, xc_done, zeroed, stored = ph.sem("tap"), ph.sem("xc_done"), ph.sem("zeroed"), ph.sem("stored")
        segs = [(COL_XM, KD // 2, ALL_CHUNKS)]
        n_out = W_PAD - 2 * PAD
        with nc.Block() as block:
            @block.sync
            def _(sp):
                stream_weights(sp, io["w_in"].rearrange("(k p) n -> p k n", p=P), w, w_in, tile_done, segs)
                for t in range(KD):
                    sp.wait_ge(xc_done, 3 + t)
                    sp.dma_start(g.xm_dram[t], g.xm[:, t, :]).then_inc(stored, 16)
                    sp.dma_start(g.xc_dram[t], g.xc[:, t, :]).then_inc(stored, 16)
                sp.wait_ge(stored, 32 * KD)

            @block.tensor
            def _(pe):
                project_tiles(nc, pe, w, w_in, tile_done, read_out, ps, g.hT, segs)

            @block.gpsimd
            def _(pool):
                for a in (0, OFF_CTX + N_CTX, OFF_LAT + N_LAT):
                    pool.memset(g.xm[:, :, a:a + PAD], 0.0).then_inc(zeroed, 1)

            @block.scalar
            def _(act):
                with act.Fori(0, KD // 2) as i:
                    for j in range(2):
                        t = 2 * i + j
                        act.wait_ge(tile_done, t + 3)
                        act.activation(g.xm[:, ds(t, 1), OFF_LAT:OFF_LAT + N_LAT].rearrange("p o n -> p (o n)"),
                                       ps[:, j, 0:2, :].rearrange("p c n -> p (c n)"), ACT.Copy)
                        act.activation(g.xm[:, ds(t, 1), OFF_CTX:OFF_CTX + N_CTX].rearrange("p o n -> p (o n)"),
                                       ps[:, j, 2, 0:N_CTX], ACT.Copy).then_inc(read_out, 1)
                        act.wait_ge(conv_done, t + 1)
                        for a, b, n in ((OFF_CTX - PAD, 0, N_CTX), (OFF_LAT - PAD, N_CTX, N_LAT)):
                            ins = act.activation(g.xc[:, ds(t, 1), b:b + n].rearrange("p o n -> p (o n)"),
                                                 cv[:, j, a:a + n], ACT.Silu,
                                                 bias=g.pa[:, ds(PA_CB + t, 1)])
                        ins.then_inc(xc_done, 1)

            @block.vector
            def _(dve):
                credit(dve, read_out, 2)
                credit(dve, xc_done, 2)
                dve.wait_ge(zeroed, 3)
                with dve.Fori(0, KD // 2) as i:
                    for j in range(2):
                        t = 2 * i + j
                        dve.wait_ge(read_out, t + 3)
                        dve.wait_ge(xc_done, t + 1)
                        for tp in range(TAPS):
                            src = g.xm[:, ds(t, 1), tp:tp + n_out].rearrange("p o n -> p (o n)")
                            cw = g.pa[:, ds(PA_CW + tp * KD + t, 1)]
                            if tp == 0:
                                dve.tensor_scalar(cv[:, j, 0:n_out], src, cw, None, ALU.mult).then_inc(tap, 1)
                            else:
                                dve.wait_ge(tap, t * (TAPS - 1) + tp)
                                dve.scalar_tensor_tensor(cv[:, j, 0:n_out], src, cw, cv[:, j, 0:n_out], ALU.mult,
                                                         ALU.add).then_inc(tap if tp < TAPS - 1 else conv_done, 1)


def gates(nc, g):
    io = g.io
    with Phase(nc, "gts") as ph:
        dense = ph.sb("dense", [P, 3, KD, 4])
        block4 = ph.sb("block4", [P, P])
        bd = ph.sb("bd", [P, 3, KD, P])
        bdt = ph.sb("bdt", [P, 3, KD, P])
        wg = ph.sb("wg", [P, 3 * KD, 16])
        wg2 = ph.sb("wg2", [P, 2 * KD, 16])
        bg = ph.sb("bg", [P, 16])
        ps = ph.ps("ps", [P, 2, BANK])
        pw = ph.ps("pw", [P, BANK])
        pg = ph.ps("pg", [P, BANK])
        loaded, built, turned, copied = ph.sem("loaded"), ph.sem("built"), ph.sem("turned"), ph.sem("copied")
        folded, wg_ready, summed, done, scaled, stored = (ph.sem("folded"), ph.sem("wg_ready"), ph.sem("summed"),
                                                          ph.sem("done"), ph.sem("scaled"), ph.sem("stored"))
        with nc.Block() as block:
            @block.sync
            def _(sp):
                for q, name in enumerate(["w_qblk", "w_kblk", "w_vblk"]):
                    sp.dma_start(dense[:, q], io[name].rearrange("(t n) j k -> (n j) t k", t=KD)).then_inc(loaded, 16)
                sp.dma_start(block4[:], io["t_block4"]).then_inc(loaded, 16)
                sp.dma_start(wg[:], io["w_gate"].rearrange("(t p) n -> p t n", p=P)).then_inc(loaded, 16)
                sp.dma_start(bg[:], spread(io["b_gate"])).then_inc(loaded, 16)
                sp.wait_ge(scaled, 1)
                sp.dma_start(g.bd_dram.rearrange("t p q n -> p q t n"), bd[:]).then_inc(stored, 16)
                sp.wait_ge(stored, 16)

            @block.vector
            def _(dve):
                dve.wait_ge(loaded, 96)
                for q in range(3):
                    for t in range(KD):
                        ins = dve.tensor_tensor(
                            bd[:, q, t, :].rearrange("p (n k) -> p n k", k=4),
                            dense[:, q, t:t + 1, :].to_broadcast([P, 32, 4]),
                            block4[:].rearrange("p (n k) -> p n k", k=4), ALU.mult)
                ins.then_inc(built, 1)
                for n in range(6):
                    dve.wait_ge(turned, n + 1)
                    dve.tensor_copy(bdt[:].rearrange("p q t n -> p (q t n)")[:, n * BANK:(n + 1) * BANK],
                                    ps[:, n % 2, :]).then_inc(copied, 1)
                dve.tensor_scalar(bd[:, 1], bd[:, 1], DH ** -0.5, None, ALU.mult).then_inc(scaled, 1)
                dve.wait_ge(folded, 1)
                dve.tensor_copy(wg2[:].rearrange("p t n -> p (t n)"), pw[:, 0:32 * KD]).then_inc(wg_ready, 1)
                dve.wait_ge(summed, 1)
                dve.tensor_tensor(g.gts[:], pg[:, 0:16 * NT].rearrange("p (c n) -> p c n", n=16),
                                  bg[:].rearrange("p (o n) -> p o n", o=1).to_broadcast([P, NT, 16]),
                                  ALU.add).then_inc(done, 1)

            @block.tensor
            def _(pe):
                pe.wait_ge(built, 1)
                for n in range(6):
                    if n >= 2:
                        pe.wait_ge(copied, n - 1)
                    for k in range(4):
                        q, t = divmod(4 * n + k, KD)
                        mm = pe.transpose(ps[:, n % 2, k * P:(k + 1) * P], bd[:, q, t, :], g.ident[:])
                    mm.then_inc(turned, 1)
                pe.wait_ge(copied, 6)
                for t in range(KD):
                    accumulate(nc, pw[:, t * 16:t * 16 + 16], [(bdt[:, q, t, :], wg[:, q * KD + t, :]) for q in (0, 1)])
                for t in range(KD):
                    mm = accumulate(nc, pw[:, (KD + t) * 16:(KD + t) * 16 + 16], [(bdt[:, 2, t, :], wg[:, 2 * KD + t, :])])
                mm.then_inc(folded, 1)
                pe.wait_ge(wg_ready, 1)
                for c in range(NT):
                    mm = accumulate(nc, pg[:, c * 16:c * 16 + 16],
                                    [(g.xc[:, t, c * P:(c + 1) * P], wg2[:, t, :]) for t in range(KD)]
                                    + [(g.xm[:, t, padded(c):padded(c) + P], wg2[:, KD + t, :]) for t in range(KD)])
                mm.then_inc(summed, 1)


def natural(u):
    return CT - 1 - u if u < CT else NT - 1 - (u - CT)


ROWS = 36
G_G, G_M, G_WI, G_EM, G_WK, G_KEEP = range(6)


def gate_rows(nc, g):
    io = g.io
    with Phase(nc, "gro") as ph:
        cat = ph.sb("cat", [P, NT, 2, ROWS])
        r = ph.sb("r", [ROWS, 2, N_ALL])
        b = ph.sb("b", [ROWS, N_ALL])
        e = ph.sb("e", [ROWS, N_ALL])
        reset = ph.sb("reset", [ROWS, N_ALL])
        m = ph.sb("m", [ROWS, NT + 1])
        qr = ph.sb("qr", [ROWS, 6, N_ALL])
        colp = ph.sb("colp", [P, NT, 6, ROWS])
        colb = ph.sb("colb", [P, NT, 6, 4])
        rv = ph.ps("rv", [P, BANK])
        tp = ph.ps("tp", [P, 2, BANK])
        loaded, cleared, rev_done, cat_done = ph.sem("loaded"), ph.sem("cleared"), ph.sem("rev_done"), ph.sem("cat_done")
        turned, copied, dve_step, act_step = ph.sem("turned"), ph.sem("copied"), ph.sem("dve_step"), ph.sem("act_step")
        to_act, rows_ready, colt, colc = ph.sem("to_act"), ph.sem("rows_ready"), ph.sem("colt"), ph.sem("colc")
        brev, bcopied = ph.sem("brev"), ph.sem("bcopied")
        stored = ph.sem("stored")
        N_T = 5
        n_col = (NT * 6 + 13) // 14
        with nc.Block() as block:
            @block.sync
            def _(sp):
                sp.dma_start(reset[:], io["t_reset"]).then_inc(loaded, 16)
                sp.wait_ge(bcopied, 2 * NT + 1)
                sp.dma_start(g.col_dram.rearrange("h p u q d -> p u q h d"), g.cols[:]).then_inc(stored, 16)
                sp.wait_ge(stored, 16)

            @block.gpsimd
            def _(pool):
                pool.memset(cat[:], 0.0).then_inc(cleared, 1)
                pool.memset(m[:], 0.0).then_inc(cleared, 1)

            @block.tensor
            def _(pe):
                nc.tensor.matmul(rv[:, 0:NT * 16], g.rev[:], g.gts[:].rearrange("p c n -> p (c n)"), start=True,
                                 stop=True).then_inc(rev_done, 1)
                pe.wait_ge(cat_done, 1 + NT)
                for n in range(N_T):
                    if n >= 2:
                        pe.wait_ge(copied, n - 1)
                    for k in range(4):
                        q, u = divmod(4 * n + k, NT)
                        mm = pe.transpose(tp[0:ROWS, n % 2, k * P:(k + 1) * P], cat[:, u, q, :], g.ident[:])
                    mm.then_inc(turned, 1)
                pe.wait_ge(rows_ready, 1)
                for n in range(n_col):
                    if n >= 2:
                        pe.wait_ge(colc, n - 1)
                    for k in range(min(14, NT * 6 - 14 * n)):
                        u, q = divmod(14 * n + k, 6)
                        mm = pe.transpose(tp[:, n % 2, k * ROWS:(k + 1) * ROWS], qr[:, q, u * P:(u + 1) * P],
                                          g.ident[0:ROWS, 0:ROWS])
                    mm.then_inc(colt, 1)
                pe.wait_ge(bcopied, 1)
                nc.tensor.matmul(rv[:, 0:NT * 24], g.rev[:], colb[:].rearrange("p u q h -> p (u q h)"), start=True,
                                 stop=True).then_inc(brev, 1)

            @block.scalar
            def _(act):
                act.wait_ge(to_act, 1)
                act.activation(e[:], e[:], ACT.Exp, scale=-1.0).then_inc(act_step, 1)
                act.wait_ge(act_step, 1)
                act.activation(e[:], e[:], ACT.Ln, bias=1.0).then_inc(act_step, 1)
                act.wait_ge(to_act, 2)
                act.activation(qr[:, G_WI, :], qr[:, G_WI, :], ACT.Exp)
                act.activation(qr[:, G_EM, :], qr[:, G_EM, :], ACT.Exp, scale=-1.0)
                act.activation(qr[:, G_WK, :], qr[:, G_WK, :], ACT.Exp)
                act.activation(qr[:, G_KEEP, :], qr[:, G_KEEP, :], ACT.Exp).then_inc(rows_ready, 1)

            @block.vector
            def _(dve):
                step = Steps(dve, dve_step)
                dve.wait_ge(cleared, 2)
                gv = g.gts[:].rearrange("p u (d q h) -> p u d q h", d=2, q=2)
                dve.tensor_copy(cat[:, :, :, 0:4], gv[:, :, 0]).then_inc(cat_done, 1)
                dve.wait_ge(rev_done, 1)
                rvv = rv[:, 0:NT * 16].rearrange("p (u d q h) -> p u d q h", u=NT, d=2, q=2)
                for u in range(NT):
                    dve.tensor_copy(cat[:, u, :, 32:36], rvv[:, natural(u), 1]).then_inc(cat_done, 1)
                for n in range(N_T):
                    dve.wait_ge(turned, n + 1)
                    dve.tensor_copy(r[:].rearrange("p q n -> p (q n)")[:, n * BANK:(n + 1) * BANK],
                                    tp[0:ROWS, n % 2, :]).then_inc(copied, 1)
                dve.wait_ge(copied, N_T)
                dve.scalar_tensor_tensor(e[:], r[:, 1, :], -1.0, r[:, 1, :], ALU.mult, ALU.max).then_inc(to_act, 1)
                dve.wait_ge(act_step, 2)
                step(dve.scalar_tensor_tensor(r[:, 1, :], r[:, 1, :], 0.0, e[:], ALU.min, ALU.subtract))
                dve.wait_ge(loaded, 16)
                step(dve.tensor_tensor_scan(b[:], reset[:], r[:, 1, :], 0.0, ALU.mult, ALU.add))
                step(dve.tensor_tensor(qr[:, G_G, :], r[:, 0, :], b[:], ALU.subtract))
                for u in range(NT):
                    a, z = u * P, (u + 1) * P
                    step(dve.tensor_tensor_scan(qr[:, G_M, a:z], qr[:, G_G, a:z], qr[:, G_G, a:z], m[:, u:u + 1],
                                                ALU.max, ALU.max))
                    step(dve.tensor_tensor(m[:, u + 1:u + 2], qr[:, G_M, z - 1:z], b[:, z - 1:z], ALU.add))
                tiles = lambda q: qr[:, q, :].rearrange("p (u t) -> p u t", t=P)
                at_start = m[:, 0:NT].rearrange("p (u o) -> p u o", o=1).to_broadcast([ROWS, NT, P])
                at_end = tiles(G_M)[:, :, P - 1:P].to_broadcast([ROWS, NT, P])
                step(dve.tensor_tensor(tiles(G_WI), at_start, tiles(G_M), ALU.subtract))
                step(dve.tensor_tensor(qr[:, G_EM, :], b[:], qr[:, G_M, :], ALU.add))
                step(dve.tensor_tensor(tiles(G_WK), tiles(G_G), at_end, ALU.subtract))
                dve.tensor_tensor(tiles(G_KEEP), at_start, at_end, ALU.subtract).then_inc(to_act, 1)
                flat = colp[:].rearrange("p u q r -> p (u q r)")
                for n in range(n_col):
                    w = min(14, NT * 6 - 14 * n) * ROWS
                    dve.wait_ge(colt, n + 1)
                    dve.tensor_copy(flat[:, n * 14 * ROWS:n * 14 * ROWS + w], tp[:, n % 2, 0:w]).then_inc(colc, 1)
                dve.wait_ge(colc, n_col)
                dve.tensor_copy(colb[:], colp[:, :, :, 32:36]).then_inc(bcopied, 1)
                for u in range(NT):
                    dve.tensor_copy(g.cols[:, u, :, :, 0], colp[:, u, :, 0:4]).then_inc(bcopied, 1)
                dve.wait_ge(brev, 1)
                rb = rv[:, 0:NT * 24].rearrange("p (u q h) -> p u q h", u=NT, q=6)
                for u in range(NT):
                    dve.tensor_copy(g.cols[:, u, :, :, 1], rb[:, u]).then_inc(bcopied, 1)


def mlstm(nc, g):
    io = g.io
    with Phase(nc, "mls") as ph:
        xc = ph.sb("xc", [P, 2, 2, N_ALL])
        xm = ph.sb("xm", [P, 2, 2, W_PAD])
        bd = ph.sb("bd", [P, 2, 2, 3, P])
        col = ph.sb("col", [P, 2, NT, 6, 2])
        qT = ph.sb("qT", [P, 2, N_LAT])
        kT = ph.sb("kT", [P, 2, N_LAT])
        k = ph.sb("k", [P, NT, DH])
        v = ph.sb("v", [P, NT, DH + 1])
        diag = ph.sb("diag", [P, 2, P])
        x1 = ph.sb("x1", [P, 2, P])
        e = ph.sb("e", [P, 2, P])
        pm = ph.sb("pm", [P, 2, P])
        vw = ph.sb("vw", [P, 2, DH + 1])
        ct = ph.sb("ct", [P, 2, 2, DH + 1])
        ti = ph.sb("ti", [P, 2, DH])
        num = ph.sb("num", [P, 2, DH])
        den = ph.sb("den", [P, 2, 2])
        dn = ph.sb("dn", [P, 4, 2])
        sb_ = ph.ps("s", [P, 2, BANK])
        hb = ph.ps("h", [P, 2, BANK])
        ub = ph.ps("u", [P, 2, 2, BANK])
        S, H, U = sb_, hb, ub
        ld = [ph.sem(f"ld{j}") for j in range(2)]
        full = [ph.sem(f"full{b}") for b in range(2)]
        free = [ph.sem(f"free{b}") for b in range(2)]
        ones_set, diag_ready, s_done, x1_done = ph.sem("ones_set"), ph.sem("diag_ready"), ph.sem("s_done"), ph.sem("x1_done")
        e_done, p_ready, vw_ready, u_done = ph.sem("e_done"), ph.sem("p_ready"), ph.sem("vw_ready"), ph.sem("u_done")
        ct_done, inter_done, ti_done, intra_done = (ph.sem("ct_done"), ph.sem("inter_done"), ph.sem("ti_done"),
                                                    ph.sem("intra_done"))
        den_done, h_done, dve_step = ph.sem("den_done"), ph.sem("h_done"), ph.sem("dve_step")
        PU = 18
        NU, NO = 2 * (NT - 1), 2 * LT

        def tile_of(u, d):
            return u if d == 0 else natural(u)

        def projections(j):
            out = []
            for q, dst in ((0, qT), (1, kT)):
                for t in range(2):
                    for c in range(2):
                        out.append((dst[:, t, c * BANK:(c + 1) * BANK],
                                    [(0, BANK, bd[:, j, t, q, :], xc[:, j, t, N_CTX + c * BANK:N_CTX + (c + 1) * BANK])]))
            for q, dst in ((1, k), (2, v)):
                for c in range(0, NT, 2):
                    parts = []
                    for a in range(2):
                        for t in range(2):
                            lhs = xc[:, j, t, (c + a) * P:(c + a + 1) * P] if q == 1 else \
                                xm[:, j, t, padded(c + a):padded(c + a) + P]
                            parts.append((a * DH + t * P, P, lhs, bd[:, j, t, q, :]))
                    out.append((dst[:, c:c + 2, 0:DH], parts))
            return out

        with nc.Block() as block:
            @block.sync
            def _(sp):
                for head in range(ML_HEADS):
                    j = head % 2
                    if head >= 2:
                        sp.wait_ge(h_done, (head - 1) * NO + 1)
                    sp.dma_start(bd[:, j], g.bd_dram[2 * head:2 * head + 2].rearrange("t p q n -> p t q n")).then_inc(ld[j], 16)
                    sp.dma_start(xc[:, j], g.xc_dram[2 * head:2 * head + 2].rearrange("t p n -> p t n")).then_inc(ld[j], 16)
                    sp.dma_start(xm[:, j], g.xm_dram[2 * head:2 * head + 2].rearrange("t p n -> p t n")).then_inc(ld[j], 16)
                    sp.dma_start(col[:, j], g.col_dram[head]).then_inc(ld[j], 16)

            @block.gpsimd
            def _(pool):
                pool.memset(v[:, :, DH:DH + 1], 1.0).then_inc(ones_set, 1)
                pool.wait_ge(ones_set, 1)
                with pool.Fori(0, ML_HEADS // 2) as i:
                    for j in range(2):
                        head = 2 * i + j
                        pool.wait_ge(ld[j], 64 * (i + 1))
                        for b in range(2):
                            pool.wait_ge(free[b], (head + 1) * (PU // 2) + 1)
                        for u in range(NT):
                            for d in range(2):
                                c, n = tile_of(u, d), 2 * u + d
                                if u < NT - 1:
                                    if n >= 2:
                                        pool.wait_ge(u_done, head * NU + n)
                                    else:
                                        pool.wait_ge(u_done, head * NU + 1)
                                    pool.tensor_tensor(vw[:, d, :], v[:, c, :], col[:, j, u, G_WK, d:d + 1]
                                                       .to_broadcast([P, DH + 1]), ALU.mult).then_inc(vw_ready, 1)
                            for d in range(2):
                                if u >= CT:
                                    m = 2 * (u - CT) + d
                                    pool.wait_ge(s_done, head * NO + max(m, 1))
                                    pool.tensor_tensor(diag[:, d, :], g.ident[:], col[:, j, u, G_M, d:d + 1]
                                                       .to_broadcast([P, P]), ALU.mult).then_inc(diag_ready, 1)

            @block.tensor
            def _(pe):
                pe.wait_ge(ones_set, 1)
                pe.sem_inc(u_done, 1)
                pe.sem_inc(s_done, 1)
                with pe.Fori(0, ML_HEADS // 2) as i:
                    for j in range(2):
                        head = 2 * i + j
                        pe.wait_ge(ld[j], 64 * (i + 1))
                        pe.wait_ge(ct_done, head * NU + 1)
                        for n, (dst, parts) in enumerate(projections(j)):
                            b = n % 2
                            pe.wait_ge(free[b], head * (PU // 2) + n // 2 + 1)
                            for at, w, lhsT, rhs in parts:
                                mm = accumulate(nc, U[:, 0, b, at:at + w], [(lhsT, rhs)])
                            mm.then_inc(full[b], 1)
                        for b in range(2):
                            pe.wait_ge(free[b], (head + 1) * (PU // 2) + 1)
                        for u in range(NT):
                            if u >= CT:
                                for d in range(2):
                                    c, m = tile_of(u, d) - CT, 2 * (u - CT) + d
                                    pe.wait_ge(diag_ready, head * NO + m + 1)
                                    pe.wait_ge(den_done, head * LT + u - CT + 1)
                                    accumulate(nc, S[:, d, 0:P], [(g.ones[:], diag[:, d, :])])
                                    accumulate(nc, S[:, d, P:2 * P], [
                                        (kT[:, t, c * P:(c + 1) * P], qT[:, t, c * P:(c + 1) * P])
                                        for t in range(2)]).then_inc(s_done, 1)
                            for d in range(2):
                                c, n = tile_of(u, d), 2 * u + d
                                if u >= CT:
                                    m = 2 * (u - CT) + d
                                    pe.wait_ge(ct_done, head * NU + n)
                                    pe.wait_ge(h_done, head * NO + max(m, 1))
                                    accumulate(nc, H[:, d, DH:2 * DH], [
                                        (qT[:, t, (c - CT) * P:(c - CT + 1) * P], ct[:, d, t, 0:DH])
                                        for t in range(2)]).then_inc(inter_done, 1)
                                if u < NT - 1:
                                    pe.wait_ge(vw_ready, head * NU + n + 1)
                                    pe.wait_ge(ct_done, head * NU + max(n, 1))
                                    if u >= CT:
                                        pe.wait_ge(p_ready, head * NO + 2 * (u - CT) + d + 1)
                                        accumulate(nc, S[:, d, 2 * P + 1:2 * P + 2], [
                                            (qT[:, t, (c - CT) * P:(c - CT + 1) * P], ct[:, d, t, DH:DH + 1])
                                            for t in range(2)])
                                    for t in range(2):
                                        mm = accumulate(nc, U[:, d, t, 0:DH + 1], [(k[:, c, t * P:(t + 1) * P], vw[:, d, :])])
                                    mm.then_inc(u_done, 1)
                            if u >= CT:
                                for d in range(2):
                                    c, m = tile_of(u, d), 2 * (u - CT) + d
                                    pe.wait_ge(p_ready, head * NO + m + 1)
                                    pe.wait_ge(ti_done, head * NO + m + 1)
                                    if u == NT - 1:
                                        accumulate(nc, S[:, d, 2 * P + 1:2 * P + 2], [
                                            (qT[:, t, (c - CT) * P:(c - CT + 1) * P], ct[:, d, t, DH:DH + 1])
                                            for t in range(2)])
                                    accumulate(nc, S[:, d, 2 * P:2 * P + 1], [(pm[:, d, :], v[:, c, DH:DH + 1])])
                                    accumulate(nc, H[:, d, 0:DH], [(pm[:, d, :], v[:, c, 0:DH])]).then_inc(intra_done, 1)

            @block.scalar
            def _(act):
                act.sem_inc(free[0], 1)
                act.sem_inc(free[1], 1)
                with act.Fori(0, ML_HEADS // 2) as i:
                    for j in range(2):
                        head = 2 * i + j
                        for n, (dst, parts) in enumerate(projections(j)):
                            if n % 2 == 0:
                                act.wait_ge(full[0], head * (PU // 2) + n // 2 + 1)
                                src = U[:, 0, 0, :] if n < 8 else U[:, 0, 0, :].rearrange("p (a n) -> p a n", a=2)
                                act.activation(dst, src, ACT.Copy).then_inc(free[0], 1)
                        for u in range(CT, NT):
                            for d in range(2):
                                m = 2 * (u - CT) + d
                                act.wait_ge(x1_done, head * NO + m + 1)
                                act.activation(e[:, d, :], x1[:, d, :], ACT.Exp, scale=-1.0).then_inc(e_done, 1)
                            for d in range(2):
                                m = 2 * (u - CT) + d
                                act.wait_ge(inter_done, head * NO + m + 1)
                                act.activation(ti[:, d, :], H[:, d, DH:2 * DH], ACT.Copy,
                                               scale=col[:, j, u, G_WI, d:d + 1]).then_inc(ti_done, 1)

            @block.vector
            def _(dve):
                step = Steps(dve, dve_step)
                for s in (ct_done, den_done, h_done):
                    dve.sem_inc(s, 1)
                with dve.Fori(0, ML_HEADS // 2) as i:
                    step.n = 0
                    per_round = 2 * LT * 7
                    step.base = i * per_round
                    for j in range(2):
                        head = 2 * i + j
                        dve.wait_ge(ld[j], 64 * (i + 1))
                        for n, (dst, parts) in enumerate(projections(j)):
                            if n % 2 == 1:
                                dve.wait_ge(full[1], head * (PU // 2) + n // 2 + 1)
                                src = U[:, 0, 1, :] if n < 8 else U[:, 0, 1, :].rearrange("p (a n) -> p a n", a=2)
                                dve.tensor_copy(dst, src).then_inc(free[1], 1)
                        for u in range(NT):
                            if u >= CT:
                                for d in range(2):
                                    m = 2 * (u - CT) + d
                                    dve.wait_ge(s_done, head * NO + m + 2)
                                    dve.scalar_tensor_tensor(x1[:, d, :], S[:, d, 0:P], col[:, j, u, G_G, d:d + 1],
                                                             g.causal[:, d, :], ALU.subtract, ALU.add).then_inc(x1_done, 1)
                                for d in range(2):
                                    m = 2 * (u - CT) + d
                                    dve.wait_ge(e_done, head * NO + m + 1)
                                    dve.tensor_tensor(pm[:, d, :], e[:, d, :], S[:, d, P:2 * P],
                                                      ALU.mult).then_inc(p_ready, 1)
                            if u < NT - 1:
                                for d in range(2):
                                    n = 2 * u + d
                                    dve.wait_ge(u_done, head * NU + n + 2)
                                    for t in range(2):
                                        if u == 0:
                                            ins = dve.tensor_copy(ct[:, d, t, :], U[:, d, t, 0:DH + 1])
                                        else:
                                            ins = dve.scalar_tensor_tensor(
                                                ct[:, d, t, :], ct[:, d, t, :], col[:, j, u, G_KEEP, d:d + 1],
                                                U[:, d, t, 0:DH + 1], ALU.mult, ALU.add)
                                    ins.then_inc(ct_done, 1)
                            if u >= CT:
                                m = 2 * (u - CT)
                                dve.wait_ge(intra_done, head * NO + m + 2)
                                dve.tensor_copy(den[:], S[:, :, 2 * P:2 * P + 2]).then_inc(den_done, 1)
                                dve.wait_ge(den_done, head * LT + u - CT + 2)
                                step(dve.tensor_tensor(dn[:, 0, :], den[:, :, 1], col[:, j, u, G_WI, :], ALU.mult))
                                step(dve.tensor_tensor(dn[:, 1, :], dn[:, 0, :], den[:, :, 0], ALU.add))
                                step(dve.scalar_tensor_tensor(dn[:, 2, :], dn[:, 1, :], -1.0, dn[:, 1, :], ALU.mult, ALU.max))
                                step(dve.tensor_tensor(dn[:, 2, :], dn[:, 2, :], col[:, j, u, G_EM, :], ALU.max))
                                step(dve.reciprocal(dn[:, 3, :], dn[:, 2, :]))
                                for d in range(2):
                                    step(dve.tensor_tensor(num[:, d, :], ti[:, d, :], H[:, d, 0:DH], ALU.add))
                                for d in range(2):
                                    c = tile_of(u, d) - CT
                                    dst = g.hs[:, c, ds(head * DH, DH)]
                                    first = u - CT < LT // 2
                                    if first:
                                        ins = dve.tensor_scalar(dst, num[:, d, :], dn[:, 3, d:d + 1], None, ALU.mult)
                                    else:
                                        ins = dve.scalar_tensor_tensor(dst, num[:, d, :], dn[:, 3, d:d + 1], dst,
                                                                       ALU.mult, ALU.add)
                                    ins.then_inc(h_done, 1)
                    assert step.n == per_round


def readout(nc, g):
    io = g.io
    with Phase(nc, "rdo") as ph:
        ss = ph.sb("ss", [P, LT, ML_HEADS])
        hn = ph.sb("hn", [P, KD, N_LAT])
        w = ph.sb("w", [P, 2, KD, P])
        sig = ph.sb("sig", [P, 2, N_LAT])
        xc = ph.sb("xc", [P, 2, N_LAT])
        y = ph.sb("y", [P, 2, N_LAT])
        tp = ph.ps("tp", [P, 4, BANK])
        ps = ph.ps("ps", [P, 2, 2, BANK])
        squared, var_done, root_done, inv_done, scaled = (ph.sem("squared"), ph.sem("var_done"), ph.sem("root_done"),
                                                          ph.sem("inv_done"), ph.sem("scaled"))
        turned = ph.sem("turned")
        out_of = [ph.sem(f"out_of{b}") for b in range(2)]
        w_in = [ph.sem(f"w_in{j}") for j in range(2)]
        xy_in = [ph.sem(f"xy_in{j}") for j in range(2)]
        tile_done, sig_done, merged, stored, dve_step = (ph.sem("tile_done"), ph.sem("sig_done"), ph.sem("merged"),
                                                         ph.sem("stored"), ph.sem("dve_step"))
        wv = io["w_in"].rearrange("(k p) n -> p k n", p=P)
        with nc.Block() as block:
            @block.sync
            def _(sp):
                with sp.Fori(0, KD) as t:
                    for j, col in ((0, COL_Z), (1, COL_GML)):
                        sp.wait_ge(tile_done, 2 * t + j + 1)
                        sp.dma_start(w[:, j], wv[:, :, ds(col + t * P, P)]).then_inc(w_in[j], 16)

            @block.gpsimd
            def _(pool):
                with pool.Fori(0, KD // 2) as i:
                    for j in range(2):
                        t = 2 * i + j
                        pool.wait_ge(merged, t + 1)
                        pool.dma_start(xc[:, j:j + 1, :], g.xc_dram[ds(t, 1), :, N_CTX:].rearrange("o p n -> p o n")
                                       ).then_inc(xy_in[j], 16)
                        pool.dma_start(y[:, j:j + 1, :], g.y_dram[ds(t, 1)].rearrange("o p n -> p o n")
                                       ).then_inc(xy_in[j], 16)

            @block.tensor
            def _(pe):
                for t in range(KD):
                    for half in range(2):
                        n = 2 * t + half
                        if n == 0:
                            pe.wait_ge(scaled, LT)
                        if n >= 4:
                            pe.wait_ge(out_of[n % 2], n // 2 - 1)
                        for c in range(4):
                            mm = pe.transpose(tp[:, n % 4, c * P:(c + 1) * P],
                                              g.hs[:, 4 * half + c, t * P:(t + 1) * P], g.ident[:])
                        mm.then_inc(turned, 1)
                credit(pe, tile_done, 2)
                with pe.Fori(0, KD) as t:
                    for j in range(2):
                        pe.wait_ge(w_in[j], 16 * (t + 1))
                        pe.wait_ge(sig_done, 2 * t + j + 1)
                        for c, (c0, cn) in enumerate(LAT_CHUNKS):
                            mm = accumulate(nc, ps[:, j, c, :], [(w[:, j, k, :], g.hT[:, k, c0:c0 + cn])
                                                                 for k in range(KD)])
                        mm.then_inc(tile_done, 1)

            @block.scalar
            def _(act):
                for c in range(LT):
                    for h in range(ML_HEADS):
                        ins = act.activation(hn[:, c, h * DH:(h + 1) * DH], g.hs[:, c, h * DH:(h + 1) * DH], ACT.Square,
                                             accum_out=ss[:, c, h:h + 1])
                ins.then_inc(squared, 1)
                act.wait_ge(var_done, 1)
                act.activation(ss[:], ss[:], ACT.Sqrt).then_inc(root_done, 1)
                for n in range(0, 2 * KD, 2):
                    act.wait_ge(turned, n + 1)
                    act.activation(hn[:, n // 2, 0:BANK], tp[:, n % 4, :], ACT.Copy).then_inc(out_of[0], 1)
                credit(act, sig_done, 2)
                with act.Fori(0, KD) as t:
                    for j in range(2):
                        act.wait_ge(tile_done, 2 * t + j + 3)
                        act.wait_ge(merged, t + 2)
                        act.activation(sig[:, j, :], ps[:, j].rearrange("p c n -> p (c n)"),
                                       ACT.Sigmoid).then_inc(sig_done, 1)

            @block.vector
            def _(dve):
                dve.wait_ge(squared, 1)
                dve.tensor_scalar(ss[:], ss[:], 1.0 / DH, EPS, ALU.mult, ALU.add).then_inc(var_done, 1)
                dve.wait_ge(root_done, 1)
                dve.reciprocal(ss[:], ss[:]).then_inc(inv_done, 1)
                dve.wait_ge(inv_done, 1)
                for c in range(LT):
                    hv = g.hs[:, c, :].rearrange("p (h n) -> p h n", h=ML_HEADS)
                    dve.tensor_tensor(hv, hv, ss[:, c, :].rearrange("p (h o) -> p h o", o=1).to_broadcast(
                        [P, ML_HEADS, DH]), ALU.mult).then_inc(scaled, 1)
                for n in range(1, 2 * KD, 2):
                    dve.wait_ge(turned, n + 1)
                    dve.tensor_copy(hn[:, n // 2, BANK:], tp[:, n % 4, :]).then_inc(out_of[1], 1)
                credit(dve, merged, 2)
                for b in range(2):
                    dve.wait_ge(out_of[b], KD)
                step = Steps(dve, dve_step)
                with dve.Fori(0, KD // 2) as i:
                    step.n, step.base = 0, i * 8
                    for j in range(2):
                        t = 2 * i + j
                        h = hn[:, ds(t, 1), :].rearrange("p o n -> p (o n)")
                        dve.wait_ge(xy_in[j], 32 * (i + 1))
                        step(dve.tensor_scalar(xc[:, j, :], xc[:, j, :], g.pa[:, ds(PA_SKIP + t, 1)], None, ALU.mult))
                        step(dve.scalar_tensor_tensor(h, h, g.pa[:, ds(PA_MLN + t, 1)], xc[:, j, :], ALU.mult, ALU.add))
                        dve.wait_ge(sig_done, 2 * t + 4)
                        step(dve.tensor_tensor(h, h, sig[:, 0, :], ALU.mult))
                        step(dve.tensor_tensor(h, h, sig[:, 1, :], ALU.mult))
                        dve.tensor_tensor(h, h, y[:, j, :], ALU.add).then_inc(merged, 1)
        with nc.Block() as block:
            @block.sync
            def _(sp):
                sp.wait_ge(merged, KD + 2)
                sp.dma_start(g.m_dram.rearrange("t p n -> p t n"), hn[:]).then_inc(stored, 16)
                sp.wait_ge(stored, 16)


def merge(nc, g):
    io = g.io
    with Phase(nc, "mrg") as ph:
        mT = ph.sb("mT", [P, KD, N_LAT])
        w = ph.sb("w", [P, KD, D])
        wr = ph.sb("wr", [P, KD, N_EXP])
        g1, a2, b2, n2 = (ph.sb(n, [P, D]) for n in ("g1", "a2", "b2", "n2"))
        x = ph.sb("x", [P, 2, D])
        h2 = ph.sb("h2", [P, 2, D])
        h2T = ph.sb("h2T", [P, 2, D])
        junk = ph.sb("junk", [P, D])
        st = ph.sb("st", [P, 2, 8])
        pr = ph.sb("pr", [P, 2, N_EXP])
        acc = ph.ps("acc", [P, 2, 2, BANK])
        tp = ph.ps("tp", [P, 2, BANK])
        lg = ph.ps("lg", [P, BANK])
        at = ph.ps("at", [P, BANK])
        loaded, rows_ready = ph.sem("loaded"), ph.sem("rows_ready")
        x_in = [ph.sem(f"x_in{j}") for j in range(2)]
        stored = [ph.sem(f"stored{j}") for j in range(2)]
        multiplied, x1_done, squared, var_done, root_done = (ph.sem(n) for n in (
            "multiplied", "x1_done", "squared", "var_done", "root_done"))
        h2_done, turned, h2t_done, logits, nmax, exped, aff, aff_t, aff_c, dve_step = (ph.sem(n) for n in (
            "h2_done", "turned", "h2t_done", "logits", "nmax", "exped", "aff", "aff_t", "aff_c", "dve_step"))
        with nc.Block() as block:
            @block.sync
            def _(sp):
                sp.dma_start(mT[:], g.m_dram.rearrange("t p n -> p t n")).then_inc(loaded, 16)
                sp.dma_start(w[:], io["w_out"].rearrange("(k p) n -> p k n", p=P)).then_inc(loaded, 16)
                sp.dma_start(wr[:], io["w_router"].rearrange("(k p) n -> p k n", p=P)).then_inc(loaded, 16)
                sp.dma_start(g1[:], spread(g.modrow[0, 2 * D:3 * D])).then_inc(loaded, 16)
                sp.dma_start(b2[:], spread(g.modrow[0, 3 * D:4 * D])).then_inc(loaded, 16)
                sp.dma_start(a2[:], spread(g.modrow[0, 4 * D:5 * D])).then_inc(loaded, 16)
                sp.dma_start(n2[:], spread(io["norm2"])).then_inc(loaded, 16)
                for n in range(LT):
                    if n >= 2:
                        sp.wait_ge(stored[n % 2], 32 * (n // 2))
                    sp.dma_start(x[:, n % 2, :], io["x"][n * P:(n + 1) * P, :]).then_inc(x_in[n % 2], 16)

            @block.gpsimd
            def _(pool):
                for n in range(LT):
                    pool.wait_ge(h2_done, n + 1)
                    pool.dma_start(g.x1[n * P:(n + 1) * P, :], x[:, n % 2, :]).then_inc(stored[n % 2], 16)
                    pool.dma_start(g.h2[n * P:(n + 1) * P, :], h2[:, n % 2, :]).then_inc(stored[n % 2], 16)
                for j in range(2):
                    pool.wait_ge(stored[j], 16 * LT)

            @block.tensor
            def _(pe):
                def multiply(n):
                    if n >= 2:
                        pe.wait_ge(x1_done, n - 1)
                    for c in range(2):
                        mm = accumulate(nc, acc[:, n % 2, c, :], [
                            (mT[:, k, n * P:(n + 1) * P], w[:, k, c * BANK:(c + 1) * BANK]) for k in range(KD)])
                    mm.then_inc(multiplied, 1)

                def route_tile(n):
                    pe.wait_ge(h2_done, n + 1)
                    pe.wait_ge(h2t_done, 2 * n)
                    for b in range(2):
                        for k in range(4):
                            mm = pe.transpose(tp[:, b, k * P:(k + 1) * P],
                                              h2[:, n % 2, (4 * b + k) * P:(4 * b + k + 1) * P], g.ident[:])
                        mm.then_inc(turned, 1)
                    pe.wait_ge(h2t_done, 2 * n + 2)
                    pe.wait_ge(aff, n)
                    accumulate(nc, lg[:, 0:N_EXP], [(h2T[:, n % 2, k * P:(k + 1) * P], wr[:, k, :])
                                                    for k in range(KD)]).then_inc(logits, 1)
                    pe.wait_ge(aff, n + 1)
                    pe.wait_ge(aff_c, n)
                    pe.transpose(at[0:N_EXP, 0:P], pr[:, n % 2, :], g.ident[:]).then_inc(aff_t, 1)

                pe.wait_ge(loaded, 16 * 7)
                multiply(0)
                for n in range(LT):
                    if n + 1 < LT:
                        multiply(n + 1)
                    route_tile(n)

            @block.scalar
            def _(act):
                for n in range(LT):
                    j = n % 2
                    act.wait_ge(x1_done, n + 1)
                    act.activation(junk[:], x[:, j, :], ACT.Square, accum_out=st[:, j, 0:1]).then_inc(squared, 1)
                    act.wait_ge(var_done, n + 1)
                    act.activation(st[:, j, 2:3], st[:, j, 1:2], ACT.Sqrt).then_inc(root_done, 1)
                    for b in range(2):
                        act.wait_ge(turned, 2 * n + b + 1)
                        act.activation(h2T[:, j, b * BANK:(b + 1) * BANK], tp[:, b, :], ACT.Copy).then_inc(h2t_done, 1)
                    act.wait_ge(nmax, n + 1)
                    act.activation(pr[:, j, :], lg[:, 0:N_EXP], ACT.Exp, bias=st[:, j, 4:5],
                                   accum_out=st[:, j, 5:6]).then_inc(exped, 1)

            @block.vector
            def _(dve):
                step = Steps(dve, dve_step)
                dve.wait_ge(loaded, 16 * 7)
                step(dve.scalar_tensor_tensor(a2[:], a2[:], 1.0, n2[:], ALU.add, ALU.mult))
                for n in range(LT):
                    j = n % 2
                    dve.wait_ge(multiplied, n + 1)
                    if n >= 2:
                        dve.wait_ge(stored[j], 32 * (n // 2))
                    step(dve.tensor_tensor(h2[:, j, :], acc[:, j].rearrange("p c n -> p (c n)"), g1[:], ALU.mult))
                    dve.wait_ge(x_in[j], 16 * (n // 2 + 1))
                    dve.tensor_tensor(x[:, j, :], x[:, j, :], h2[:, j, :], ALU.add).then_inc(x1_done, 1)
                    dve.wait_ge(squared, n + 1)
                    dve.tensor_scalar(st[:, j, 1:2], st[:, j, 0:1], 1.0 / D, EPS, ALU.mult, ALU.add).then_inc(var_done, 1)
                    dve.wait_ge(root_done, n + 1)
                    step(dve.reciprocal(st[:, j, 3:4], st[:, j, 2:3]))
                    step(dve.scalar_tensor_tensor(h2[:, j, :], x[:, j, :], st[:, j, 3:4], a2[:], ALU.mult, ALU.mult))
                    dve.tensor_tensor(h2[:, j, :], h2[:, j, :], b2[:], ALU.add).then_inc(h2_done, 1)
                    dve.wait_ge(logits, n + 1)
                    step(dve.tensor_reduce(st[:, j, 6:7], lg[:, 0:N_EXP], AX.X, ALU.max))
                    dve.tensor_scalar(st[:, j, 4:5], st[:, j, 6:7], -1.0, None, ALU.mult).then_inc(nmax, 1)
                    dve.wait_ge(exped, n + 1)
                    step(dve.reciprocal(st[:, j, 7:8], st[:, j, 5:6]))
                    dve.tensor_scalar(pr[:, j, :], pr[:, j, :], st[:, j, 7:8], None, ALU.mult).then_inc(aff, 1)
                    dve.wait_ge(aff_t, n + 1)
                    dve.tensor_copy(g.affT[:, n * P:(n + 1) * P], at[0:N_EXP, 0:P]).then_inc(aff_c, 1)


def route(nc, g):
    with Phase(nc, "rte") as ph:
        work = ph.sb("work", [N_EXP, 2, N_LAT])
        val = ph.sb("val", [N_EXP, CAP])
        idx = ph.sb("idx", [N_EXP, CAP], U32)
        idf = ph.sb("idf", [N_EXP, CAP])
        zero = ph.sb("zero", [P, D])
        tp = ph.ps("tp", [P, BANK])
        dve_step, found, turned, cleared, stored = (ph.sem(n) for n in (
            "dve_step", "found", "turned", "cleared", "stored"))
        with nc.Block() as block:
            @block.gpsimd
            def _(pool):
                pool.memset(zero[:], 0.0).then_inc(cleared, 1)
                pool.wait_ge(cleared, 1)
                for n in range(LT):
                    pool.dma_start(g.moe[n * P:(n + 1) * P, :], zero[:]).then_inc(stored, 16)
                pool.wait_ge(stored, 16 * LT)

            @block.vector
            def _(dve):
                step = Steps(dve, dve_step)
                src = g.affT
                for r in range(CAP // 8):
                    cur = g.affT[:, :] if r == 0 else work[:, (r - 1) % 2, :]
                    a = slice(8 * r, 8 * r + 8)
                    step(dve.max(val[:, a], cur))
                    dve.max_index(idx[:, a], val[:, a], cur)
                    step(dve.match_replace(work[:, r % 2, :], val[:, a], cur, -1.0))
                dve.tensor_copy(idf[:], idx[:]).then_inc(found, 1)
                dve.wait_ge(turned, 1)
                step(dve.tensor_copy(g.gval[:], tp[:, 0:N_EXP]))
                step(dve.tensor_copy(g.gidx[:], tp[:, N_EXP:2 * N_EXP]))

            @block.tensor
            def _(pe):
                pe.wait_ge(found, 1)
                pe.transpose(tp[:, 0:N_EXP], val[:], g.ident[0:N_EXP, 0:N_EXP])
                pe.transpose(tp[:, N_EXP:2 * N_EXP], idf[:], g.ident[0:N_EXP, 0:N_EXP]).then_inc(turned, 1)


def experts(nc, g):
    io = g.io
    with Phase(nc, "exp") as ph:
        w = ph.sb("w", [P, 6, KD, BANK])
        ix = ph.sb("ix", [P, 2], U32)
        xs = ph.sb("xs", [P, D])
        xsT = ph.sb("xsT", [P, D])
        act_a = ph.sb("act_a", [P, FF])
        hid = ph.sb("hid", [P, FF])
        hidT = ph.sb("hidT", [P, FF])
        y = ph.sb("y", [P, D])
        gu = ph.ps("gu", [P, 4, BANK])
        tp = ph.ps("tp", [P, 2, BANK])
        dn = ph.ps("dn", [P, 2, BANK])
        w_in = [ph.sem(f"w_in{s}") for s in range(6)]
        used = [ph.sem(f"used{s}") for s in range(6)]
        names = ("ix_ready", "gathered", "x_turned", "xt_done", "silu_done", "hid_done", "h_turned", "ht_done",
                 "y_done", "scattered")
        to_ready, may_go, y_free = ph.sem("to_ready"), ph.sem("may_go"), ph.sem("y_free")
        ix_ready, gathered, x_turned, xt_done, silu_done, hid_done, h_turned, ht_done, y_done, scattered = (
            ph.sem(n) for n in names)
        views = [io[n].rearrange("e (k p) n -> e p k n", p=P) for n in ("w_e_gate", "w_e_up", "w_e_down")]
        with nc.Block() as block:
            @block.sync
            def _(sp):
                with sp.Fori(0, N_EXP) as e:
                    for s in range(6):
                        src = views[s % 2] if s < 4 else views[2]
                        half = s // 2 if s < 4 else s - 4
                        sp.wait_ge(used[s], e + 1)
                        sp.dma_start(w[:, s:s + 1], src[ds(e, 1), :, :, half * BANK:(half + 1) * BANK]
                                     .rearrange("e p k n -> p e k n")).then_inc(w_in[s], 16)

            @block.gpsimd
            def _(pool):
                def gather(e):
                    if not isinstance(e, int):
                        pool.wait_ge(x_turned, 2 * e)
                    if isinstance(e, int):
                        pool.tensor_copy(ix[:, 0:1], g.gidx[:, e:e + 1]).then_inc(ix_ready, 1)
                    else:
                        pool.tensor_copy(ix[:, 0:1], g.gidx[:, ds(e, 1)]).then_inc(ix_ready, 1)
                    pool.wait_ge(ix_ready, e + 1)
                    pool.sem_inc(may_go, 1)
                    pool.indirect_dma_start(xs[:], None, g.h2, bass.IndirectOffsetOnAxis(ix[:, 0:1], 0)
                                            ).then_inc(gathered, 16)

                def scatter(e):
                    pool.tensor_copy(ix[:, 1:2], g.gidx[:, ds(e, 1)] if not isinstance(e, int) else g.gidx[:, e:e + 1]
                                     ).then_inc(to_ready, 1)
                    pool.wait_ge(to_ready, e + 1)
                    pool.wait_ge(y_done, e + 2)
                    pool.sem_inc(may_go, 1)
                    pool.indirect_dma_start(g.moe, bass.IndirectOffsetOnAxis(ix[:, 1:2], 0), y[:], None,
                                            compute_op=ALU.add).then_inc(scattered, 16)
                    pool.wait_ge(scattered, 16 * (e + 1))
                    pool.sem_inc(y_free, 1)

                pool.sem_inc(y_free, 1)
                gather(0)
                with pool.Fori(0, N_EXP - 1) as e:
                    gather(e + 1)
                    scatter(e)
                scatter(N_EXP - 1)

            @block.tensor
            def _(pe):
                for s in range(6):
                    credit(pe, used[s], 1)

                def turn_x(e):
                    pe.wait_ge(gathered, 16 * (e + 1))
                    for b in range(2):
                        for k in range(4):
                            mm = pe.transpose(tp[:, b, k * P:(k + 1) * P], xs[:, (4 * b + k) * P:(4 * b + k + 1) * P],
                                              g.ident[:])
                        mm.then_inc(x_turned, 1)

                def one(e, more):
                    pe.wait_ge(xt_done, 2 * e + 2)
                    pe.wait_ge(hid_done, 2 * e + 1)
                    for s in range(4):
                        pe.wait_ge(w_in[s], 16 * (e + 1))
                        accumulate(nc, gu[:, s, :], [(xsT[:, k * P:(k + 1) * P], w[:, s, k, :])
                                                     for k in range(KD)]).then_inc(used[s], 1)
                    pe.wait_ge(hid_done, 2 * e + 3)
                    for b in range(2):
                        for k in range(4):
                            mm = pe.transpose(tp[:, b, k * P:(k + 1) * P], hid[:, (4 * b + k) * P:(4 * b + k + 1) * P],
                                              g.ident[:])
                        mm.then_inc(h_turned, 1)
                    pe.wait_ge(ht_done, 2 * e + 2)
                    if more:
                        turn_x(e + 1)
                    pe.wait_ge(y_done, e + 1)
                    for b in range(2):
                        s = 4 + b
                        pe.wait_ge(w_in[s], 16 * (e + 1))
                        accumulate(nc, dn[:, b, :], [(hidT[:, k * P:(k + 1) * P], w[:, s, k, :])
                                                     for k in range(FT)]).then_inc(used[s], 1)

                turn_x(0)
                with pe.Fori(0, N_EXP - 1) as e:
                    one(e, True)
                one(N_EXP - 1, False)

            @block.scalar
            def _(act):
                def copy_x(e):
                    for b in range(2):
                        act.wait_ge(x_turned, 2 * e + b + 1)
                        act.activation(xsT[:, b * BANK:(b + 1) * BANK], tp[:, b, :], ACT.Copy).then_inc(xt_done, 1)

                def one(e, more):
                    for half in range(2):
                        act.wait_ge(used[2 * half], e + 2)
                        act.activation(act_a[:, half * BANK:(half + 1) * BANK], gu[:, 2 * half, :],
                                       ACT.Silu).then_inc(silu_done, 1)
                    for b in range(2):
                        act.wait_ge(h_turned, 2 * e + b + 1)
                        act.activation(hidT[:, b * BANK:(b + 1) * BANK], tp[:, b, :], ACT.Copy).then_inc(ht_done, 1)
                    if more:
                        copy_x(e + 1)

                copy_x(0)
                with act.Fori(0, N_EXP - 1) as e:
                    one(e, True)
                one(N_EXP - 1, False)

            @block.vector
            def _(dve):
                dve.sem_inc(hid_done, 1)
                dve.sem_inc(y_done, 1)
                with dve.Fori(0, N_EXP) as e:
                    for half in range(2):
                        dve.wait_ge(silu_done, 2 * e + half + 1)
                        dve.wait_ge(used[2 * half + 1], e + 2)
                        dve.tensor_tensor(hid[:, half * BANK:(half + 1) * BANK], act_a[:, half * BANK:(half + 1) * BANK],
                                          gu[:, 2 * half + 1, :], ALU.mult).then_inc(hid_done, 1)
                    dve.wait_ge(used[5], e + 2)
                    dve.wait_ge(y_free, e + 1)
                    dve.tensor_scalar(y[:], dn[:].rearrange("p b n -> p (b n)"), g.gval[:, ds(e, 1)], None,
                                      ALU.mult).then_inc(y_done, 1)


def moe_out(nc, g):
    io = g.io
    with Phase(nc, "fin") as ph:
        g2, fn = ph.sb("g2", [P, D]), ph.sb("fn", [P, D])
        x = ph.sb("x", [P, 2, D])
        y = ph.sb("y", [P, 2, D])
        junk = ph.sb("junk", [P, D])
        st = ph.sb("st", [P, 2, 4])
        loaded = ph.sem("loaded")
        x_in = [ph.sem(f"x_in{j}") for j in range(2)]
        free = [ph.sem(f"free{j}") for j in range(2)]
        stored = [ph.sem(f"stored{j}") for j in range(2)]
        names = ("x2_done", "squared", "var_done", "root_done", "out_done", "dve_step")
        x2_done, squared, var_done, root_done, out_done, dve_step = (ph.sem(n) for n in names)
        with nc.Block() as block:
            @block.sync
            def _(sp):
                sp.dma_start(g2[:], spread(g.modrow[0, 5 * D:6 * D])).then_inc(loaded, 16)
                sp.dma_start(fn[:], spread(io["final_norm"])).then_inc(loaded, 16)
                with sp.Fori(0, LT // 2) as i:
                    for j in range(2):
                        sp.wait_ge(free[j], i + 1)
                        sp.dma_start(x[:, j, :], g.x1[ds((2 * i + j) * P, P), :]).then_inc(x_in[j], 16)
                        sp.dma_start(y[:, j, :], g.moe[ds((2 * i + j) * P, P), :]).then_inc(x_in[j], 16)

            @block.gpsimd
            def _(pool):
                for j in range(2):
                    pool.sem_inc(free[j], 1)
                with pool.Fori(0, LT // 2) as i:
                    for j in range(2):
                        pool.wait_ge(out_done, 2 * i + j + 1)
                        pool.dma_start(g.xa[ds((2 * i + j) * P, P), :], y[:, j, :]).then_inc(stored[j], 16)
                        pool.wait_ge(stored[j], 16 * (i + 1))
                        pool.sem_inc(free[j], 1)

            @block.scalar
            def _(act):
                with act.Fori(0, LT // 2) as i:
                    for j in range(2):
                        n = 2 * i + j
                        act.wait_ge(x2_done, n + 1)
                        act.activation(junk[:], x[:, j, :], ACT.Square, accum_out=st[:, j, 0:1]).then_inc(squared, 1)
                        act.wait_ge(var_done, n + 1)
                        act.activation(st[:, j, 2:3], st[:, j, 1:2], ACT.Sqrt).then_inc(root_done, 1)

            @block.vector
            def _(dve):
                step = Steps(dve, dve_step)
                dve.wait_ge(loaded, 32)
                with dve.Fori(0, LT // 2) as i:
                    step.n, step.base = 0, i * 4
                    for j in range(2):
                        n = 2 * i + j
                        dve.wait_ge(x_in[j], 32 * (i + 1))
                        step(dve.tensor_tensor(y[:, j, :], y[:, j, :], g2[:], ALU.mult))
                        dve.tensor_tensor(x[:, j, :], x[:, j, :], y[:, j, :], ALU.add).then_inc(x2_done, 1)
                        dve.wait_ge(squared, n + 1)
                        dve.tensor_scalar(st[:, j, 1:2], st[:, j, 0:1], 1.0 / D, EPS, ALU.mult, ALU.add).then_inc(var_done, 1)
                        dve.wait_ge(root_done, n + 1)
                        step(dve.reciprocal(st[:, j, 3:4], st[:, j, 2:3]))
                        dve.scalar_tensor_tensor(y[:, j, :], x[:, j, :], st[:, j, 3:4], fn[:], ALU.mult,
                                                 ALU.mult).then_inc(out_done, 1)


def parts_of(nc, g, l, last):
    io = g.io
    with Phase(nc, f"pr{l}") as ph:
        w = ph.sb("w", [P, 2, KD, P])
        ps = ph.ps("ps", [P, 2, 3, BANK])
        w_in = [ph.sem(f"w_in{j}") for j in range(2)]
        tile_done, read_out = ph.sem("tile_done"), ph.sem("read_out")
        segs = [(0, 1, LAT_CHUNKS), (2 * P, 1, ALL_CHUNKS), (4 * P, 9, LAT_CHUNKS)] if last else [(0, 11, ALL_CHUNKS)]
        with nc.Block() as block:
            @block.sync
            def _(sp):
                stream_weights(sp, io["w_in_2"][l].rearrange("(k p) n -> p k n", p=P), w, w_in, tile_done, segs)

            @block.tensor
            def _(pe):
                project_tiles(nc, pe, w, w_in, tile_done, read_out, ps, g.hT, segs)

            @block.scalar
            def _(act):
                credit(act, read_out, 2)
                base = 0
                for _, pairs, chunks in segs:
                    with act.Fori(0, pairs) as i:
                        for j in range(2):
                            t = base + 2 * i + j
                            act.wait_ge(tile_done, t + 3)
                            if len(chunks) == 3:
                                act.activation(g.parts[:, ds(t, 1), 0:N_CTX].rearrange("p o n -> p (o n)"),
                                               ps[:, j, 2, 0:N_CTX], ACT.Copy)
                            act.activation(g.parts[:, ds(t, 1), N_CTX:].rearrange("p o n -> p (o n)"),
                                           ps[:, j, 0:2, :].rearrange("p c n -> p (c n)"), ACT.Copy).then_inc(read_out, 1)
                    base += 2 * pairs


def queries_keys(nc, g, l, last):
    io = g.io
    with Phase(nc, f"qk{l}") as ph:
        sq = ph.sb("sq", [P, 3, N_ALL])
        rs = ph.sb("rs", [P, 3, N_ALL])
        cos, sin = ph.sb("cos", [P, N_LAT]), ph.sb("sin", [P, N_LAT])
        ps = ph.ps("ps", [P, 2, BANK])
        cs_in, squared, root_done, normed, summed = (ph.sem(n) for n in ("cs_in", "squared", "root_done", "normed", "summed"))
        full = [ph.sem(f"full{b}") for b in range(2)]
        free = [ph.sem(f"free{b}") for b in range(2)]
        dve_step = ph.sem("dve_step")
        jobs = [(t, c) for t in (T_Q, T_Q + 1, T_K) for c in (ALL_CHUNKS if t == T_K or not last else LAT_CHUNKS)]
        turns = [(t, c) for t in (T_Q, T_Q + 1, T_K) for c in LAT_CHUNKS]
        lo = [N_CTX if last else 0, N_CTX if last else 0, 0]
        with nc.Block() as block:
            @block.sync
            def _(sp):
                sp.dma_start(cos[:], io["t_cos"]).then_inc(cs_in, 16)
                sp.dma_start(sin[:], io["t_sin"]).then_inc(cs_in, 16)

            @block.scalar
            def _(act):
                for t in range(3):
                    act.activation(sq[:, t, lo[t]:], g.parts[:, t, lo[t]:], ACT.Square).then_inc(squared, 1)
                for b in range(2):
                    act.wait_ge(free[b], (len(jobs) + 1 - b) // 2)
                for t in range(3):
                    act.activation(rs[:, t, lo[t]:], rs[:, t, lo[t]:], ACT.Sqrt).then_inc(root_done, 1)

            @block.tensor
            def _(pe):
                for n, (t, (c0, cn)) in enumerate(jobs):
                    pe.wait_ge(squared, t + 1)
                    if n >= 2:
                        pe.wait_ge(free[n % 2], n // 2)
                    accumulate(nc, ps[:, n % 2, 0:cn], [(g.block64[:], sq[:, t, c0:c0 + cn])]).then_inc(full[n % 2], 1)
                for n, (t, (c0, cn)) in enumerate(turns, len(jobs)):
                    pe.wait_ge(normed, t + 1)
                    pe.wait_ge(free[n % 2], n // 2)
                    accumulate(nc, ps[:, n % 2, 0:cn], [(g.rot[:], g.parts[:, t, c0:c0 + cn])]).then_inc(full[n % 2], 1)

            @block.vector
            def _(dve):
                step = Steps(dve, dve_step)
                for n, (t, (c0, cn)) in enumerate(jobs):
                    dve.wait_ge(full[n % 2], n // 2 + 1)
                    dve.tensor_scalar(rs[:, t, c0:c0 + cn], ps[:, n % 2, 0:cn], 1.0 / HD, EPS, ALU.mult,
                                      ALU.add).then_inc(free[n % 2], 1)
                for t in range(3):
                    gain = g.pb[:, (PB_QG if t < 2 else PB_KG) + l:(PB_QG if t < 2 else PB_KG) + l + 1]
                    dve.wait_ge(root_done, t + 1)
                    step(dve.reciprocal(rs[:, t, lo[t]:], rs[:, t, lo[t]:]))
                    dve.scalar_tensor_tensor(g.parts[:, t, lo[t]:], g.parts[:, t, lo[t]:], gain, rs[:, t, lo[t]:],
                                             ALU.mult, ALU.mult).then_inc(normed, 1)
                dve.wait_ge(cs_in, 32)
                for n, (t, (c0, cn)) in enumerate(turns, len(jobs)):
                    a = c0 - N_CTX
                    dve.wait_ge(full[n % 2], n // 2 + 1)
                    dve.tensor_tensor(sq[:, t, c0:c0 + cn], ps[:, n % 2, 0:cn], sin[:, a:a + cn],
                                      ALU.mult).then_inc(free[n % 2], 1)
                    step(dve.tensor_tensor(rs[:, t, c0:c0 + cn], g.parts[:, t, c0:c0 + cn], cos[:, a:a + cn], ALU.mult))
                    dve.wait_ge(free[n % 2], n // 2 + 1)
                    step(dve.tensor_tensor(g.parts[:, t, c0:c0 + cn], rs[:, t, c0:c0 + cn], sq[:, t, c0:c0 + cn], ALU.add))


def attention_2(nc, g, l, last):
    with Phase(nc, f"at{l}") as ph:
        k2 = ph.sb("k2", [P, KVH, N_ALL])
        v = ph.sb("v", [P, NT, P])
        p = ph.sb("p", [P, 2, N_ALL])
        pT = ph.sb("pT", [P, 2, NT, P])
        st = ph.sb("st", [P, 2, 4])
        sc = ph.ps("sc", [P, 2, 3, BANK])
        tb = ph.ps("tb", [P, 2, BANK])
        k_in, z_done = ph.sem("k_in"), ph.sem("z_done")
        full = [ph.sem(f"full{b}") for b in range(2)]
        free = [ph.sem(f"free{b}") for b in range(2)]
        names = ("scored", "maxed", "bias_ready", "exped", "inv_ready", "p_ready", "out_done", "y_done")
        scored, maxed, bias_ready, exped, inv_ready, p_ready, out_done, y_done = (ph.sem(n) for n in names)
        items = [(h, N_CTX + t * P, N_ALL) for h in range(H2) for t in range(LT)]
        if not last:
            items += [(h, t * P, N_CTX) for h in range(H2) for t in range(CT)]
        groups = lambda keys: [(a, min(4, keys // P - a)) for a in range(0, keys // P, 4)]
        V_USES = 3
        first_use = [V_USES + sum(len(groups(k)) for _, _, k in items[:n]) for n in range(len(items))]
        lo = N_CTX if last else 0

        def half(h):
            return slice((h % 2) * HD, (h % 2) * HD + HD)

        with nc.Block() as block:
            @block.sync
            def _(sp):
                for kv in range(KVH):
                    for side in range(2):
                        sp.dma_start(k2[side * HD:(side + 1) * HD, kv, :],
                                     g.parts[kv * HD:(kv + 1) * HD, T_K, :]).then_inc(k_in, 16)

            @block.tensor
            def _(pe):
                def turn(n, srcs):
                    b = n % 2
                    if n >= 2:
                        pe.wait_ge(free[b], n // 2)
                    for k, src in enumerate(srcs):
                        mm = pe.transpose(tb[:, b, k * P:(k + 1) * P], src, g.ident[:])
                    mm.then_inc(full[b], 1)

                def scores(n):
                    h, q0, keys = items[n]
                    s = n % 2
                    if n >= 2:
                        pe.wait_ge(y_done, n - 1)
                    for c0 in range(0, keys, BANK):
                        cn = min(BANK, keys - c0)
                        mm = accumulate(nc, sc[:, s, c0 // BANK, 0:cn], [
                            (g.parts[half(h), T_Q + h // 2, q0:q0 + P], k2[half(h), h // 2, c0:c0 + cn])])
                    mm.then_inc(scored, 1)

                for c, (t0, tn) in enumerate(groups(N_ALL)):
                    turn(c, [g.parts[:, T_V, (t0 + k) * P:(t0 + k + 1) * P] for k in range(tn)])
                pe.wait_ge(k_in, 64)
                scores(0)
                for n, (h, q0, keys) in enumerate(items):
                    if n + 1 < len(items):
                        scores(n + 1)
                    pe.wait_ge(p_ready, n + 1)
                    gs = groups(keys)
                    for c, (t0, tn) in enumerate(gs):
                        turn(first_use[n] + c, [p[:, n % 2, (t0 + k) * P:(t0 + k + 1) * P] for k in range(tn)])
                    for c in range(len(gs)):
                        m = first_use[n] + c
                        pe.wait_ge(free[m % 2], m // 2 + 1)
                    accumulate(nc, sc[half(h), n % 2, 2, 256:256 + P], [
                        (v[:, k, (h // 2) * HD:(h // 2 + 1) * HD], pT[:, n % 2, k, :])
                        for k in range(keys // P)]).then_inc(out_done, 1)

            @block.scalar
            def _(act):
                def out_of_bank(n, dst, w):
                    act.wait_ge(full[n % 2], n // 2 + 1)
                    act.activation(dst, tb[:, n % 2, 0:w], ACT.Copy).then_inc(free[n % 2], 1)

                def exp(n):
                    keys = items[n][2]
                    act.wait_ge(bias_ready, n + 1)
                    act.activation(p[:, n % 2, 0:keys], sc[:, n % 2].rearrange("p b n -> p (b n)")[:, 0:keys], ACT.Exp,
                                   bias=st[:, n % 2, 1:2], scale=ATT2_SCALE,
                                   accum_out=st[:, n % 2, 2:3]).then_inc(exped, 1)

                for t in (T_ZA, T_ZA + 1):
                    act.activation(g.parts[:, t, lo:], g.parts[:, t, lo:], ACT.Silu).then_inc(z_done, 1)
                for c, (t0, tn) in enumerate(groups(N_ALL)):
                    out_of_bank(c, v[:, t0:t0 + tn, :].rearrange("p t d -> p (t d)"), tn * P)
                exp(0)
                for n in range(len(items)):
                    for c, (t0, tn) in enumerate(groups(items[n][2])):
                        out_of_bank(first_use[n] + c, pT[:, n % 2, t0:t0 + tn, :].rearrange("p t d -> p (t d)"), tn * P)
                    if n + 1 < len(items):
                        exp(n + 1)

            @block.vector
            def _(dve):
                def maximum(n):
                    keys = items[n][2]
                    dve.wait_ge(scored, n + 1)
                    dve.tensor_reduce(st[:, n % 2, 0:1], sc[:, n % 2].rearrange("p b n -> p (b n)")[:, 0:keys],
                                      AX.X, ALU.max).then_inc(maxed, 1)
                    dve.wait_ge(maxed, n + 1)
                    dve.tensor_scalar(st[:, n % 2, 1:2], st[:, n % 2, 0:1], -ATT2_SCALE, None,
                                      ALU.mult).then_inc(bias_ready, 1)

                dve.wait_ge(z_done, 2)
                maximum(0)
                for n, (h, q0, keys) in enumerate(items):
                    dve.wait_ge(exped, n + 1)
                    dve.reciprocal(st[:, n % 2, 3:4], st[:, n % 2, 2:3]).then_inc(inv_ready, 1)
                    dve.wait_ge(inv_ready, n + 1)
                    dve.tensor_scalar(p[:, n % 2, 0:keys], p[:, n % 2, 0:keys], st[:, n % 2, 3:4], None,
                                      ALU.mult).then_inc(p_ready, 1)
                    if n + 1 < len(items):
                        maximum(n + 1)
                    dve.wait_ge(out_done, n + 1)
                    dve.tensor_tensor(g.hT[half(h), 2 + h // 2, q0:q0 + P], sc[half(h), n % 2, 2, 256:256 + P],
                                      g.parts[half(h), T_ZA + h // 2, q0:q0 + P], ALU.mult).then_inc(y_done, 1)


def fourier(nc, g, l, name):
    io = g.io
    c0, n_tok = (0, N_CTX) if name == "ctx" else (N_CTX, N_LAT)
    nt, width = n_tok // P, min(n_tok, BANK)
    halves = n_tok // width
    with Phase(nc, f"f{name}{l}") as ph:
        u = ph.sb("u", [P, nt, 2 * P])
        dft = ph.sb("dft", [P, 2, 2, n_tok])
        small = ph.sb("small", [P, 2, P])
        wf = ph.sb("wf", [P, 2, 2 * P])
        w2 = ph.sb("w2", [P, 2, 2, 2 * P])
        ab = ph.sb("ab", [P, 2, 2, n_tok])
        bank = ph.ps("bank", [P, 2, 2, 2, BANK])
        flat = bank[:].rearrange("p f s h n -> p (f s h) n")
        loaded, u_full, u_free, w_full, w_free = (ph.sem(n) for n in ("loaded", "u_full", "u_free", "w_full", "w_free"))
        d_in = [ph.sem(f"d_in{j}") for j in range(2)]
        d_used, copied, out_full, out_read, z_done = (ph.sem(n) for n in ("d_used", "copied", "out_full", "out_read",
                                                                          "z_done"))
        with nc.Block() as block:
            @block.sync
            def _(sp):
                sp.dma_start(small[:], io["t_dftd_" + name].rearrange("s p n -> p s n")).then_inc(loaded, 16)
                sp.dma_start(wf[:], io["w_fourier_2"][l].rearrange("(k p) n -> p k n", p=P)).then_inc(loaded, 16)
                for t in range(nt):
                    if t >= 2:
                        sp.wait_ge(d_used, t - 1)
                    sp.dma_start(dft[:, t % 2], io["t_dft_" + name][:, t * P:(t + 1) * P, :].rearrange("s p n -> p s n")
                                 ).then_inc(d_in[t % 2], 16)

            @block.tensor
            def _(pe):
                for t in range(0, nt, 2):
                    b = (t // 2) % 2
                    if t >= 4:
                        pe.wait_ge(u_free, t // 2 - 1)
                    for k in range(4):
                        a, f = divmod(k, 2)
                        mm = pe.transpose(flat[:, b, k * P:(k + 1) * P],
                                          g.parts[:, T_UF + f, c0 + (t + a) * P:c0 + (t + a + 1) * P], g.ident[:])
                    mm.then_inc(u_full, 1)
                pe.wait_ge(loaded, 32)
                for s in range(2):
                    for k in range(2):
                        mm = accumulate(nc, flat[:, 2 + s, k * 2 * P:(k + 1) * 2 * P], [(small[:, s, :], wf[:, k, :])])
                mm.then_inc(w_full, 1)
                pe.wait_ge(u_free, nt // 2)
                pe.wait_ge(w_free, 1)
                for t in range(nt):
                    pe.wait_ge(d_in[t % 2], 16 * (t // 2 + 1))
                    for f in range(2):
                        for s in range(2):
                            for h in range(halves):
                                mm = nc.tensor.matmul(bank[:, f, s, h, 0:width], u[:, t, f * P:(f + 1) * P],
                                                      dft[:, t % 2, s, h * width:(h + 1) * width],
                                                      start=t == 0, stop=t == nt - 1)
                    mm.then_inc(d_used, 1)
                pe.wait_ge(copied, 4)
                for j in range(2):
                    for h in range(halves):
                        accumulate(nc, bank[:, j, 0, h, 0:width], [
                            (w2[:, s, f, j * P:(j + 1) * P], ab[:, f, s, h * width:(h + 1) * width])
                            for s in range(2) for f in range(2)]).then_inc(out_full, 1)

            @block.scalar
            def _(act):
                for t in (T_ZF, T_ZF + 1):
                    act.activation(g.parts[:, t, c0:c0 + n_tok], g.parts[:, t, c0:c0 + n_tok], ACT.Silu).then_inc(z_done, 1)

            @block.vector
            def _(dve):
                for t in range(0, nt, 2):
                    dve.wait_ge(u_full, t // 2 + 1)
                    dve.tensor_copy(u[:, t:t + 2, :].rearrange("p t n -> p (t n)"),
                                    flat[:, (t // 2) % 2, :]).then_inc(u_free, 1)
                dve.wait_ge(w_full, 1)
                dve.tensor_copy(w2[:].rearrange("p s k n -> p s (k n)"), flat[:, 2:4, :]).then_inc(w_free, 1)
                dve.wait_ge(d_used, nt)
                for f in range(2):
                    for s in range(2):
                        dve.tensor_copy(ab[:, f, s, :].rearrange("p (h n) -> p h n", h=halves),
                                        bank[:, f, s, 0:halves, 0:width]).then_inc(copied, 1)
                dve.wait_ge(z_done, 2)
                for j in range(2):
                    for h in range(halves):
                        a = c0 + h * width
                        dve.wait_ge(out_full, j * halves + h + 1)
                        dve.tensor_tensor(g.hT[:, j, a:a + width], bank[:, j, 0, h, 0:width],
                                          g.parts[:, T_ZF + j, a:a + width], ALU.mult).then_inc(out_read, 1)


def conv_pool(nc, g, l, streams):
    io = g.io
    CP, PP = 1, 8
    with Phase(nc, f"cp{l}") as ph:
        tc = ph.sb("tc", [P, N_ALL + 3 * CP])
        yc = ph.sb("yc", [P, N_ALL])
        up = ph.sb("up", [P, N_ALL + 3 * PP])
        s = [ph.sb(f"s{i}", [P, N_ALL + 3 * PP]) for i in range(2)]
        dd = ph.sb("dd", [P, 2, N_ALL])
        rc = ph.sb("rc", [P, 2, N_ALL])
        pw = ph.sb("pw", [P, 2, P])
        ps = ph.ps("ps", [P, 2, BANK])
        zeroed, loaded, z_done, d_done, y_done, up_ready = (ph.sem(n) for n in (
            "zeroed", "loaded", "z_done", "d_done", "y_done", "up_ready"))
        full, dve_step, pool_step, up_used = ph.sem("full"), ph.sem("dve_step"), ph.sem("pool_step"), ph.sem("up_used")
        at_c = {0: CP, N_CTX: 2 * CP + N_CTX}
        at_p = {0: PP, N_CTX: 2 * PP + N_CTX}
        lo = streams[0][1]
        width = N_ALL + 3 * PP
        chunks = [c for c in ALL_CHUNKS if c[0] >= lo]
        jobs = [(j, c) for j in range(2) for c in chunks]
        with nc.Block() as block:
            @block.sync
            def _(sp):
                for name, c0, n in streams:
                    sp.dma_start(rc[:, :, c0:c0 + n], io["t_rcnt_" + name].rearrange("j p n -> p j n")).then_inc(loaded, 16)
                sp.wait_ge(zeroed, 3)
                for j in range(2):
                    for h in range(2):
                        sp.dma_start(pw[h * HD:(h + 1) * HD, j, h * HD:(h + 1) * HD],
                                     io["pool_w_2"][l, 2 * j + h]).then_inc(loaded, 16)

            @block.gpsimd
            def _(pool):
                pool.memset(tc[:], 0.0).then_inc(zeroed, 1)
                pool.memset(up[:], 0.0).then_inc(zeroed, 1)
                pool.memset(pw[:], 0.0).then_inc(zeroed, 1)

            @block.scalar
            def _(act):
                for t in (T_ZC, T_ZC + 1, T_ZP, T_ZP + 1):
                    act.activation(g.parts[:, t, lo:], g.parts[:, t, lo:], ACT.Silu).then_inc(z_done, 1)
                act.wait_ge(zeroed, 3)
                for j in range(2):
                    act.wait_ge(up_used, j)
                    for _, c0, n in streams:
                        ins = act.activation(up[:, at_p[c0]:at_p[c0] + n], g.parts[:, T_UP + j, c0:c0 + n], ACT.Copy)
                    ins.then_inc(up_ready, 1)

            @block.vector
            def _(dve):
                step = Steps(dve, dve_step)
                dve.wait_ge(loaded, 16 * (len(streams) + 4))
                for j in range(2):
                    dve.wait_ge(up_ready, j + 1)
                    src, w = up, 1
                    for q in range(2 * j + 2):
                        dst = s[q % 2]
                        ins = dve.tensor_tensor(dst[:, 0:width - 2 * w + 1], src[:, 0:width - 2 * w + 1],
                                                src[:, w:width - w + 1], ALU.add)
                        if q == 0:
                            ins.then_inc(up_used, 1)
                            dve.wait_ge(up_used, j + 1)
                        else:
                            step(ins)
                        src, w = dst, 2 * w
                        h = q - 2 * j
                        if h >= 0:
                            r = slice(h * HD, (h + 1) * HD)
                            for _, c0, n in streams:
                                a = at_p[c0] - w // 2
                                step(dve.tensor_tensor(dd[r, j, c0:c0 + n], src[r, a:a + n], rc[r, j, c0:c0 + n], ALU.mult))
                    dve.tensor_tensor(dd[:, j, lo:], dd[:, j, lo:], g.parts[:, T_UP + j, lo:],
                                      ALU.subtract).then_inc(d_done, 1)
                dve.wait_ge(z_done, 4)
                for j in range(2):
                    taps = [g.pb[:, PB_CW + l * 6 + tap * 2 + j:PB_CW + l * 6 + tap * 2 + j + 1] for tap in range(3)]
                    bias = g.pb[:, PB_CB + l * 2 + j:PB_CB + l * 2 + j + 1]
                    for _, c0, n in streams:
                        a = at_c[c0]
                        step(dve.tensor_tensor(tc[:, a:a + n], g.parts[:, T_C + j, c0:c0 + n], g.parts[:, T_H + j, c0:c0 + n],
                                               ALU.mult))
                    for _, c0, n in streams:
                        a = at_c[c0] - 1
                        step(dve.tensor_scalar(yc[:, c0:c0 + n], tc[:, a:a + n], taps[0], bias, ALU.mult, ALU.add))
                        for tap in (1, 2):
                            step(dve.scalar_tensor_tensor(yc[:, c0:c0 + n], tc[:, a + tap:a + tap + n], taps[tap],
                                                          yc[:, c0:c0 + n], ALU.mult, ALU.add))
                    step(dve.tensor_tensor(yc[:, lo:], yc[:, lo:], g.parts[:, T_B + j, lo:], ALU.mult))
                    step(dve.tensor_tensor(g.hT[:, 4 + j, lo:], yc[:, lo:], g.parts[:, T_ZC + j, lo:], ALU.mult))
                for n, (j, (c0, cn)) in enumerate(jobs):
                    dve.wait_ge(full, n + 1)
                    dve.scalar_tensor_tensor(g.hT[:, 6 + j, c0:c0 + cn], ps[:, n % 2, 0:cn],
                                             g.pb[:, PB_PS + l * 2 + j:PB_PS + l * 2 + j + 1],
                                             g.parts[:, T_ZP + j, c0:c0 + cn], ALU.mult, ALU.mult).then_inc(y_done, 1)

            @block.tensor
            def _(pe):
                pe.wait_ge(loaded, 16 * (len(streams) + 4))
                for n, (j, (c0, cn)) in enumerate(jobs):
                    pe.wait_ge(d_done, j + 1)
                    if n >= 2:
                        pe.wait_ge(y_done, n - 1)
                    accumulate(nc, ps[:, n % 2, 0:cn], [(pw[:, j, :], dd[:, j, c0:c0 + cn])]).then_inc(full, 1)


def project_out(nc, g, l, jobs):
    io = g.io
    with Phase(nc, f"po{l}") as ph:
        w = ph.sb("w", [P, KD, D])
        gate = ph.sb("gate", [P, 2, D])
        x = ph.sb("x", [P, 2, D])
        y = ph.sb("y", [P, 2, D])
        acc = ph.ps("acc", [P, 2, 2, BANK])
        loaded = ph.sem("loaded")
        x_in = [ph.sem(f"x_in{j}") for j in range(2)]
        stored = [ph.sem(f"stored{j}") for j in range(2)]
        multiplied, y_done, out_done = ph.sem("multiplied"), ph.sem("y_done"), ph.sem("out_done")
        tiles = [(src[t * P:(t + 1) * P, :], dst[t * P:(t + 1) * P, :], s, col + t * P)
                 for src, dst, s, col, n in jobs for t in range(n)]
        with nc.Block() as block:
            @block.sync
            def _(sp):
                sp.dma_start(w[:], io["w_out_2"][l].rearrange("(k p) n -> p k n", p=P)).then_inc(loaded, 16)
                for s in range(2):
                    a = (48 + l * 24 + 16) * P
                    sp.dma_start(gate[:, s, :], spread(g.modrow[s, a:a + D])).then_inc(loaded, 16)
                for n, (src, _, _, _) in enumerate(tiles):
                    if n >= 2:
                        sp.wait_ge(out_done, n - 1)
                    sp.dma_start(x[:, n % 2, :], src).then_inc(x_in[n % 2], 16)

            @block.gpsimd
            def _(pool):
                for n, (_, dst, _, _) in enumerate(tiles):
                    pool.wait_ge(out_done, n + 1)
                    pool.dma_start(dst, y[:, n % 2, :]).then_inc(stored[n % 2], 16)
                for j in range(2):
                    pool.wait_ge(stored[j], 8 * len(tiles))

            @block.tensor
            def _(pe):
                pe.wait_ge(loaded, 48)
                for n, (_, _, _, col) in enumerate(tiles):
                    if n >= 2:
                        pe.wait_ge(y_done, n - 1)
                    for c in range(2):
                        mm = accumulate(nc, acc[:, n % 2, c, :], [
                            (g.hT[:, k, col:col + P], w[:, k, c * BANK:(c + 1) * BANK]) for k in range(KD)])
                    mm.then_inc(multiplied, 1)

            @block.vector
            def _(dve):
                for n, (_, _, s, _) in enumerate(tiles):
                    j = n % 2
                    dve.wait_ge(multiplied, n + 1)
                    if n >= 2:
                        dve.wait_ge(stored[j], 16 * (n // 2))
                    dve.tensor_tensor(y[:, j, :], acc[:, j].rearrange("p c n -> p (c n)"), gate[:, s, :],
                                      ALU.mult).then_inc(y_done, 1)
                    dve.wait_ge(x_in[j], 16 * (n // 2 + 1))
                    dve.wait_ge(y_done, n + 1)
                    dve.tensor_tensor(y[:, j, :], y[:, j, :], x[:, j, :], ALU.add).then_inc(out_done, 1)


def layer(nc, g, l, sb):
    last = l == 1
    x, xc = (g.xb, g.xcb) if last else (g.xa, g.io["ctx_2"])
    streams = [("lat", N_CTX, N_LAT)] if last else [("ctx", 0, N_CTX), ("lat", N_CTX, N_LAT)]
    with ExitStack() as outer:
        g.hT = sb("hT", [P, KD, N_ALL], outer, tag=f"l{l}")
        with ExitStack() as inner_:
            g.parts = sb("parts", [P, D_IN2 // P, N_ALL], inner_, tag=f"l{l}")
            normed_transposed(nc, g, f"n2{l}", [(xc, CT // 2, 1, 0), (x, LT // 2, 0, N_CTX)],
                              g.pb[:, PB_NORM + l * KD:PB_NORM + (l + 1) * KD], g.mod2, l * 24, l * 24 + KD, g.hT)
            parts_of(nc, g, l, last)
            queries_keys(nc, g, l, last)
            attention_2(nc, g, l, last)
            for name, _, _ in streams:
                fourier(nc, g, l, name)
            conv_pool(nc, g, l, streams)
        if last:
            project_out(nc, g, l, [(x, g.out.rearrange("b n d -> (b n) d"), 0, N_CTX, LT)])
        else:
            project_out(nc, g, l, [(xc, g.xcb, 1, 0, CT), (x, g.xb, 0, N_CTX, LT)])


class Shared:
    pass


def program(nc, io, out):
    g = Shared()
    g.io, g.out = io, out
    with ExitStack() as whole:
        def sb(name, shape, stack=whole, dt=F32, tag="g"):
            return stack.enter_context(nc.sbuf_tensor(f"{tag}_{name}", shape, dt))

        def dram(name, shape, dt=F32):
            return nc.dram_tensor("g_" + name, shape, dt).ap()

        g.ident, g.rev, g.ones, g.block64, g.rot = (sb(n, [P, P]) for n in ("ident", "rev", "ones", "block64", "rot"))
        g.causal = sb("causal", [P, 2, P])
        g.pa = sb("pa", [P, P])
        g.pb = sb("pb", [P, P])
        g.mod1 = sb("mod1", [P, 2, 48])
        g.mod2 = sb("mod2", [P, 2, 48])
        g.modrow = dram("modrow", [2, 96 * P])
        g.y_dram = dram("y_dram", [HEADS, P, N_LAT])
        g.xm_dram = dram("xm_dram", [KD, P, W_PAD])
        g.xc_dram = dram("xc_dram", [KD, P, N_ALL])
        g.bd_dram = dram("bd_dram", [KD, P, 3, P])
        g.col_dram = dram("col_dram", [ML_HEADS, P, NT, 6, 2])
        g.m_dram = dram("m_dram", [KD, P, N_LAT])
        g.x1 = dram("x1", [N_LAT, D])
        g.h2 = dram("h2", [N_LAT, D])
        g.moe = dram("moe", [N_LAT, D])
        g.xa = dram("xa", [N_LAT, D])
        g.xb = dram("xb", [N_LAT, D])
        g.xcb = dram("xcb", [N_CTX, D])
        modulation(nc, g)
        with ExitStack() as first:
            g.hT = sb("hT", [P, KD, N_ALL], first)
            normed_transposed(nc, g, "n1", [(io["ctx"], CT // 2, 1, 0), (io["x"], LT // 2, 0, N_CTX)],
                              g.pa[:, PA_NORM1:PA_NORM1 + KD], g.mod1, 0, KD, g.hT)
            with ExitStack() as att:
                g.ql = sb("ql", [P, QL, N_LAT], att)
                g.kl = sb("kl", [P, KL, N_ALL], att)
                g.kpe_hi = sb("kpe_hi", [P, N_ALL], att, FR)
                g.kpe_lo = sb("kpe_lo", [ROPE, N_ALL], att, FR)
                g.cos = sb("cos", [P, N_LAT], att)
                g.sin = sb("sin", [P, N_LAT], att)
                latents(nc, g)
                g.yT = sb("yT", [P, HEADS, N_LAT], att)
                attention(nc, g)
                gate_attention(nc, g)
            with ExitStack() as ml:
                g.gts = sb("gts", [P, NT, 16], ml)
                g.cols = sb("cols", [P, NT, 6, 4, 2], ml)
                with ExitStack() as inn:
                    g.xm = sb("xm", [P, KD, W_PAD], inn)
                    g.xc = sb("xc", [P, KD, N_ALL], inn)
                    inner(nc, g)
                    gates(nc, g)
                gate_rows(nc, g)
            g.hs = sb("hs", [P, LT, D], first)
            mlstm(nc, g)
            readout(nc, g)
        with ExitStack() as moe:
            g.affT = sb("affT", [N_EXP, N_LAT], moe)
            g.gval = sb("gval", [P, N_EXP], moe)
            g.gidx = sb("gidx", [P, N_EXP], moe, U32)
            merge(nc, g)
            route(nc, g)
            experts(nc, g)
        moe_out(nc, g)
        for l in range(2):
            layer(nc, g, l, sb)


_IN = ["x", "c", "ctx", "c_ctx", "w_mod", "b_mod", "norm1", "w_in", "q_norm", "w_uq", "kv_norm", "w_ukv", "conv_w",
       "conv_b", "w_qblk", "w_kblk", "w_vblk", "w_gate", "b_gate", "ml_norm", "ml_skip", "w_out", "norm2", "w_router",
       "w_e_gate", "w_e_up", "w_e_down", "final_norm", "c_2", "ctx_2", "c_ctx_2", "w_mod_2", "b_mod_2", "norm_g_2",
       "w_in_2", "q_gain_2", "k_gain_2", "w_fourier_2", "conv_w_2", "conv_b_2", "pool_w_2", "pool_scale_2", "w_out_2"]
_FLAT = {"c", "b_mod", "norm1", "q_norm", "kv_norm", "conv_w", "conv_b", "b_gate", "ml_norm", "ml_skip", "norm2",
         "c_2", "b_mod_2", "norm_g_2", "conv_w_2", "conv_b_2", "pool_scale_2"}
_DROP = {"x", "ctx", "w_mod", "w_in", "w_uq", "w_ukv", "w_qblk", "w_kblk", "w_vblk", "w_gate", "w_out", "w_router",
         "w_e_gate", "w_e_up", "w_e_down", "ctx_2"}


def kernel(**inputs):
    import concourse.bacc as bacc
    from concourse.bass_utils import run_bass_kernel_spmd

    nc = bacc.Bacc("TRN2", target_bir_lowering=False, num_devices=1)
    arrays, io = {}, {}

    def give(name, a):
        arrays[f"in_{name}"] = a
        io[name] = nc.dram_tensor(f"in_{name}", a.shape, mybir.dt.from_np(a.dtype), kind="ExternalInput").ap()

    for name in _IN:
        a = np.ascontiguousarray(inputs[name])
        give(name, a.reshape(-1) if name in _FLAT else a.reshape(a.shape[1:]) if name in _DROP else a)
    for name, a in tables().items():
        give("t_" + name, a)
    out = nc.dram_tensor("out", (1, N_LAT, D), F32, kind="ExternalOutput").ap()
    program(nc, io, out)
    r = run_bass_kernel_spmd(nc, [arrays], core_ids=[0])
    return r.results[0]["out"]
```

```python
from contextlib import ExitStack

import numpy as np

import concourse.bass as bass
from concourse import mybir

F32 = mybir.dt.float32
FR = mybir.dt.float32r
I32 = mybir.dt.int32
U32 = mybir.dt.uint32
ALU = mybir.AluOpType
ACT = mybir.ActivationFunctionType
AX = mybir.AxisListType
ds = bass.ds

P = 128
BANK = 512
D = 1024
KD = D // P
N_LAT, N_CTX = 1024, 256
N_ALL = N_CTX + N_LAT
LT, CT = N_LAT // P, N_CTX // P
NT = LT + CT
EPS = 1e-6
LAT_CHUNKS = [(256, 512), (768, 512)]
ALL_CHUNKS = LAT_CHUNKS + [(0, 256)]

HEADS, NOPE, ROPE, VD = 8, 128, 64, 128
QL, KL = 384 // P, 256 // P
QK = NOPE + ROPE
ATT_SCALE = QK ** -0.5
COL_KV, COL_KR, COL_XM = 384, 640, 704
COL_Z, COL_GMLA, COL_GML = 1728, 2752, 3776
ML_HEADS, DH = 4, 256
TAPS = 5
N_EXP, FF = 16, 1024
CAP = 2 * N_LAT // N_EXP
FT = FF // P

PA_NORM1, PA_QN, PA_KVN, PA_CB, PA_MLN, PA_SKIP, PA_CW = 0, 8, 11, 13, 21, 29, 37
PB_C, PB_NORM, PB_PS, PB_CB, PB_CW, PB_QG, PB_KG = 0, 32, 48, 52, 56, 68, 70

D_IN2 = 2816
H2, KVH, HD = 4, 2, 64
ATT2_SCALE = HD ** -0.5
T_Q, T_K, T_V, T_ZA, T_UF, T_ZF, T_B, T_C, T_H, T_ZC, T_UP, T_ZP = 0, 2, 3, 4, 6, 8, 10, 12, 14, 16, 18, 20


def tables():
    f = np.float32
    out = {"ident": np.eye(P, dtype=f), "rev": np.ascontiguousarray(np.eye(P, dtype=f)[::-1])}
    s, t = np.arange(P)[:, None], np.arange(P)[None, :]
    out["causal"] = np.stack([np.where(s <= t, 0, 1e30), np.where(s >= t, 0, 1e30)]).astype(f)
    out["block4"] = (s // 4 == t // 4).astype(f)
    out["block64"] = (s // 64 == t // 64).astype(f)
    rot = np.zeros((P, P), f)
    for j in range(P):
        if j % 32 < 16:
            rot[j + 16, j] = -1
        else:
            rot[j - 16, j] = 1
    out["rot"] = rot
    pos = np.arange(N_LAT)
    inv = (10000.0 ** (-np.arange(16, dtype=f) / f(16))).astype(f)
    ang = np.zeros((P, N_LAT), f)
    for j in range(P):
        base = (pos // 64 if (j % 64) < 32 else pos % 64).astype(f)
        ang[j] = base * inv[j % 16]
    out["cos"], out["sin"] = np.cos(ang).astype(f), np.sin(ang).astype(f)
    for n, name in ((N_LAT, "lat"), (N_CTX, "ctx")):
        k = (np.arange(n)[:, None] * np.arange(n)[None, :]) % n
        out["dft_" + name] = np.stack([np.cos(2 * np.pi * k / n), np.sin(2 * np.pi * k / n)]).astype(f)
        d = (np.arange(64)[:, None] * np.arange(64)[None, :]) % 64
        norm = 1.0 / np.sqrt(n * 64.0)
        small = np.zeros((2, P, P))
        for b in (0, 64):
            small[0, b:b + 64, b:b + 64] = np.cos(2 * np.pi * d / 64) * norm
            small[1, b:b + 64, b:b + 64] = -np.sin(2 * np.pi * d / 64) * norm
        out["dftd_" + name] = small.astype(f)
        cnt = np.zeros((2, P, n), f)
        for i, w in enumerate((2, 4, 8, 16)):
            left, right = w // 2, w - 1 - w // 2
            p = np.arange(n)
            c = np.clip(p + right + 1, 0, n) - np.clip(p - left, 0, n)
            cnt[i // 2, (i % 2) * 64:(i % 2) * 64 + 64] = 1.0 / c
        out["rcnt_" + name] = cnt
    reset = np.ones((36, NT, P), f)
    reset[:, :, 0] = 0
    out["reset"] = reset.reshape(36, N_ALL)
    return out


class Phase(ExitStack):

    def __init__(self, nc, tag):
        super().__init__()
        self.nc, self.tag, self.sems = nc, tag, []

    def sb(self, name, shape, dt=F32):
        return self.enter_context(self.nc.sbuf_tensor(f"{self.tag}_{name}", shape, dt))

    def ps(self, name, shape, dt=F32):
        return self.enter_context(self.nc.psum_tensor(f"{self.tag}_{name}", shape, dt))

    def sem(self, name):
        self.sems.append(self.nc.alloc_semaphore(f"{self.tag}_{name}"))
        return self.sems[-1]

    def __exit__(self, *exc):
        if exc[0] is None:
            self.nc.clear_and_free_semaphores(self.sems)
            self.nc.all_engine_barrier(sem_only=True)
        return super().__exit__(*exc)


class Steps:

    def __init__(self, eng, sem):
        self.eng, self.sem, self.n, self.base = eng, sem, 0, 0

    def __call__(self, ins):
        self.n += 1
        ins.then_inc(self.sem, 1)
        self.eng.wait_ge(self.sem, self.base + self.n)


def accumulate(nc, out, pairs):
    last = len(pairs) - 1
    for n, (lhsT, rhs) in enumerate(pairs):
        mm = nc.tensor.matmul(out, lhsT, rhs, start=n == 0, stop=n == last)
    return mm


def rows(ap):
    return ap.rearrange("(r p) -> r p", p=P)


def spread(ap, parts=P):
    return bass.AP(tensor=ap.tensor, offset=ap.offset, ap=[[0, parts]] + [list(x) for x in ap.ap])


def modulation(nc, g):
    io = g.io
    RING = 6
    MOD_N = 2 * 6 * D
    with Phase(nc, "mod") as ph:
        raw = ph.sb("raw", [P, 2, P])
        w = [ph.sb(f"w{j}", [P, KD, BANK]) for j in range(RING)]
        c4 = ph.sb("c4", [P, 4, KD])
        c2 = ph.sb("c2", [P, 2, KD, 2])
        row = ph.sb("row", [2, MOD_N])
        back = ph.sb("back", [96, 2, P])
        tp = ph.ps("tp", [P, 2, BANK])
        acc = ph.ps("acc", [2, 2, BANK])
        par_in, par_t, par_c = ph.sem("par_in"), ph.sem("par_t"), ph.sem("par_c")
        zero = ph.sem("zero")
        act_c, dve_c = ph.sem("act_c"), ph.sem("dve_c")
        w_in = [ph.sem(f"w_in{j}") for j in range(RING)]
        mm_done, mod_done = ph.sem("mm_done"), ph.sem("mod_done")
        bias_in, row_out, back_in, turned = ph.sem("bias_in"), ph.sem("row_out"), ph.sem("back_in"), ph.sem("turned")
        srcs = [(io["w_mod"], 12), (io["w_mod_2"][0], 6), (io["w_mod_2"][1], 6)]
        n_par = [0]
        first = [(io["norm1"], 8), (io["q_norm"], 3), (io["kv_norm"], 2), (io["conv_b"], 8), (io["ml_norm"], 8),
                 (io["ml_skip"], 8), (io["conv_w"], 40)]
        second = [(io["c"], 8), (io["c_ctx"], 8), (io["c_2"], 8), (io["c_ctx_2"], 8),
                  (io["norm_g_2"], 16), (io["pool_scale_2"], 4), (io["conv_b_2"], 4), (io["conv_w_2"], 12)]

        with nc.Block() as block:
            @block.gpsimd
            def _(pool):
                pool.memset(raw[:], 0.0).then_inc(zero, 1)
                pool.memset(g.ones[:], 1.0).then_inc(zero, 1)

            @block.sync
            def _(sp):
                for dst, name in ((g.ident, "ident"), (g.rev, "rev"), (g.block64, "block64"), (g.rot, "rot")):
                    sp.dma_start(dst[:], io["t_" + name]).then_inc(par_in, 16)
                    n_par[0] += 1
                sp.dma_start(g.causal[:], io["t_causal"].rearrange("d s t -> s d t")).then_inc(par_in, 16)
                n_par[0] += 1
                sp.wait_ge(zero, 1)
                for side, group in enumerate((first, second)):
                    at = 0
                    for ap, n in group:
                        sp.dma_start(raw[at:at + n, side, :], rows(ap)).then_inc(par_in, 16)
                        at += n
                        n_par[0] += 1
                for l in range(2):
                    for half in (0, HD):
                        for at, gain in ((PB_QG, io["q_gain_2"]), (PB_KG, io["k_gain_2"])):
                            sp.dma_start(raw[at + l:at + l + 1, 1, half:half + HD],
                                         gain[l:l + 1, :]).then_inc(par_in, 16)
                            n_par[0] += 1
                for s in range(2):
                    sp.dma_start(row[s:s + 1, 0:6 * D], io["b_mod"].rearrange("(o n) -> o n", o=1)).then_inc(bias_in, 16)
                    sp.dma_start(row[s:s + 1, 6 * D:], io["b_mod_2"].rearrange("(o n) -> o n", o=1)
                                 ).then_inc(bias_in, 16)
                base = 0
                for src, n in srcs:
                    wv = src.rearrange("(k p) n -> p k n", p=P)
                    with sp.Fori(0, n // RING) as i:
                        for j in range(RING):
                            sp.wait_ge(mm_done, base + RING * i + j + 1)
                            sp.dma_start(w[j][:], wv[:, :, ds((RING * i + j) * BANK, BANK)]).then_inc(w_in[j], 16)
                    base += n
                sp.wait_ge(mod_done, 2 + base)
                sp.dma_start(g.modrow, row[:]).then_inc(row_out, 16)
                sp.wait_ge(row_out, 16)
                for s in range(2):
                    sp.dma_start(back[:, s, :], rows(g.modrow[s])).then_inc(back_in, 16)

            @block.tensor
            def _(pe):
                pe.sem_inc(mm_done, RING)
                pe.wait_ge(par_in, 16 * n_par[0])
                for side in range(2):
                    pe.transpose(tp[:, side, 0:P], raw[:, side, :], g.ident[:]).then_inc(par_t, 1)
                pe.wait_ge(dve_c, 4)
                base = 0
                for blk, (_, n) in enumerate(srcs):
                    with pe.Fori(0, n // RING) as i:
                        for j in range(RING):
                            pe.wait_ge(w_in[j], 16 * (base // RING + i + 1))
                            pe.wait_ge(mod_done, base + RING * i + j + 1)
                            accumulate(nc, acc[:, j % 2, :], [(c2[:, min(blk, 1), k, :], w[j][:, k, :])
                                                              for k in range(KD)]).then_inc(mm_done, 1)
                    base += n
                pe.wait_ge(back_in, 32)
                for s in range(2):
                    pe.transpose(tp[:, s, 0:96], back[:, s, :], g.ident[0:96, 0:96]).then_inc(turned, 1)

            @block.scalar
            def _(act):
                act.wait_ge(par_c, 2)
                act.activation(c4[:].rearrange("p a k -> p (a k)"), g.pb[:, PB_C:PB_C + 32], ACT.Silu).then_inc(act_c, 1)

            @block.vector
            def _(dve):
                for side, dst in enumerate((g.pa, g.pb)):
                    dve.wait_ge(par_t, side + 1)
                    dve.tensor_copy(dst[:], tp[:, side, 0:P]).then_inc(par_c, 1)
                dve.wait_ge(act_c, 1)
                for blk in range(2):
                    for s in range(2):
                        dve.tensor_copy(c2[:, blk, :, s], c4[:, 2 * blk + s, :]).then_inc(dve_c, 1)
                dve.sem_inc(mod_done, 2)
                dve.wait_ge(bias_in, 64)
                base = 0
                for _, n in srcs:
                    with dve.Fori(0, n // RING) as i:
                        for j in range(RING):
                            dve.wait_ge(mm_done, base + RING * i + j + RING + 1)
                            cols = ds((base + RING * i + j) * BANK, BANK)
                            dve.tensor_tensor(row[:, cols], row[:, cols], acc[:, j % 2, :], ALU.add).then_inc(mod_done, 1)
                    base += n
                for s in range(2):
                    dve.wait_ge(turned, s + 1)
                    dve.tensor_copy(g.mod1[:, s, :], tp[:, s, 0:48])
                    dve.tensor_copy(g.mod2[:, s, :], tp[:, s, 48:96])


def normed_transposed(nc, g, tag, segments, norm, mod, at_shift, at_scale, hT, low=None, scratch=None):
    with Phase(nc, tag) as ph:
        tiles = [(s, col + t * P) for _, pairs, s, col in segments for t in range(2 * pairs)]
        pairs = [(src, t) for src, n, _, _ in segments for t in range(n)]
        x = ph.sb("x", [P, NT, D])[:] if scratch is None else \
            scratch[:, 0:NT * D].rearrange("p (t n) -> p t n", n=D)
        y = None if low is None else scratch[:, NT * D:(NT + 2) * D].rearrange("p (j k n) -> p j k n", j=2, k=KD)
        junk = ph.sb("junk", [P, 2, D])
        total, var, root, inv = (ph.sb(n, [P, NT]) for n in ("total", "var", "root", "inv"))
        gain = ph.sb("gain", [P, 2, KD])
        SLOTS = 4
        tp = ph.ps("tp", [P, SLOTS, 2, BANK])
        x_in = [ph.sem(f"x_in{n}") for n in range(len(pairs))]
        names = ("gain_done", "squared", "var_done", "root_done", "inv_done", "xn_done", "turned", "out_a", "out_b",
                 "high_done", "low_done")
        gain_done, squared, var_done, root_done, inv_done, xn_done, turned, out_a, out_b, high_done, low_done = (
            ph.sem(n) for n in names)

        def target(n, k):
            col = tiles[n][1]
            return hT[:, k, col:col + P] if low is None else y[:, n % 2, k, :]

        with nc.Block() as block:
            @block.sync
            def _(sp):
                for n, (src, t) in enumerate(pairs):
                    sp.dma_start(x[:, 2 * n:2 * n + 2, :], src[2 * t * P:2 * (t + 1) * P, :].rearrange(
                        "(t p) n -> p t n", p=P)).then_inc(x_in[n], 16)

            @block.scalar
            def _(act):
                def squares(m):
                    act.wait_ge(x_in[m], 16)
                    for n in (2 * m, 2 * m + 1):
                        ins = act.activation(junk[:, n % 2], x[:, n, :], ACT.Square, accum_out=total[:, n:n + 1])
                    ins.then_inc(squared, 1)
                    act.wait_ge(var_done, m + 1)
                    act.activation(root[:, 2 * m:2 * m + 2], var[:, 2 * m:2 * m + 2], ACT.Sqrt).then_inc(root_done, 1)

                squares(0)
                act.wait_ge(gain_done, 2)
                for m in range(len(pairs)):
                    if m + 1 < len(pairs):
                        squares(m + 1)
                    for n in (2 * m, 2 * m + 1):
                        s = tiles[n][0]
                        act.wait_ge(turned, n + 1)
                        if low is not None and n >= 2:
                            act.wait_ge(low_done, n - 1)
                        for k in range(4):
                            ins = act.activation(target(n, k), tp[:, n % SLOTS, 0, k * P:(k + 1) * P], ACT.Identity,
                                                 bias=mod[:, s, at_shift + k:at_shift + k + 1],
                                                 scale=gain[:, s, k:k + 1])
                        ins.then_inc(out_a, 1)
                        if low is not None:
                            act.wait_ge(out_a, n + 1)
                            act.wait_ge(out_b, n + 1)
                            col = tiles[n][1]
                            act.activation(hT[:, :, col:col + P], y[:, n % 2], ACT.Copy).then_inc(high_done, 1)

            @block.gpsimd
            def _(pool):
                if low is not None:
                    for n, (_, col) in enumerate(tiles):
                        pool.wait_ge(high_done, n + 1)
                        pool.tensor_tensor(low[:, :, col:col + P], y[:, n % 2], hT[:, :, col:col + P].bitcast(F32),
                                           ALU.subtract).then_inc(low_done, 1)

            @block.vector
            def _(dve):
                def scale_rows(m):
                    dve.wait_ge(squared, m + 1)
                    pair = slice(2 * m, 2 * m + 2)
                    dve.tensor_scalar(var[:, pair], total[:, pair], 1.0 / D, EPS, ALU.mult, ALU.add).then_inc(var_done, 1)
                    dve.wait_ge(root_done, m + 1)
                    dve.reciprocal(inv[:, pair], root[:, pair]).then_inc(inv_done, 1)
                    dve.wait_ge(inv_done, m + 1)
                    for n in (2 * m, 2 * m + 1):
                        dve.tensor_scalar(x[:, n, :], x[:, n, :], inv[:, n:n + 1], None, ALU.mult).then_inc(xn_done, 1)

                for s in range(2):
                    dve.scalar_tensor_tensor(gain[:, s, :], mod[:, s, at_scale:at_scale + KD], 1.0, norm,
                                             ALU.add, ALU.mult).then_inc(gain_done, 1)
                dve.wait_ge(gain_done, 2)
                scale_rows(0)
                for m in range(len(pairs)):
                    if m + 1 < len(pairs):
                        scale_rows(m + 1)
                    for n in (2 * m, 2 * m + 1):
                        s = tiles[n][0]
                        dve.wait_ge(turned, n + 1)
                        if low is not None and n >= 2:
                            dve.wait_ge(low_done, n - 1)
                        for k in range(4, KD):
                            ins = dve.tensor_scalar(target(n, k), tp[:, n % SLOTS, 1, (k - 4) * P:(k - 3) * P],
                                                    gain[:, s, k:k + 1], mod[:, s, at_shift + k:at_shift + k + 1],
                                                    ALU.mult, ALU.add)
                        ins.then_inc(out_b, 1)

            @block.tensor
            def _(pe):
                for n in range(len(tiles)):
                    pe.wait_ge(xn_done, n + 1)
                    if n >= SLOTS:
                        pe.wait_ge(out_a, n - SLOTS + 1)
                        pe.wait_ge(out_b, n - SLOTS + 1)
                    for k in range(KD):
                        mm = pe.transpose(tp[:, n % SLOTS, k // 4, (k % 4) * P:(k % 4 + 1) * P],
                                          x[:, n, k * P:(k + 1) * P], g.ident[:])
                    mm.then_inc(turned, 1)


def latents(nc, g):
    io = g.io
    with Phase(nc, "lat") as ph:
        w = ph.sb("w", [P, KD, COL_XM + ROPE])
        sq = ph.sb("sq", [P, 5, N_ALL])
        kr = ph.sb("kr", [P, N_ALL])
        kpe = ph.sb("kpe", [P, N_ALL])
        rstd = ph.sb("rstd", [P, 2, N_ALL])
        t1 = ph.sb("t1", [P, N_LAT])
        ps = ph.ps("ps", [P, 2, BANK])
        w_in, cs_in = ph.sem("w_in"), ph.sem("cs_in")
        full = [ph.sem(f"full{b}") for b in range(2)]
        free = [ph.sem(f"free{b}") for b in range(2)]
        act_step, dve_step, sq_done = ph.sem("act_step"), ph.sem("dve_step"), ph.sem("sq_done")
        root_ready, kpe_ready, kpe_high = ph.sem("root_ready"), ph.sem("kpe_ready"), ph.sem("kpe_high")
        uses = [(m, c) for m in range(3) for c in LAT_CHUNKS] + [(m, c) for m in range(3, 6) for c in ALL_CHUNKS]
        sums = [(0, c) for c in LAT_CHUNKS] + [(1, c) for c in ALL_CHUNKS]
        n1, n2 = len(uses), len(uses) + len(sums)

        with nc.Block() as block:
            @block.sync
            def _(sp):
                view = io["w_in"].rearrange("(k p) n -> p k n", p=P)
                sp.dma_start(w[:, :, 0:COL_XM], view[:, :, 0:COL_XM]).then_inc(w_in, 16)
                sp.dma_start(w[:, :, COL_XM:], view[:, :, COL_KR:COL_XM]).then_inc(w_in, 16)
                sp.dma_start(g.cos[:], io["t_cos"]).then_inc(cs_in, 16)
                sp.dma_start(g.sin[:], io["t_sin"]).then_inc(cs_in, 16)

            @block.tensor
            def _(pe):
                pe.wait_ge(w_in, 32)
                for n, (m, (c0, cn)) in enumerate(uses):
                    b, M = n % 2, P
                    if n >= 2:
                        pe.wait_ge(free[b], n // 2)
                    accumulate(nc, ps[0:M, b, 0:cn], [(w[:, k, m * P:m * P + M], g.hT[:, k, c0:c0 + cn])
                                                      for k in range(KD)]).then_inc(full[b], 1)
                pe.wait_ge(sq_done, n1 - 3)
                for n, (q, (c0, cn)) in enumerate(sums, n1):
                    b = n % 2
                    pe.wait_ge(free[b], n // 2)
                    src = range(3) if q == 0 else range(3, 5)
                    accumulate(nc, ps[:, b, 0:cn], [(g.ones[:], sq[:, k, c0:c0 + cn]) for k in src]).then_inc(full[b], 1)
                for n, (c0, cn) in enumerate(LAT_CHUNKS, n2):
                    b = n % 2
                    pe.wait_ge(free[b], n // 2)
                    accumulate(nc, ps[:, b, 0:cn], [(g.rot[:], kr[:, c0:c0 + cn])]).then_inc(full[b], 1)

            @block.vector
            def _(dve):
                step = Steps(dve, dve_step)
                for n, (m, (c0, cn)) in enumerate(uses):
                    b = n % 2
                    dst = g.ql[:, m, c0 - N_CTX:c0 - N_CTX + cn] if m < 3 else g.kl[:, m - 3, c0:c0 + cn] if m < 5 \
                        else kr[:, c0:c0 + cn]
                    dve.wait_ge(full[b], n // 2 + 1)
                    dve.tensor_copy(dst, ps[0:dst.shape[0], b, 0:cn]).then_inc(free[b], 1)
                for n, (q, (c0, cn)) in enumerate(sums, n1):
                    b = n % 2
                    dve.wait_ge(full[b], n // 2 + 1)
                    dve.tensor_scalar(rstd[:, q, c0:c0 + cn], ps[:, b, 0:cn], 1.0 / ((QL, KL)[q] * P), EPS,
                                      ALU.mult, ALU.add).then_inc(free[b], 1)
                dve.wait_ge(root_ready, 2)
                step(dve.reciprocal(rstd[:, 0, N_CTX:], rstd[:, 0, N_CTX:]))
                step(dve.reciprocal(rstd[:, 1, :], rstd[:, 1, :]))
                for m in range(QL):
                    step(dve.scalar_tensor_tensor(g.ql[:, m, :], g.ql[:, m, :], g.pa[:, PA_QN + m:PA_QN + m + 1],
                                                  rstd[:, 0, N_CTX:], ALU.mult, ALU.mult))
                for m in range(KL):
                    step(dve.scalar_tensor_tensor(g.kl[:, m, :], g.kl[:, m, :], g.pa[:, PA_KVN + m:PA_KVN + m + 1],
                                                  rstd[:, 1, :], ALU.mult, ALU.mult))
                dve.wait_ge(cs_in, 32)
                for n, (c0, cn) in enumerate(LAT_CHUNKS, n2):
                    b = n % 2
                    dve.wait_ge(full[b], n // 2 + 1)
                    dve.tensor_tensor(t1[:, c0 - N_CTX:c0 - N_CTX + cn], ps[:, b, 0:cn],
                                      g.sin[:, c0 - N_CTX:c0 - N_CTX + cn], ALU.mult).then_inc(free[b], 1)
                for b in range(2):
                    dve.wait_ge(free[b], (n2 + 3 - b) // 2)
                dve.tensor_copy(kpe[:, 0:N_CTX], kr[:, 0:N_CTX])
                step(dve.tensor_tensor(kpe[:, N_CTX:], kr[:, N_CTX:], g.cos[:], ALU.mult))
                dve.tensor_tensor(kpe[:, N_CTX:], kpe[:, N_CTX:], t1[:], ALU.add).then_inc(kpe_ready, 1)
                dve.wait_ge(kpe_high, 1)
                dve.tensor_tensor(g.kpe_lo[:], kpe[0:ROPE, :], g.kpe_hi[0:ROPE, :].bitcast(F32), ALU.subtract)

            @block.scalar
            def _(act):
                for n, (m, (c0, cn)) in enumerate(uses):
                    if m == 5:
                        continue
                    b = n % 2
                    src = g.ql[:, m, c0 - N_CTX:c0 - N_CTX + cn] if m < 3 else g.kl[:, m - 3, c0:c0 + cn]
                    act.wait_ge(free[b], n // 2 + 1)
                    act.activation(sq[:, m, c0:c0 + cn], src, ACT.Square).then_inc(sq_done, 1)
                for b in range(2):
                    act.wait_ge(free[b], (n2 + 1 - b) // 2)
                act.activation(rstd[:, 0, N_CTX:], rstd[:, 0, N_CTX:], ACT.Sqrt).then_inc(root_ready, 1)
                act.activation(rstd[:, 1, :], rstd[:, 1, :], ACT.Sqrt).then_inc(root_ready, 1)
                act.wait_ge(kpe_ready, 1)
                act.activation(g.kpe_hi[:], kpe[:], ACT.Copy).then_inc(kpe_high, 1)


def wait_count(eng, sem, count):
    if not isinstance(count, int) or count > 0:
        eng.wait_ge(sem, count)


def attention(nc, g):
    io = g.io
    with Phase(nc, "att") as ph:
        wq = ph.sb("wq", [P, QL, QK + ROPE])
        wkv = ph.sb("wkv", [P, KL, NOPE + VD])
        qh, qlo = ph.sb("qh", [P, 2, N_LAT], FR), ph.sb("qlo", [P, 2, N_LAT], FR)
        kh, klo = ph.sb("kh", [P, 2, N_ALL], FR), ph.sb("klo", [P, 2, N_ALL], FR)
        qraw = ph.sb("qraw", [P, N_LAT])
        qsum = ph.sb("qsum", [P, N_LAT])
        qp = ph.sb("qp", [P, 2, N_LAT], FR)
        v = ph.sb("v", [P, 2, NT, VD])
        p = ph.sb("p", [P, 2, N_ALL])
        pT = ph.sb("pT", [P, 2, NT, P])
        st = ph.sb("st", [P, 2, 4])
        sc = ph.ps("sc", [P, 2, 3, BANK])
        tb = ph.ps("tb", [P, 2, BANK])
        wt_in = ph.sem("wt_in")
        full = [ph.sem(f"full{b}") for b in range(2)]
        free = [ph.sem(f"free{b}") for b in range(2)]
        high, sum_ready, qp_high, qp_ready = ph.sem("high"), ph.sem("sum_ready"), ph.sem("qp_high"), ph.sem("qp_ready")
        cos_done = ph.sem("cos_done")
        scored, maxed, bias_ready, exped = ph.sem("scored"), ph.sem("maxed"), ph.sem("bias_ready"), ph.sem("exped")
        inv_ready, p_ready = ph.sem("inv_ready"), ph.sem("p_ready")
        ROPE_USE, NOPE_USE, ROT_USE, KEY_USE, VAL_USE, PROJ, TURN = 0, 2, 4, 6, 9, 12, 3
        USES = PROJ + TURN * LT
        LAG = 2
        GROUPS = [(0, 4), (4, 4), (8, 2)]
        HALVES = [slice(c * BANK, (c + 1) * BANK) for c in range(2)]

        def use(head, n):
            m = n if isinstance(head, int) and head == 0 and n < PROJ else n - LAG * TURN
            return m % 2, head * (USES // 2) + m // 2

        def turn_use(head, t, c):
            if t < LT - LAG or isinstance(head, int) and head == HEADS - 1:
                return use(head, PROJ + TURN * (t + LAG) + c)
            return use(head + 1, PROJ + TURN * (t - LT + LAG) + c)

        def steps(head, first):
            if not first:
                for t in range(LT - LAG, LT):
                    yield head - 1, t
            for t in range(LT - LAG):
                yield head, t

        def after(head, t):
            return (head, t + 1) if t + 1 < LT else (head + 1, 0)

        def before(head, t):
            return (head, t - 1) if t else (head - 1, LT - 1)

        def over_heads(eng, body):
            for j in range(2):
                body(j, j, j == 0)
            with eng.Fori(0, HEADS // 2 - 1) as i:
                for j in range(2):
                    body(2 * i + 2 + j, j, False)

        with nc.Block() as block:
            @block.sync
            def _(sp):
                def load(head, j, first):
                    if not first:
                        b, earlier = use(head - 1, PROJ - 1)
                        sp.wait_ge(full[b], earlier + 1)
                    q_cols = io["w_uq"].rearrange("(k p) n -> p k n", p=P)
                    kv_cols = io["w_ukv"].rearrange("(k p) n -> p k n", p=P)
                    sp.dma_start(wq[:, :, 0:QK], q_cols[:, :, ds(head * QK, QK)]).then_inc(wt_in, 16)
                    sp.dma_start(wq[:, :, QK:], q_cols[:, :, ds(head * QK + NOPE, ROPE)]).then_inc(wt_in, 16)
                    sp.dma_start(wkv[:], kv_cols[:, :, ds(head * (NOPE + VD), NOPE + VD)]).then_inc(wt_in, 16)
                over_heads(sp, load)

            @block.tensor
            def _(pe):
                def into_bank(head, n, make):
                    b, earlier = use(head, n)
                    wait_count(pe, free[b], earlier)
                    make(b).then_inc(full[b], 1)

                def project(head, j):
                    pe.wait_ge(wt_in, 48 * (head + 1))
                    for c in range(2):
                        into_bank(head, ROPE_USE + c, lambda b: accumulate(nc, tb[:, b, :], [
                            (wq[:, k, NOPE:], g.ql[:, k, HALVES[c]]) for k in range(QL)]))
                    for c in range(2):
                        into_bank(head, NOPE_USE + c, lambda b: accumulate(nc, tb[:, b, :], [
                            (wq[:, k, 0:NOPE], g.ql[:, k, HALVES[c]]) for k in range(QL)]))
                    for c in range(2):
                        into_bank(head, ROT_USE + c, lambda b: accumulate(nc, tb[:, b, :], [
                            (g.rot[:], qraw[:, HALVES[c]])]))
                    for c, (c0, cn) in enumerate(ALL_CHUNKS):
                        into_bank(head, KEY_USE + c, lambda b: accumulate(nc, tb[:, b, 0:cn], [
                            (wkv[:, k, 0:NOPE], g.kl[:, k, c0:c0 + cn]) for k in range(KL)]))
                    for c, (t0, tn) in enumerate(GROUPS):
                        def values(b):
                            for t in range(tn):
                                mm = accumulate(nc, tb[:, b, t * P:(t + 1) * P], [
                                    (g.kl[:, k, (t0 + t) * P:(t0 + t + 1) * P], wkv[:, k, NOPE:])
                                    for k in range(KL)])
                            return mm
                        into_bank(head, VAL_USE + c, values)

                def scores(head, t, j):
                    n = head * LT + t
                    if t == 0:
                        for c in (1, 2):
                            b, earlier = use(head, PROJ - c)
                            pe.wait_ge(free[b], earlier + 1)
                        pe.wait_ge(qp_ready, head + 1)
                    wait_count(pe, exped, n - 1)
                    tile = slice(t * P, (t + 1) * P)
                    for c0, cn in [(0, BANK), (BANK, BANK), (2 * BANK, N_ALL - 2 * BANK)]:
                        cols = slice(c0, c0 + cn)
                        mm = accumulate(nc, sc[:, t % 2, c0 // BANK, 0:cn], [
                            (qh[:, j, tile], kh[:, j, cols]), (qh[:, j, tile], klo[:, j, cols]),
                            (qlo[:, j, tile], kh[:, j, cols]), (qp[:, j, tile], g.kpe_hi[:, cols]),
                            (qp[0:ROPE, j, tile], g.kpe_lo[:, cols])])
                    mm.then_inc(scored, 1)

                def turn(head, t, c, more=None):
                    def make(b):
                        t0, tn = GROUPS[c]
                        for k in range(tn):
                            mm = pe.transpose(tb[:, b, k * P:(k + 1) * P],
                                              p[:, t % 2, (t0 + k) * P:(t0 + k + 1) * P], g.ident[:])
                        return more(b) if more else mm
                    b, earlier = turn_use(head, t, c)
                    wait_count(pe, free[b], earlier)
                    make(b).then_inc(full[b], 1)

                def output(t, j):
                    return lambda b: accumulate(nc, tb[:, b, 2 * P:3 * P], [
                        (v[:, j, k, :], pT[:, t % 2, k, :]) for k in range(NT)])

                def wait_turned(head, t):
                    for c in (1, 2):
                        b, earlier = turn_use(head, t, c)
                        pe.wait_ge(free[b], earlier + 1)

                def one(head, j, first):
                    project(head, j)
                    if first:
                        for t in range(LAG):
                            scores(head, t, j)
                    for h, t in steps(head, first):
                        scores(head, (t + LAG) % LT, j)
                        pe.wait_ge(p_ready, h * LT + t + 1)
                        turn(h, t, 0)
                        turn(h, t, 1)
                        if first and t == 0:
                            turn(h, t, 2)
                        else:
                            pj = j if h is head and t > 0 else 1 - j
                            turn(h, t, 2, output(before(h, t)[1], pj))

                over_heads(pe, one)
                last = HEADS - 1
                for t in range(LT - LAG, LT):
                    pe.wait_ge(p_ready, last * LT + t + 1)
                    turn(last, t, 0)
                    turn(last, t, 1)
                    turn(last, t, 2, output(t - 1, 1))
                wait_turned(last, LT - 1)
                b, earlier = use(last, USES + LAG * TURN)
                output(LT - 1, 1)(b).then_inc(full[b], 1)

            @block.scalar
            def _(act):
                def out_of_bank(b, earlier, dst, src, sem):
                    act.wait_ge(full[b], earlier + 1)
                    act.activation(dst, src, ACT.Copy).then_inc(sem, 1)

                def exp(head, t):
                    act.wait_ge(bias_ready, head * LT + t + 1)
                    act.activation(p[:, t % 2, :], sc[:, t % 2].rearrange("p b n -> p (b n)")[:, 0:N_ALL], ACT.Exp,
                                   bias=st[:, t % 2, 1:2], scale=ATT_SCALE,
                                   accum_out=st[:, t % 2, 2:3]).then_inc(exped, 1)

                def copy_projections(head, j):
                    for c in range(2):
                        b, earlier = use(head, ROPE_USE + c)
                        out_of_bank(b, earlier, qraw[:, HALVES[c]], tb[:, b, :], free[b])
                    for c in range(2):
                        b, earlier = use(head, NOPE_USE + c)
                        out_of_bank(b, earlier, qh[:, j, HALVES[c]], tb[:, b, :], high)
                    for c, (c0, cn) in enumerate(ALL_CHUNKS):
                        b, earlier = use(head, KEY_USE + c)
                        out_of_bank(b, earlier, kh[:, j, c0:c0 + cn], tb[:, b, 0:cn], high)
                    act.wait_ge(sum_ready, head + 1)
                    act.activation(qp[:, j, :], qsum[:], ACT.Copy).then_inc(qp_high, 1)
                    for c, (t0, tn) in enumerate(GROUPS):
                        b, earlier = use(head, VAL_USE + c)
                        out_of_bank(b, earlier, v[:, j, t0:t0 + tn, :].rearrange("p t d -> p (t d)"),
                                    tb[:, b, 0:tn * P], free[b])

                def copy_turned(head, t, c, output_of=None):
                    t0, tn = GROUPS[c]
                    b, earlier = turn_use(head, t, c)
                    act.wait_ge(full[b], earlier + 1)
                    ins = act.activation(pT[:, t % 2, t0:t0 + tn, :].rearrange("p t d -> p (t d)"),
                                         tb[:, b, 0:tn * P], ACT.Copy)
                    if output_of:
                        ins = copy_output(b, *output_of)
                    ins.then_inc(free[b], 1)

                def copy_output(b, head, t):
                    return act.activation(g.yT[:, ds(head, 1), t * P:(t + 1) * P].rearrange("p o n -> p (o n)"),
                                          tb[:, b, 2 * P:3 * P], ACT.Copy)

                def one(head, j, first):
                    copy_projections(head, j)
                    if first:
                        exp(head, 0)
                    for h, t in steps(head, first):
                        exp(*after(h, t))
                        copy_turned(h, t, 0)
                        copy_turned(h, t, 1)
                        copy_turned(h, t, 2, None if first and t == 0 else before(h, t))

                over_heads(act, one)
                last = HEADS - 1
                for t in range(LT - LAG, LT):
                    if t + 1 < LT:
                        exp(last, t + 1)
                    for c in range(TURN):
                        copy_turned(last, t, c, (last, t - 1) if c == TURN - 1 else None)
                b, earlier = use(last, USES + LAG * TURN)
                act.wait_ge(full[b], earlier + 1)
                copy_output(b, last, LT - 1)

            @block.vector
            def _(dve):
                def maximum(head, t):
                    n = head * LT + t
                    dve.wait_ge(scored, n + 1)
                    dve.tensor_reduce(st[:, t % 2, 0:1], sc[:, t % 2].rearrange("p b n -> p (b n)")[:, 0:N_ALL],
                                      AX.X, ALU.max).then_inc(maxed, 1)
                    dve.wait_ge(maxed, n + 1)
                    dve.tensor_scalar(st[:, t % 2, 1:2], st[:, t % 2, 0:1], -ATT_SCALE, None,
                                      ALU.mult).then_inc(bias_ready, 1)

                def normalise(head, t):
                    n = head * LT + t
                    dve.wait_ge(exped, n + 1)
                    dve.reciprocal(st[:, t % 2, 3:4], st[:, t % 2, 2:3]).then_inc(inv_ready, 1)
                    dve.wait_ge(inv_ready, n + 1)
                    dve.tensor_scalar(p[:, t % 2, :], p[:, t % 2, :], st[:, t % 2, 3:4], None,
                                      ALU.mult).then_inc(p_ready, 1)

                def low(head, n, order, lo, hi):
                    b, _ = use(head, n)
                    dve.wait_ge(high, 5 * head + order + 1)
                    dve.tensor_tensor(lo, tb[:, b, 0:lo.shape[1]], hi.bitcast(F32), ALU.subtract).then_inc(free[b], 1)

                def split(head, j):
                    for c in range(2):
                        low(head, NOPE_USE + c, c, qlo[:, j, HALVES[c]], qh[:, j, HALVES[c]])
                    for c in range(2):
                        b, earlier = use(head, ROT_USE + c)
                        dve.wait_ge(full[b], earlier + 1)
                        dve.tensor_tensor(qsum[:, HALVES[c]], tb[:, b, :], g.sin[:, HALVES[c]],
                                          ALU.mult).then_inc(free[b], 1)
                    dve.tensor_tensor(qraw[:], qraw[:], g.cos[:], ALU.mult).then_inc(cos_done, 1)
                    dve.wait_ge(cos_done, head + 1)
                    dve.tensor_tensor(qsum[:], qsum[:], qraw[:], ALU.add).then_inc(sum_ready, 1)
                    for c, (c0, cn) in enumerate(ALL_CHUNKS):
                        low(head, KEY_USE + c, 2 + c, klo[:, j, c0:c0 + cn], kh[:, j, c0:c0 + cn])
                    dve.wait_ge(qp_high, head + 1)
                    dve.tensor_tensor(qp[ROPE:, j, :], qsum[ROPE:, :], qp[ROPE:, j, :].bitcast(F32),
                                      ALU.subtract).then_inc(qp_ready, 1)

                def one(head, j, first):
                    split(head, j)
                    if first:
                        maximum(head, 0)
                    for h, t in steps(head, first):
                        maximum(*after(h, t))
                        normalise(h, t)

                over_heads(dve, one)
                last = HEADS - 1
                for t in range(LT - LAG, LT):
                    if t + 1 < LT:
                        maximum(last, t + 1)
                    normalise(last, t)


def credit(eng, sem, n):
    eng.sem_inc(sem, n)


def stream_weights(sp, view, w, w_in, tile_done, segs, width=P):
    base = 0
    for col, pairs, _ in segs:
        with sp.Fori(0, pairs) as i:
            for j in range(2):
                sp.wait_ge(tile_done, base + 2 * i + j + 1)
                sp.dma_start(w[:, j], view[:, :, ds(col + (2 * i + j) * width, width)]).then_inc(w_in[j], 16)
        base += 2 * pairs


def project_tiles(nc, pe, w, w_in, tile_done, read_out, ps, hT, segs):
    credit(pe, tile_done, 2)
    base = 0
    for _, pairs, chunks in segs:
        with pe.Fori(0, pairs) as i:
            for j in range(2):
                pe.wait_ge(w_in[j], 16 * (base // 2 + i + 1))
                pe.wait_ge(read_out, base + 2 * i + j + 1)
                for c, (c0, cn) in enumerate(chunks):
                    mm = accumulate(nc, ps[:, j, c, 0:cn], [(w[:, j, k, :], hT[:, k, c0:c0 + cn])
                                                            for k in range(KD)])
                mm.then_inc(tile_done, 1)
        base += 2 * pairs


def gate_attention(nc, g):
    io = g.io
    with Phase(nc, "gat") as ph:
        w = ph.sb("w", [P, 2, KD, P])
        sig = ph.sb("sig", [P, 2, N_LAT])
        ps = ph.ps("ps", [P, 2, 2, BANK])
        w_in = [ph.sem(f"w_in{j}") for j in range(2)]
        tile_done, read_out, gated, stored = ph.sem("tile_done"), ph.sem("read_out"), ph.sem("gated"), ph.sem("stored")
        segs = [(COL_GMLA, KD // 2, LAT_CHUNKS)]
        with nc.Block() as block:
            @block.sync
            def _(sp):
                stream_weights(sp, io["w_in"].rearrange("(k p) n -> p k n", p=P), w, w_in, tile_done, segs)

            @block.tensor
            def _(pe):
                project_tiles(nc, pe, w, w_in, tile_done, read_out, ps, g.hT, segs)

            @block.scalar
            def _(act):
                credit(act, read_out, 2)
                with act.Fori(0, KD // 2) as i:
                    for j in range(2):
                        act.wait_ge(tile_done, 2 * i + j + 3)
                        act.wait_ge(gated, 2 * i + j + 1)
                        act.activation(sig[:, j, :], ps[:, j].rearrange("p c n -> p (c n)"),
                                       ACT.Sigmoid).then_inc(read_out, 1)

            @block.vector
            def _(dve):
                credit(dve, gated, 2)
                with dve.Fori(0, KD // 2) as i:
                    for j in range(2):
                        dve.wait_ge(read_out, 2 * i + j + 3)
                        y = g.yT[:, ds(2 * i + j, 1), :]
                        dve.tensor_tensor(y, y, sig[:, j:j + 1, :], ALU.mult).then_inc(gated, 1)

            @block.gpsimd
            def _(pool):
                pool.wait_ge(gated, KD + 2)
                pool.dma_start(g.y_dram.rearrange("k p n -> p k n"), g.yT[:]).then_inc(stored, 16)
                pool.wait_ge(stored, 16)


PAD = TAPS // 2
W_PAD = N_ALL + 3 * PAD
OFF_CTX, OFF_LAT = PAD, 2 * PAD + N_CTX


def padded(c):
    return OFF_CTX + c * P if c < CT else OFF_LAT + (c - CT) * P


def inner(nc, g):
    io = g.io
    with Phase(nc, "inn") as ph:
        w = ph.sb("w", [P, 2, KD, P])
        cv = ph.sb("cv", [P, 2, W_PAD])
        ps = ph.ps("ps", [P, 2, 3, BANK])
        w_in = [ph.sem(f"w_in{j}") for j in range(2)]
        tile_done, read_out, conv_done = ph.sem("tile_done"), ph.sem("read_out"), ph.sem("conv_done")
        tap, xc_done, zeroed, stored = ph.sem("tap"), ph.sem("xc_done"), ph.sem("zeroed"), ph.sem("stored")
        gate_in = ph.sem("gate_in")
        segs = [(COL_XM, KD // 2, ALL_CHUNKS)]
        n_out = W_PAD - 2 * PAD
        with nc.Block() as block:
            @block.sync
            def _(sp):
                stream_weights(sp, io["w_in"].rearrange("(k p) n -> p k n", p=P), w, w_in, tile_done, segs)
                for q, name in enumerate(["w_qblk", "w_kblk", "w_vblk"]):
                    sp.dma_start(g.dense[:, q], io[name].rearrange("(t n) j k -> (n j) t k", t=KD)).then_inc(gate_in, 16)
                sp.dma_start(g.block4[:], io["t_block4"]).then_inc(gate_in, 16)
                sp.dma_start(g.wg[:], io["w_gate"].rearrange("(t p) n -> p t n", p=P)).then_inc(gate_in, 16)
                sp.dma_start(g.bg[:], spread(io["b_gate"])).then_inc(gate_in, 16)
                for t in range(KD):
                    sp.wait_ge(xc_done, 3 + t)
                    sp.dma_start(g.xm_dram[t], g.xm[:, t, :]).then_inc(stored, 16)
                    sp.dma_start(g.xc_dram[t], g.xc[:, t, :]).then_inc(stored, 16)
                sp.wait_ge(stored, 32 * KD)
                sp.wait_ge(gate_in, 96)

            @block.tensor
            def _(pe):
                project_tiles(nc, pe, w, w_in, tile_done, read_out, ps, g.hT, segs)

            @block.gpsimd
            def _(pool):
                for a in (0, OFF_CTX + N_CTX, OFF_LAT + N_LAT):
                    pool.memset(g.xm[:, :, a:a + PAD], 0.0).then_inc(zeroed, 1)

            @block.scalar
            def _(act):
                with act.Fori(0, KD // 2) as i:
                    for j in range(2):
                        t = 2 * i + j
                        act.wait_ge(tile_done, t + 3)
                        act.activation(g.xm[:, ds(t, 1), OFF_LAT:OFF_LAT + N_LAT].rearrange("p o n -> p (o n)"),
                                       ps[:, j, 0:2, :].rearrange("p c n -> p (c n)"), ACT.Copy)
                        act.activation(g.xm[:, ds(t, 1), OFF_CTX:OFF_CTX + N_CTX].rearrange("p o n -> p (o n)"),
                                       ps[:, j, 2, 0:N_CTX], ACT.Copy).then_inc(read_out, 1)
                        act.wait_ge(conv_done, t + 1)
                        for a, b, n in ((OFF_CTX - PAD, 0, N_CTX), (OFF_LAT - PAD, N_CTX, N_LAT)):
                            ins = act.activation(g.xc[:, ds(t, 1), b:b + n].rearrange("p o n -> p (o n)"),
                                                 cv[:, j, a:a + n], ACT.Silu,
                                                 bias=g.pa[:, ds(PA_CB + t, 1)])
                        ins.then_inc(xc_done, 1)

            @block.vector
            def _(dve):
                credit(dve, read_out, 2)
                credit(dve, xc_done, 2)
                dve.wait_ge(zeroed, 3)
                with dve.Fori(0, KD // 2) as i:
                    for j in range(2):
                        t = 2 * i + j
                        dve.wait_ge(read_out, t + 3)
                        dve.wait_ge(xc_done, t + 1)
                        for tp in range(TAPS):
                            src = g.xm[:, ds(t, 1), tp:tp + n_out].rearrange("p o n -> p (o n)")
                            cw = g.pa[:, ds(PA_CW + tp * KD + t, 1)]
                            if tp == 0:
                                dve.tensor_scalar(cv[:, j, 0:n_out], src, cw, None, ALU.mult).then_inc(tap, 1)
                            else:
                                dve.wait_ge(tap, t * (TAPS - 1) + tp)
                                dve.scalar_tensor_tensor(cv[:, j, 0:n_out], src, cw, cv[:, j, 0:n_out], ALU.mult,
                                                         ALU.add).then_inc(tap if tp < TAPS - 1 else conv_done, 1)


def gates(nc, g):
    io = g.io
    with Phase(nc, "gts") as ph:
        dense, block4, wg, bg = g.dense, g.block4, g.wg, g.bg
        bd = ph.sb("bd", [P, 3, KD, P])
        bdt = ph.sb("bdt", [P, 3, KD, P])
        wg2 = ph.sb("wg2", [P, 2 * KD, 16])
        ps = ph.ps("ps", [P, 2, BANK])
        pw = ph.ps("pw", [P, BANK])
        pg = ph.ps("pg", [P, BANK])
        grow = ph.sb("grow", [16, N_ALL])
        pr = ph.ps("pr", [16, 3, BANK])
        row_full, row_copied = ph.sem("row_full"), ph.sem("row_copied")
        built, turned, copied = ph.sem("built"), ph.sem("turned"), ph.sem("copied")
        folded, wg_ready, summed, done, scaled, stored = (ph.sem("folded"), ph.sem("wg_ready"), ph.sem("summed"),
                                                          ph.sem("done"), ph.sem("scaled"), ph.sem("stored"))
        with nc.Block() as block:
            @block.sync
            def _(sp):
                sp.wait_ge(scaled, 1)
                sp.dma_start(g.bd_dram.rearrange("t p q n -> p q t n"), bd[:]).then_inc(stored, 16)
                sp.wait_ge(stored, 16)

            @block.vector
            def _(dve):
                for q in range(3):
                    for t in range(KD):
                        ins = dve.tensor_tensor(
                            bd[:, q, t, :].rearrange("p (n k) -> p n k", k=4),
                            dense[:, q, t:t + 1, :].to_broadcast([P, 32, 4]),
                            block4[:].rearrange("p (n k) -> p n k", k=4), ALU.mult)
                ins.then_inc(built, 1)
                for n in range(6):
                    dve.wait_ge(turned, n + 1)
                    dve.tensor_copy(bdt[:].rearrange("p q t n -> p (q t n)")[:, n * BANK:(n + 1) * BANK],
                                    ps[:, n % 2, :]).then_inc(copied, 1)
                dve.tensor_scalar(bd[:, 1], bd[:, 1], DH ** -0.5, None, ALU.mult).then_inc(scaled, 1)
                dve.wait_ge(folded, 1)
                dve.tensor_copy(wg2[:].rearrange("p t n -> p (t n)"), pw[:, 0:32 * KD]).then_inc(wg_ready, 1)
                for n, (c0, cn) in enumerate(ALL_CHUNKS):
                    dve.wait_ge(row_full, n + 1)
                    dve.tensor_copy(grow[:, c0:c0 + cn], pr[:, n, 0:cn]).then_inc(row_copied, 1)
                dve.wait_ge(summed, 1)
                dve.tensor_tensor(g.gts[:], pg[:, 0:16 * NT].rearrange("p (c n) -> p c n", n=16),
                                  bg[:].rearrange("p (o n) -> p o n", o=1).to_broadcast([P, NT, 16]),
                                  ALU.add).then_inc(done, 1)

            @block.tensor
            def _(pe):
                pe.wait_ge(built, 1)
                for n in range(6):
                    if n >= 2:
                        pe.wait_ge(copied, n - 1)
                    for k in range(4):
                        q, t = divmod(4 * n + k, KD)
                        mm = pe.transpose(ps[:, n % 2, k * P:(k + 1) * P], bd[:, q, t, :], g.ident[:])
                    mm.then_inc(turned, 1)
                pe.wait_ge(copied, 6)
                for t in range(KD):
                    accumulate(nc, pw[:, t * 16:t * 16 + 16], [(bdt[:, q, t, :], wg[:, q * KD + t, :]) for q in (0, 1)])
                for t in range(KD):
                    mm = accumulate(nc, pw[:, (KD + t) * 16:(KD + t) * 16 + 16], [(bdt[:, 2, t, :], wg[:, 2 * KD + t, :])])
                mm.then_inc(folded, 1)
                pe.wait_ge(wg_ready, 1)
                for n, (c0, cn) in enumerate(ALL_CHUNKS):
                    a = padded(c0 // P)
                    accumulate(nc, pr[:, n, 0:cn], [(wg2[:, t, :], g.xc[:, t, c0:c0 + cn]) for t in range(KD)]
                               + [(wg2[:, KD + t, :], g.xm[:, t, a:a + cn]) for t in range(KD)]).then_inc(row_full, 1)
                pe.wait_ge(row_copied, 3)
                for c in range(NT):
                    mm = pe.transpose(pg[:, c * 16:c * 16 + 16], grow[:, c * P:(c + 1) * P], g.ident[0:16, 0:16])
                mm.then_inc(summed, 1)


def natural(u):
    return CT - 1 - u if u < CT else NT - 1 - (u - CT)


ROWS = 36
G_G, G_M, G_WI, G_EM, G_WK, G_KEEP = range(6)


def gate_rows(nc, g):
    io = g.io
    with Phase(nc, "gro") as ph:
        cat = ph.sb("cat", [P, NT, 2, ROWS])
        r = ph.sb("r", [ROWS, 2, N_ALL])
        b = ph.sb("b", [ROWS, N_ALL])
        e = ph.sb("e", [ROWS, N_ALL])
        reset = ph.sb("reset", [ROWS, N_ALL])
        m = ph.sb("m", [ROWS, NT + 1])
        qr = ph.sb("qr", [ROWS, 6, N_ALL])
        colp = ph.sb("colp", [P, NT, 6, ROWS])
        colb = ph.sb("colb", [P, NT, 6, 4])
        rv = ph.ps("rv", [P, BANK])
        tp = ph.ps("tp", [P, 2, BANK])
        loaded, cleared, rev_done, cat_done = ph.sem("loaded"), ph.sem("cleared"), ph.sem("rev_done"), ph.sem("cat_done")
        turned, copied, dve_step, act_step = ph.sem("turned"), ph.sem("copied"), ph.sem("dve_step"), ph.sem("act_step")
        to_act, rows_ready, colt, colc = ph.sem("to_act"), ph.sem("rows_ready"), ph.sem("colt"), ph.sem("colc")
        brev, bcopied = ph.sem("brev"), ph.sem("bcopied")
        stored = ph.sem("stored")
        N_T = 5
        n_col = (NT * 6 + 13) // 14
        with nc.Block() as block:
            @block.sync
            def _(sp):
                sp.dma_start(reset[:], io["t_reset"]).then_inc(loaded, 16)
                sp.wait_ge(bcopied, 2 * NT + 1)
                sp.dma_start(g.col_dram.rearrange("h p u q d -> p u q h d"), g.cols[:]).then_inc(stored, 16)
                sp.wait_ge(stored, 16)

            @block.gpsimd
            def _(pool):
                pool.memset(cat[:], 0.0).then_inc(cleared, 1)
                pool.memset(m[:], 0.0).then_inc(cleared, 1)

            @block.tensor
            def _(pe):
                nc.tensor.matmul(rv[:, 0:NT * 16], g.rev[:], g.gts[:].rearrange("p c n -> p (c n)"), start=True,
                                 stop=True).then_inc(rev_done, 1)
                pe.wait_ge(cat_done, 1 + NT)
                for n in range(N_T):
                    if n >= 2:
                        pe.wait_ge(copied, n - 1)
                    for k in range(4):
                        q, u = divmod(4 * n + k, NT)
                        mm = pe.transpose(tp[0:ROWS, n % 2, k * P:(k + 1) * P], cat[:, u, q, :], g.ident[:])
                    mm.then_inc(turned, 1)
                pe.wait_ge(rows_ready, 1)
                for n in range(n_col):
                    if n >= 2:
                        pe.wait_ge(colc, n - 1)
                    for k in range(min(14, NT * 6 - 14 * n)):
                        u, q = divmod(14 * n + k, 6)
                        mm = pe.transpose(tp[:, n % 2, k * ROWS:(k + 1) * ROWS], qr[:, q, u * P:(u + 1) * P],
                                          g.ident[0:ROWS, 0:ROWS])
                    mm.then_inc(colt, 1)
                pe.wait_ge(bcopied, 1)
                nc.tensor.matmul(rv[:, 0:NT * 24], g.rev[:], colb[:].rearrange("p u q h -> p (u q h)"), start=True,
                                 stop=True).then_inc(brev, 1)

            @block.scalar
            def _(act):
                act.wait_ge(to_act, 1)
                act.activation(e[:], e[:], ACT.Exp, scale=-1.0).then_inc(act_step, 1)
                act.wait_ge(act_step, 1)
                act.activation(e[:], e[:], ACT.Ln, bias=1.0).then_inc(act_step, 1)
                act.wait_ge(to_act, 2)
                act.activation(qr[:, G_WI, :], qr[:, G_WI, :], ACT.Exp)
                act.activation(qr[:, G_EM, :], qr[:, G_EM, :], ACT.Exp, scale=-1.0)
                act.activation(qr[:, G_WK, :], qr[:, G_WK, :], ACT.Exp)
                act.activation(qr[:, G_KEEP, :], qr[:, G_KEEP, :], ACT.Exp).then_inc(rows_ready, 1)

            @block.vector
            def _(dve):
                step = Steps(dve, dve_step)
                dve.wait_ge(cleared, 2)
                gv = g.gts[:].rearrange("p u (d q h) -> p u d q h", d=2, q=2)
                dve.tensor_copy(cat[:, :, :, 0:4], gv[:, :, 0]).then_inc(cat_done, 1)
                dve.wait_ge(rev_done, 1)
                rvv = rv[:, 0:NT * 16].rearrange("p (u d q h) -> p u d q h", u=NT, d=2, q=2)
                for u in range(NT):
                    dve.tensor_copy(cat[:, u, :, 32:36], rvv[:, natural(u), 1]).then_inc(cat_done, 1)
                for n in range(N_T):
                    dve.wait_ge(turned, n + 1)
                    dve.tensor_copy(r[:].rearrange("p q n -> p (q n)")[:, n * BANK:(n + 1) * BANK],
                                    tp[0:ROWS, n % 2, :]).then_inc(copied, 1)
                dve.wait_ge(copied, N_T)
                dve.scalar_tensor_tensor(e[:], r[:, 1, :], -1.0, r[:, 1, :], ALU.mult, ALU.max).then_inc(to_act, 1)
                dve.wait_ge(act_step, 2)
                step(dve.scalar_tensor_tensor(r[:, 1, :], r[:, 1, :], 0.0, e[:], ALU.min, ALU.subtract))
                dve.wait_ge(loaded, 16)
                step(dve.tensor_tensor_scan(b[:], reset[:], r[:, 1, :], 0.0, ALU.mult, ALU.add))
                step(dve.tensor_tensor(qr[:, G_G, :], r[:, 0, :], b[:], ALU.subtract))
                for u in range(NT):
                    a, z = u * P, (u + 1) * P
                    step(dve.tensor_tensor_scan(qr[:, G_M, a:z], qr[:, G_G, a:z], qr[:, G_G, a:z], m[:, u:u + 1],
                                                ALU.max, ALU.max))
                    step(dve.tensor_tensor(m[:, u + 1:u + 2], qr[:, G_M, z - 1:z], b[:, z - 1:z], ALU.add))
                tiles = lambda q: qr[:, q, :].rearrange("p (u t) -> p u t", t=P)
                at_start = m[:, 0:NT].rearrange("p (u o) -> p u o", o=1).to_broadcast([ROWS, NT, P])
                at_end = tiles(G_M)[:, :, P - 1:P].to_broadcast([ROWS, NT, P])
                step(dve.tensor_tensor(tiles(G_WI), at_start, tiles(G_M), ALU.subtract))
                step(dve.tensor_tensor(qr[:, G_EM, :], b[:], qr[:, G_M, :], ALU.add))
                step(dve.tensor_tensor(tiles(G_WK), tiles(G_G), at_end, ALU.subtract))
                dve.tensor_tensor(tiles(G_KEEP), at_start, at_end, ALU.subtract).then_inc(to_act, 1)
                flat = colp[:].rearrange("p u q r -> p (u q r)")
                for n in range(n_col):
                    w = min(14, NT * 6 - 14 * n) * ROWS
                    dve.wait_ge(colt, n + 1)
                    dve.tensor_copy(flat[:, n * 14 * ROWS:n * 14 * ROWS + w], tp[:, n % 2, 0:w]).then_inc(colc, 1)
                dve.wait_ge(colc, n_col)
                dve.tensor_copy(colb[:], colp[:, :, :, 32:36]).then_inc(bcopied, 1)
                for u in range(NT):
                    dve.tensor_copy(g.cols[:, u, :, :, 0], colp[:, u, :, 0:4]).then_inc(bcopied, 1)
                dve.wait_ge(brev, 1)
                rb = rv[:, 0:NT * 24].rearrange("p (u q h) -> p u q h", u=NT, q=6)
                for u in range(NT):
                    dve.tensor_copy(g.cols[:, u, :, :, 1], rb[:, u]).then_inc(bcopied, 1)


def mlstm(nc, g):
    io = g.io
    with Phase(nc, "mls") as ph:
        xc = ph.sb("xc", [P, 2, 2, N_ALL])
        xm = ph.sb("xm", [P, 2, 2, W_PAD])
        bd = ph.sb("bd", [P, 2, 2, 3, P])
        col = ph.sb("col", [P, 2, NT, 6, 2])
        qT = ph.sb("qT", [P, 2, N_LAT])
        kT = ph.sb("kT", [P, 2, N_LAT])
        k = ph.sb("k", [P, NT, DH])
        v = ph.sb("v", [P, NT, DH + 1])
        diag = ph.sb("diag", [P, 2, P])
        x1 = ph.sb("x1", [P, 2, P])
        e = ph.sb("e", [P, 2, P])
        pm = ph.sb("pm", [P, 2, P])
        vw = ph.sb("vw", [P, 2, DH + 1])
        ct = ph.sb("ct", [P, 2, 2, DH + 1])
        ti = ph.sb("ti", [P, 2, DH])
        num = ph.sb("num", [P, 2, DH])
        den = ph.sb("den", [P, 2, 2])
        dn = ph.sb("dn", [P, 4, 2])
        sb_ = ph.ps("s", [P, 2, BANK])
        hb = ph.ps("h", [P, 2, BANK])
        ub = ph.ps("u", [P, 2, 2, BANK])
        S, H, U = sb_, hb, ub
        ld = [ph.sem(f"ld{j}") for j in range(2)]
        full = [ph.sem(f"full{b}") for b in range(2)]
        free = [ph.sem(f"free{b}") for b in range(2)]
        ones_set, diag_ready, s_done, x1_done = ph.sem("ones_set"), ph.sem("diag_ready"), ph.sem("s_done"), ph.sem("x1_done")
        e_done, p_ready, vw_ready, u_done = ph.sem("e_done"), ph.sem("p_ready"), ph.sem("vw_ready"), ph.sem("u_done")
        ct_done, inter_done, ti_done, intra_done = (ph.sem("ct_done"), ph.sem("inter_done"), ph.sem("ti_done"),
                                                    ph.sem("intra_done"))
        den_done, h_done, dve_step = ph.sem("den_done"), ph.sem("h_done"), ph.sem("dve_step")
        PU = 18
        NU, NO = 2 * (NT - 1), 2 * LT

        def tile_of(u, d):
            return u if d == 0 else natural(u)

        def projections(j):
            out = []
            for q, dst in ((0, qT), (1, kT)):
                for t in range(2):
                    for c in range(2):
                        out.append((dst[:, t, c * BANK:(c + 1) * BANK],
                                    [(0, BANK, bd[:, j, t, q, :], xc[:, j, t, N_CTX + c * BANK:N_CTX + (c + 1) * BANK])]))
            for q, dst in ((1, k), (2, v)):
                for c in range(0, NT, 2):
                    parts = []
                    for a in range(2):
                        for t in range(2):
                            lhs = xc[:, j, t, (c + a) * P:(c + a + 1) * P] if q == 1 else \
                                xm[:, j, t, padded(c + a):padded(c + a) + P]
                            parts.append((a * DH + t * P, P, lhs, bd[:, j, t, q, :]))
                    out.append((dst[:, c:c + 2, 0:DH], parts))
            return out

        with nc.Block() as block:
            @block.sync
            def _(sp):
                for head in range(ML_HEADS):
                    j = head % 2
                    if head >= 2:
                        sp.wait_ge(h_done, (head - 1) * NO + 1)
                    sp.dma_start(bd[:, j], g.bd_dram[2 * head:2 * head + 2].rearrange("t p q n -> p t q n")).then_inc(ld[j], 16)
                    sp.dma_start(xc[:, j], g.xc_dram[2 * head:2 * head + 2].rearrange("t p n -> p t n")).then_inc(ld[j], 16)
                    sp.dma_start(xm[:, j], g.xm_dram[2 * head:2 * head + 2].rearrange("t p n -> p t n")).then_inc(ld[j], 16)
                    sp.dma_start(col[:, j], g.col_dram[head]).then_inc(ld[j], 16)

            @block.gpsimd
            def _(pool):
                pool.memset(v[:, :, DH:DH + 1], 1.0).then_inc(ones_set, 1)
                pool.wait_ge(ones_set, 1)
                with pool.Fori(0, ML_HEADS // 2) as i:
                    for j in range(2):
                        head = 2 * i + j
                        pool.wait_ge(ld[j], 64 * (i + 1))
                        for b in range(2):
                            pool.wait_ge(free[b], (head + 1) * (PU // 2) + 1)
                        for u in range(NT):
                            for d in range(2):
                                c, n = tile_of(u, d), 2 * u + d
                                if u < NT - 1:
                                    if n >= 2:
                                        pool.wait_ge(u_done, head * NU + n)
                                    else:
                                        pool.wait_ge(u_done, head * NU + 1)
                                    pool.tensor_tensor(vw[:, d, :], v[:, c, :], col[:, j, u, G_WK, d:d + 1]
                                                       .to_broadcast([P, DH + 1]), ALU.mult).then_inc(vw_ready, 1)
                            for d in range(2):
                                if u >= CT:
                                    m = 2 * (u - CT) + d
                                    pool.wait_ge(s_done, head * NO + max(m, 1))
                                    pool.tensor_tensor(diag[:, d, :], g.ident[:], col[:, j, u, G_M, d:d + 1]
                                                       .to_broadcast([P, P]), ALU.mult).then_inc(diag_ready, 1)

            @block.tensor
            def _(pe):
                pe.wait_ge(ones_set, 1)
                pe.sem_inc(u_done, 1)
                pe.sem_inc(s_done, 1)
                with pe.Fori(0, ML_HEADS // 2) as i:
                    for j in range(2):
                        head = 2 * i + j
                        pe.wait_ge(ld[j], 64 * (i + 1))
                        pe.wait_ge(ct_done, head * NU + 1)
                        for n, (dst, parts) in enumerate(projections(j)):
                            b = n % 2
                            pe.wait_ge(free[b], head * (PU // 2) + n // 2 + 1)
                            for at, w, lhsT, rhs in parts:
                                mm = accumulate(nc, U[:, 0, b, at:at + w], [(lhsT, rhs)])
                            mm.then_inc(full[b], 1)
                        for b in range(2):
                            pe.wait_ge(free[b], (head + 1) * (PU // 2) + 1)
                        for u in range(NT):
                            if u >= CT:
                                for d in range(2):
                                    c, m = tile_of(u, d) - CT, 2 * (u - CT) + d
                                    pe.wait_ge(diag_ready, head * NO + m + 1)
                                    pe.wait_ge(den_done, head * LT + u - CT + 1)
                                    accumulate(nc, S[:, d, 0:P], [(g.ones[:], diag[:, d, :])])
                                    accumulate(nc, S[:, d, P:2 * P], [
                                        (kT[:, t, c * P:(c + 1) * P], qT[:, t, c * P:(c + 1) * P])
                                        for t in range(2)]).then_inc(s_done, 1)
                            for d in range(2):
                                c, n = tile_of(u, d), 2 * u + d
                                if u >= CT:
                                    m = 2 * (u - CT) + d
                                    pe.wait_ge(ct_done, head * NU + n)
                                    pe.wait_ge(h_done, head * NO + max(m, 1))
                                    accumulate(nc, H[:, d, DH:2 * DH], [
                                        (qT[:, t, (c - CT) * P:(c - CT + 1) * P], ct[:, d, t, 0:DH])
                                        for t in range(2)]).then_inc(inter_done, 1)
                                if u < NT - 1:
                                    pe.wait_ge(vw_ready, head * NU + n + 1)
                                    pe.wait_ge(ct_done, head * NU + max(n, 1))
                                    if u >= CT:
                                        pe.wait_ge(p_ready, head * NO + 2 * (u - CT) + d + 1)
                                        accumulate(nc, S[:, d, 2 * P + 1:2 * P + 2], [
                                            (qT[:, t, (c - CT) * P:(c - CT + 1) * P], ct[:, d, t, DH:DH + 1])
                                            for t in range(2)])
                                    for t in range(2):
                                        mm = accumulate(nc, U[:, d, t, 0:DH + 1], [(k[:, c, t * P:(t + 1) * P], vw[:, d, :])])
                                    mm.then_inc(u_done, 1)
                            if u >= CT:
                                for d in range(2):
                                    c, m = tile_of(u, d), 2 * (u - CT) + d
                                    pe.wait_ge(p_ready, head * NO + m + 1)
                                    pe.wait_ge(ti_done, head * NO + m + 1)
                                    if u == NT - 1:
                                        accumulate(nc, S[:, d, 2 * P + 1:2 * P + 2], [
                                            (qT[:, t, (c - CT) * P:(c - CT + 1) * P], ct[:, d, t, DH:DH + 1])
                                            for t in range(2)])
                                    accumulate(nc, S[:, d, 2 * P:2 * P + 1], [(pm[:, d, :], v[:, c, DH:DH + 1])])
                                    accumulate(nc, H[:, d, 0:DH], [(pm[:, d, :], v[:, c, 0:DH])]).then_inc(intra_done, 1)

            @block.scalar
            def _(act):
                act.sem_inc(free[0], 1)
                act.sem_inc(free[1], 1)
                with act.Fori(0, ML_HEADS // 2) as i:
                    for j in range(2):
                        head = 2 * i + j
                        for n, (dst, parts) in enumerate(projections(j)):
                            if n % 2 == 0:
                                act.wait_ge(full[0], head * (PU // 2) + n // 2 + 1)
                                src = U[:, 0, 0, :] if n < 8 else U[:, 0, 0, :].rearrange("p (a n) -> p a n", a=2)
                                act.activation(dst, src, ACT.Copy).then_inc(free[0], 1)
                        for u in range(CT, NT):
                            for d in range(2):
                                m = 2 * (u - CT) + d
                                act.wait_ge(x1_done, head * NO + m + 1)
                                act.activation(e[:, d, :], x1[:, d, :], ACT.Exp, scale=-1.0).then_inc(e_done, 1)
                            for d in range(2):
                                m = 2 * (u - CT) + d
                                act.wait_ge(inter_done, head * NO + m + 1)
                                act.activation(ti[:, d, :], H[:, d, DH:2 * DH], ACT.Copy,
                                               scale=col[:, j, u, G_WI, d:d + 1]).then_inc(ti_done, 1)

            @block.vector
            def _(dve):
                step = Steps(dve, dve_step)
                for s in (ct_done, den_done, h_done):
                    dve.sem_inc(s, 1)
                with dve.Fori(0, ML_HEADS // 2) as i:
                    step.n = 0
                    per_round = 2 * LT * 7
                    step.base = i * per_round
                    for j in range(2):
                        head = 2 * i + j
                        dve.wait_ge(ld[j], 64 * (i + 1))
                        for n, (dst, parts) in enumerate(projections(j)):
                            if n % 2 == 1:
                                dve.wait_ge(full[1], head * (PU // 2) + n // 2 + 1)
                                src = U[:, 0, 1, :] if n < 8 else U[:, 0, 1, :].rearrange("p (a n) -> p a n", a=2)
                                dve.tensor_copy(dst, src).then_inc(free[1], 1)
                        for u in range(NT):
                            if u >= CT:
                                for d in range(2):
                                    m = 2 * (u - CT) + d
                                    dve.wait_ge(s_done, head * NO + m + 2)
                                    dve.scalar_tensor_tensor(x1[:, d, :], S[:, d, 0:P], col[:, j, u, G_G, d:d + 1],
                                                             g.causal[:, d, :], ALU.subtract, ALU.add).then_inc(x1_done, 1)
                                for d in range(2):
                                    m = 2 * (u - CT) + d
                                    dve.wait_ge(e_done, head * NO + m + 1)
                                    dve.tensor_tensor(pm[:, d, :], e[:, d, :], S[:, d, P:2 * P],
                                                      ALU.mult).then_inc(p_ready, 1)
                            if u < NT - 1:
                                for d in range(2):
                                    n = 2 * u + d
                                    dve.wait_ge(u_done, head * NU + n + 2)
                                    for t in range(2):
                                        if u == 0:
                                            ins = dve.tensor_copy(ct[:, d, t, :], U[:, d, t, 0:DH + 1])
                                        else:
                                            ins = dve.scalar_tensor_tensor(
                                                ct[:, d, t, :], ct[:, d, t, :], col[:, j, u, G_KEEP, d:d + 1],
                                                U[:, d, t, 0:DH + 1], ALU.mult, ALU.add)
                                    ins.then_inc(ct_done, 1)
                            if u >= CT:
                                m = 2 * (u - CT)
                                dve.wait_ge(intra_done, head * NO + m + 2)
                                dve.tensor_copy(den[:], S[:, :, 2 * P:2 * P + 2]).then_inc(den_done, 1)
                                dve.wait_ge(den_done, head * LT + u - CT + 2)
                                step(dve.tensor_tensor(dn[:, 0, :], den[:, :, 1], col[:, j, u, G_WI, :], ALU.mult))
                                step(dve.tensor_tensor(dn[:, 1, :], dn[:, 0, :], den[:, :, 0], ALU.add))
                                step(dve.scalar_tensor_tensor(dn[:, 2, :], dn[:, 1, :], -1.0, dn[:, 1, :], ALU.mult, ALU.max))
                                step(dve.tensor_tensor(dn[:, 2, :], dn[:, 2, :], col[:, j, u, G_EM, :], ALU.max))
                                step(dve.reciprocal(dn[:, 3, :], dn[:, 2, :]))
                                for d in range(2):
                                    step(dve.tensor_tensor(num[:, d, :], ti[:, d, :], H[:, d, 0:DH], ALU.add))
                                for d in range(2):
                                    c = tile_of(u, d) - CT
                                    dst = g.hs[:, c, ds(head * DH, DH)]
                                    first = u - CT < LT // 2
                                    if first:
                                        ins = dve.tensor_scalar(dst, num[:, d, :], dn[:, 3, d:d + 1], None, ALU.mult)
                                    else:
                                        ins = dve.scalar_tensor_tensor(dst, num[:, d, :], dn[:, 3, d:d + 1], dst,
                                                                       ALU.mult, ALU.add)
                                    ins.then_inc(h_done, 1)
                    assert step.n == per_round


def readout(nc, g):
    io = g.io
    with Phase(nc, "rdo") as ph:
        ss = ph.sb("ss", [P, LT, ML_HEADS])
        hn = ph.sb("hn", [P, KD, N_LAT])
        w = ph.sb("w", [P, 2, KD, P])
        sig = ph.sb("sig", [P, 2, N_LAT])
        xc = ph.sb("xc", [P, 2, N_LAT])
        y = ph.sb("y", [P, 2, N_LAT])
        tp = ph.ps("tp", [P, 4, BANK])
        ps = ph.ps("ps", [P, 2, 2, BANK])
        squared, var_done, root_done, inv_done, scaled = (ph.sem("squared"), ph.sem("var_done"), ph.sem("root_done"),
                                                          ph.sem("inv_done"), ph.sem("scaled"))
        turned = ph.sem("turned")
        out_of = [ph.sem(f"out_of{b}") for b in range(2)]
        w_in = [ph.sem(f"w_in{j}") for j in range(2)]
        xy_in = [ph.sem(f"xy_in{j}") for j in range(2)]
        tile_done, sig_done, merged, stored, dve_step = (ph.sem("tile_done"), ph.sem("sig_done"), ph.sem("merged"),
                                                         ph.sem("stored"), ph.sem("dve_step"))
        wv = io["w_in"].rearrange("(k p) n -> p k n", p=P)
        with nc.Block() as block:
            @block.sync
            def _(sp):
                with sp.Fori(0, KD) as t:
                    for j, col in ((0, COL_Z), (1, COL_GML)):
                        sp.wait_ge(tile_done, 2 * t + j + 1)
                        sp.dma_start(w[:, j], wv[:, :, ds(col + t * P, P)]).then_inc(w_in[j], 16)

            @block.gpsimd
            def _(pool):
                with pool.Fori(0, KD // 2) as i:
                    for j in range(2):
                        t = 2 * i + j
                        pool.wait_ge(merged, t + 1)
                        pool.dma_start(xc[:, j:j + 1, :], g.xc_dram[ds(t, 1), :, N_CTX:].rearrange("o p n -> p o n")
                                       ).then_inc(xy_in[j], 16)
                        pool.dma_start(y[:, j:j + 1, :], g.y_dram[ds(t, 1)].rearrange("o p n -> p o n")
                                       ).then_inc(xy_in[j], 16)

            @block.tensor
            def _(pe):
                for t in range(KD):
                    for half in range(2):
                        n = 2 * t + half
                        if n == 0:
                            pe.wait_ge(scaled, LT)
                        if n >= 4:
                            pe.wait_ge(out_of[n % 2], n // 2 - 1)
                        for c in range(4):
                            mm = pe.transpose(tp[:, n % 4, c * P:(c + 1) * P],
                                              g.hs[:, 4 * half + c, t * P:(t + 1) * P], g.ident[:])
                        mm.then_inc(turned, 1)
                credit(pe, tile_done, 2)
                with pe.Fori(0, KD) as t:
                    for j in range(2):
                        pe.wait_ge(w_in[j], 16 * (t + 1))
                        pe.wait_ge(sig_done, 2 * t + j + 1)
                        for c, (c0, cn) in enumerate(LAT_CHUNKS):
                            mm = accumulate(nc, ps[:, j, c, :], [(w[:, j, k, :], g.hT[:, k, c0:c0 + cn])
                                                                 for k in range(KD)])
                        mm.then_inc(tile_done, 1)

            @block.scalar
            def _(act):
                for c in range(LT):
                    for h in range(ML_HEADS):
                        ins = act.activation(hn[:, c, h * DH:(h + 1) * DH], g.hs[:, c, h * DH:(h + 1) * DH], ACT.Square,
                                             accum_out=ss[:, c, h:h + 1])
                ins.then_inc(squared, 1)
                act.wait_ge(var_done, 1)
                act.activation(ss[:], ss[:], ACT.Sqrt).then_inc(root_done, 1)
                for n in range(0, 2 * KD, 2):
                    act.wait_ge(turned, n + 1)
                    act.activation(hn[:, n // 2, 0:BANK], tp[:, n % 4, :], ACT.Copy).then_inc(out_of[0], 1)
                credit(act, sig_done, 2)
                with act.Fori(0, KD) as t:
                    for j in range(2):
                        act.wait_ge(tile_done, 2 * t + j + 3)
                        act.wait_ge(merged, t + 2)
                        act.activation(sig[:, j, :], ps[:, j].rearrange("p c n -> p (c n)"),
                                       ACT.Sigmoid).then_inc(sig_done, 1)

            @block.vector
            def _(dve):
                dve.wait_ge(squared, 1)
                dve.tensor_scalar(ss[:], ss[:], 1.0 / DH, EPS, ALU.mult, ALU.add).then_inc(var_done, 1)
                dve.wait_ge(root_done, 1)
                dve.reciprocal(ss[:], ss[:]).then_inc(inv_done, 1)
                dve.wait_ge(inv_done, 1)
                for c in range(LT):
                    hv = g.hs[:, c, :].rearrange("p (h n) -> p h n", h=ML_HEADS)
                    dve.tensor_tensor(hv, hv, ss[:, c, :].rearrange("p (h o) -> p h o", o=1).to_broadcast(
                        [P, ML_HEADS, DH]), ALU.mult).then_inc(scaled, 1)
                for n in range(1, 2 * KD, 2):
                    dve.wait_ge(turned, n + 1)
                    dve.tensor_copy(hn[:, n // 2, BANK:], tp[:, n % 4, :]).then_inc(out_of[1], 1)
                credit(dve, merged, 2)
                for b in range(2):
                    dve.wait_ge(out_of[b], KD)
                step = Steps(dve, dve_step)
                with dve.Fori(0, KD // 2) as i:
                    step.n, step.base = 0, i * 8
                    for j in range(2):
                        t = 2 * i + j
                        h = hn[:, ds(t, 1), :].rearrange("p o n -> p (o n)")
                        dve.wait_ge(xy_in[j], 32 * (i + 1))
                        step(dve.tensor_scalar(xc[:, j, :], xc[:, j, :], g.pa[:, ds(PA_SKIP + t, 1)], None, ALU.mult))
                        step(dve.scalar_tensor_tensor(h, h, g.pa[:, ds(PA_MLN + t, 1)], xc[:, j, :], ALU.mult, ALU.add))
                        dve.wait_ge(sig_done, 2 * t + 4)
                        step(dve.tensor_tensor(h, h, sig[:, 0, :], ALU.mult))
                        step(dve.tensor_tensor(h, h, sig[:, 1, :], ALU.mult))
                        dve.tensor_tensor(h, h, y[:, j, :], ALU.add).then_inc(merged, 1)
        with nc.Block() as block:
            @block.sync
            def _(sp):
                sp.wait_ge(merged, KD + 2)
                sp.dma_start(g.m_dram.rearrange("t p n -> p t n"), hn[:]).then_inc(stored, 16)
                sp.wait_ge(stored, 16)


def merge(nc, g):
    io = g.io
    with Phase(nc, "mrg") as ph:
        mT = ph.sb("mT", [P, KD, N_LAT])
        w = ph.sb("w", [P, KD, D])
        wr = ph.sb("wr", [P, KD, N_EXP])
        g1, a2, b2, n2 = (ph.sb(n, [P, D]) for n in ("g1", "a2", "b2", "n2"))
        x = ph.sb("x", [P, 2, D])
        h2 = ph.sb("h2", [P, 2, D])
        h2T = ph.sb("h2T", [P, 2, D])
        junk = ph.sb("junk", [P, D])
        st = ph.sb("st", [P, 2, 8])
        pr = ph.sb("pr", [P, 2, N_EXP])
        acc = ph.ps("acc", [P, 2, 2, BANK])
        tp = ph.ps("tp", [P, 2, BANK])
        lg = ph.ps("lg", [P, BANK])
        at = ph.ps("at", [P, BANK])
        loaded, rows_ready = ph.sem("loaded"), ph.sem("rows_ready")
        x_in = [ph.sem(f"x_in{j}") for j in range(2)]
        stored = [ph.sem(f"stored{j}") for j in range(2)]
        multiplied, x1_done, squared, var_done, root_done = (ph.sem(n) for n in (
            "multiplied", "x1_done", "squared", "var_done", "root_done"))
        h2_done, turned, h2t_done, logits, nmax, exped, aff, aff_t, aff_c, dve_step = (ph.sem(n) for n in (
            "h2_done", "turned", "h2t_done", "logits", "nmax", "exped", "aff", "aff_t", "aff_c", "dve_step"))
        with nc.Block() as block:
            @block.sync
            def _(sp):
                sp.dma_start(mT[:], g.m_dram.rearrange("t p n -> p t n")).then_inc(loaded, 16)
                sp.dma_start(w[:], io["w_out"].rearrange("(k p) n -> p k n", p=P)).then_inc(loaded, 16)
                sp.dma_start(wr[:], io["w_router"].rearrange("(k p) n -> p k n", p=P)).then_inc(loaded, 16)
                sp.dma_start(g1[:], spread(g.modrow[0, 2 * D:3 * D])).then_inc(loaded, 16)
                sp.dma_start(b2[:], spread(g.modrow[0, 3 * D:4 * D])).then_inc(loaded, 16)
                sp.dma_start(a2[:], spread(g.modrow[0, 4 * D:5 * D])).then_inc(loaded, 16)
                sp.dma_start(n2[:], spread(io["norm2"])).then_inc(loaded, 16)
                for n in range(LT):
                    if n >= 2:
                        sp.wait_ge(stored[n % 2], 32 * (n // 2))
                    sp.dma_start(x[:, n % 2, :], io["x"][n * P:(n + 1) * P, :]).then_inc(x_in[n % 2], 16)

            @block.gpsimd
            def _(pool):
                for n in range(LT):
                    pool.wait_ge(h2_done, n + 1)
                    pool.dma_start(g.x1[n * P:(n + 1) * P, :], x[:, n % 2, :]).then_inc(stored[n % 2], 16)
                    pool.dma_start(g.h2[n * P:(n + 1) * P, :], h2[:, n % 2, :]).then_inc(stored[n % 2], 16)
                for j in range(2):
                    pool.wait_ge(stored[j], 16 * LT)

            @block.tensor
            def _(pe):
                def multiply(n):
                    if n >= 2:
                        pe.wait_ge(x1_done, n - 1)
                    for c in range(2):
                        mm = accumulate(nc, acc[:, n % 2, c, :], [
                            (mT[:, k, n * P:(n + 1) * P], w[:, k, c * BANK:(c + 1) * BANK]) for k in range(KD)])
                    mm.then_inc(multiplied, 1)

                def route_tile(n):
                    pe.wait_ge(h2_done, n + 1)
                    pe.wait_ge(h2t_done, 2 * n)
                    for b in range(2):
                        for k in range(4):
                            mm = pe.transpose(tp[:, b, k * P:(k + 1) * P],
                                              h2[:, n % 2, (4 * b + k) * P:(4 * b + k + 1) * P], g.ident[:])
                        mm.then_inc(turned, 1)
                    pe.wait_ge(h2t_done, 2 * n + 2)
                    pe.wait_ge(aff, n)
                    accumulate(nc, lg[:, 0:N_EXP], [(h2T[:, n % 2, k * P:(k + 1) * P], wr[:, k, :])
                                                    for k in range(KD)]).then_inc(logits, 1)

                def turn_aff(n):
                    pe.wait_ge(aff, n + 1)
                    pe.wait_ge(aff_c, n)
                    pe.transpose(at[0:N_EXP, 0:P], pr[:, n % 2, :], g.ident[:]).then_inc(aff_t, 1)

                pe.wait_ge(loaded, 16 * 7)
                multiply(0)
                for n in range(LT):
                    if n + 1 < LT:
                        multiply(n + 1)
                    route_tile(n)
                    if n:
                        turn_aff(n - 1)
                turn_aff(LT - 1)

            @block.scalar
            def _(act):
                def probabilities(n):
                    j = n % 2
                    act.wait_ge(nmax, n + 1)
                    act.activation(pr[:, j, :], lg[:, 0:N_EXP], ACT.Exp, bias=st[:, j, 4:5],
                                   accum_out=st[:, j, 5:6]).then_inc(exped, 1)

                for n in range(LT):
                    j = n % 2
                    act.wait_ge(x1_done, n + 1)
                    act.activation(junk[:], x[:, j, :], ACT.Square, accum_out=st[:, j, 0:1]).then_inc(squared, 1)
                    act.wait_ge(var_done, n + 1)
                    act.activation(st[:, j, 2:3], st[:, j, 1:2], ACT.Sqrt).then_inc(root_done, 1)
                    if n:
                        probabilities(n - 1)
                    for b in range(2):
                        act.wait_ge(turned, 2 * n + b + 1)
                        act.activation(h2T[:, j, b * BANK:(b + 1) * BANK], tp[:, b, :], ACT.Copy).then_inc(h2t_done, 1)
                probabilities(LT - 1)

            @block.vector
            def _(dve):
                step = Steps(dve, dve_step)
                dve.wait_ge(loaded, 16 * 7)
                step(dve.scalar_tensor_tensor(a2[:], a2[:], 1.0, n2[:], ALU.add, ALU.mult))

                def softmax(n):
                    j = n % 2
                    if n:
                        copy_aff(n - 1)
                    dve.wait_ge(logits, n + 1)
                    step(dve.tensor_reduce(st[:, j, 6:7], lg[:, 0:N_EXP], AX.X, ALU.max))
                    dve.tensor_scalar(st[:, j, 4:5], st[:, j, 6:7], -1.0, None, ALU.mult).then_inc(nmax, 1)
                    dve.wait_ge(exped, n + 1)
                    step(dve.reciprocal(st[:, j, 7:8], st[:, j, 5:6]))
                    dve.tensor_scalar(pr[:, j, :], pr[:, j, :], st[:, j, 7:8], None, ALU.mult).then_inc(aff, 1)

                def copy_aff(n):
                    dve.wait_ge(aff_t, n + 1)
                    dve.tensor_copy(g.affT[:, n * P:(n + 1) * P], at[0:N_EXP, 0:P]).then_inc(aff_c, 1)

                for n in range(LT):
                    j = n % 2
                    dve.wait_ge(multiplied, n + 1)
                    if n >= 2:
                        dve.wait_ge(stored[j], 32 * (n // 2))
                    step(dve.tensor_tensor(h2[:, j, :], acc[:, j].rearrange("p c n -> p (c n)"), g1[:], ALU.mult))
                    dve.wait_ge(x_in[j], 16 * (n // 2 + 1))
                    dve.tensor_tensor(x[:, j, :], x[:, j, :], h2[:, j, :], ALU.add).then_inc(x1_done, 1)
                    dve.wait_ge(squared, n + 1)
                    dve.tensor_scalar(st[:, j, 1:2], st[:, j, 0:1], 1.0 / D, EPS, ALU.mult, ALU.add).then_inc(var_done, 1)
                    dve.wait_ge(root_done, n + 1)
                    step(dve.reciprocal(st[:, j, 3:4], st[:, j, 2:3]))
                    step(dve.scalar_tensor_tensor(h2[:, j, :], x[:, j, :], st[:, j, 3:4], a2[:], ALU.mult, ALU.mult))
                    dve.tensor_tensor(h2[:, j, :], h2[:, j, :], b2[:], ALU.add).then_inc(h2_done, 1)
                    if n:
                        softmax(n - 1)
                softmax(LT - 1)
                copy_aff(LT - 1)


def expert_weights(sp, g, e, s):
    src = g.io[("w_e_gate", "w_e_up")[s % 2] if s < 4 else "w_e_down"].rearrange("e (k p) n -> e p k n", p=P)
    half = s // 2 if s < 4 else s - 4
    sp.dma_start(g.we[:, s:s + 1], src[ds(e, 1), :, :, half * BANK:(half + 1) * BANK]
                 .rearrange("e p k n -> p e k n")).then_inc(g.we_in[s], 16)


def route(nc, g):
    with Phase(nc, "rte") as ph:
        work = ph.sb("work", [N_EXP, 2, N_LAT])
        val = ph.sb("val", [N_EXP, CAP])
        idx = ph.sb("idx", [N_EXP, CAP], U32)
        idf = ph.sb("idf", [N_EXP, CAP])
        zero = ph.sb("zero", [P, D])
        tp = ph.ps("tp", [P, BANK])
        dve_step, found, turned, cleared, stored = (ph.sem(n) for n in (
            "dve_step", "found", "turned", "cleared", "stored"))
        with nc.Block() as block:
            @block.sync
            def _(sp):
                for s in range(6):
                    expert_weights(sp, g, 0, s)

            @block.gpsimd
            def _(pool):
                pool.memset(zero[:], 0.0).then_inc(cleared, 1)
                pool.wait_ge(cleared, 1)
                for n in range(LT):
                    pool.dma_start(g.moe[n * P:(n + 1) * P, :], zero[:]).then_inc(stored, 16)
                pool.wait_ge(stored, 16 * LT)

            @block.vector
            def _(dve):
                step = Steps(dve, dve_step)
                src = g.affT
                for r in range(CAP // 8):
                    cur = g.affT[:, :] if r == 0 else work[:, (r - 1) % 2, :]
                    a = slice(8 * r, 8 * r + 8)
                    step(dve.max(val[:, a], cur))
                    dve.max_index(idx[:, a], val[:, a], cur)
                    step(dve.match_replace(work[:, r % 2, :], val[:, a], cur, -1.0))
                dve.tensor_copy(idf[:], idx[:]).then_inc(found, 1)
                dve.wait_ge(turned, 1)
                step(dve.tensor_copy(g.gval[:], tp[:, 0:N_EXP]))
                step(dve.tensor_copy(g.gidx[:], tp[:, N_EXP:2 * N_EXP]))

            @block.tensor
            def _(pe):
                pe.wait_ge(found, 1)
                pe.transpose(tp[:, 0:N_EXP], val[:], g.ident[0:N_EXP, 0:N_EXP])
                pe.transpose(tp[:, N_EXP:2 * N_EXP], idf[:], g.ident[0:N_EXP, 0:N_EXP]).then_inc(turned, 1)


def experts(nc, g):
    io = g.io
    with Phase(nc, "exp") as ph:
        w, w_in = g.we, g.we_in
        ix = ph.sb("ix", [P, 2], U32)
        xs = ph.sb("xs", [P, D])
        xsT = ph.sb("xsT", [P, D])
        act_a = ph.sb("act_a", [P, FF])
        hid = ph.sb("hid", [P, FF])
        hidT = ph.sb("hidT", [P, FF])
        y = ph.sb("y", [P, D])
        gu = ph.ps("gu", [P, 4, BANK])
        tp = ph.ps("tp", [P, 2, BANK])
        dn = ph.ps("dn", [P, 2, BANK])
        used = [ph.sem(f"used{s}") for s in range(6)]
        names = ("ix_ready", "gathered", "x_turned", "xt_done", "silu_done", "hid_done", "h_turned", "ht_done",
                 "y_done", "scattered")
        to_ready, may_go, y_free = ph.sem("to_ready"), ph.sem("may_go"), ph.sem("y_free")
        ix_ready, gathered, x_turned, xt_done, silu_done, hid_done, h_turned, ht_done, y_done, scattered = (
            ph.sem(n) for n in names)
        with nc.Block() as block:
            @block.sync
            def _(sp):
                with sp.Fori(0, N_EXP - 1) as e:
                    for s in range(6):
                        sp.wait_ge(used[s], e + 2)
                        expert_weights(sp, g, e + 1, s)

            @block.gpsimd
            def _(pool):
                def gather(e):
                    if not isinstance(e, int):
                        pool.wait_ge(x_turned, 2 * e)
                    if isinstance(e, int):
                        pool.tensor_copy(ix[:, 0:1], g.gidx[:, e:e + 1]).then_inc(ix_ready, 1)
                    else:
                        pool.tensor_copy(ix[:, 0:1], g.gidx[:, ds(e, 1)]).then_inc(ix_ready, 1)
                    pool.wait_ge(ix_ready, e + 1)
                    pool.sem_inc(may_go, 1)
                    pool.indirect_dma_start(xs[:], None, g.h2, bass.IndirectOffsetOnAxis(ix[:, 0:1], 0)
                                            ).then_inc(gathered, 16)

                def scatter(e):
                    pool.tensor_copy(ix[:, 1:2], g.gidx[:, ds(e, 1)] if not isinstance(e, int) else g.gidx[:, e:e + 1]
                                     ).then_inc(to_ready, 1)
                    pool.wait_ge(to_ready, e + 1)
                    pool.wait_ge(y_done, e + 2)
                    pool.sem_inc(may_go, 1)
                    pool.indirect_dma_start(g.moe, bass.IndirectOffsetOnAxis(ix[:, 1:2], 0), y[:], None,
                                            compute_op=ALU.add).then_inc(scattered, 16)
                    pool.wait_ge(scattered, 16 * (e + 1))
                    pool.sem_inc(y_free, 1)

                pool.sem_inc(y_free, 1)
                gather(0)
                with pool.Fori(0, N_EXP - 1) as e:
                    gather(e + 1)
                    scatter(e)
                scatter(N_EXP - 1)

            @block.tensor
            def _(pe):
                for s in range(6):
                    credit(pe, used[s], 1)

                def turn_x(e):
                    pe.wait_ge(gathered, 16 * (e + 1))
                    for b in range(2):
                        for k in range(4):
                            mm = pe.transpose(tp[:, b, k * P:(k + 1) * P], xs[:, (4 * b + k) * P:(4 * b + k + 1) * P],
                                              g.ident[:])
                        mm.then_inc(x_turned, 1)

                def one(e, more):
                    pe.wait_ge(xt_done, 2 * e + 2)
                    pe.wait_ge(hid_done, 2 * e + 1)
                    for s in range(4):
                        pe.wait_ge(w_in[s], 16 * (e + 1))
                        accumulate(nc, gu[:, s, :], [(xsT[:, k * P:(k + 1) * P], w[:, s, k, :])
                                                     for k in range(KD)]).then_inc(used[s], 1)
                    pe.wait_ge(hid_done, 2 * e + 3)
                    for b in range(2):
                        for k in range(4):
                            mm = pe.transpose(tp[:, b, k * P:(k + 1) * P], hid[:, (4 * b + k) * P:(4 * b + k + 1) * P],
                                              g.ident[:])
                        mm.then_inc(h_turned, 1)
                    pe.wait_ge(ht_done, 2 * e + 2)
                    if more:
                        turn_x(e + 1)
                    pe.wait_ge(y_done, e + 1)
                    for b in range(2):
                        s = 4 + b
                        pe.wait_ge(w_in[s], 16 * (e + 1))
                        accumulate(nc, dn[:, b, :], [(hidT[:, k * P:(k + 1) * P], w[:, s, k, :])
                                                     for k in range(FT)]).then_inc(used[s], 1)

                turn_x(0)
                with pe.Fori(0, N_EXP - 1) as e:
                    one(e, True)
                one(N_EXP - 1, False)

            @block.scalar
            def _(act):
                def copy_x(e):
                    for b in range(2):
                        act.wait_ge(x_turned, 2 * e + b + 1)
                        act.activation(xsT[:, b * BANK:(b + 1) * BANK], tp[:, b, :], ACT.Copy).then_inc(xt_done, 1)

                def one(e, more):
                    for half in range(2):
                        act.wait_ge(used[2 * half], e + 2)
                        act.activation(act_a[:, half * BANK:(half + 1) * BANK], gu[:, 2 * half, :],
                                       ACT.Silu).then_inc(silu_done, 1)
                    for b in range(2):
                        act.wait_ge(h_turned, 2 * e + b + 1)
                        act.activation(hidT[:, b * BANK:(b + 1) * BANK], tp[:, b, :], ACT.Copy).then_inc(ht_done, 1)
                    if more:
                        copy_x(e + 1)

                copy_x(0)
                with act.Fori(0, N_EXP - 1) as e:
                    one(e, True)
                one(N_EXP - 1, False)

            @block.vector
            def _(dve):
                dve.sem_inc(hid_done, 1)
                dve.sem_inc(y_done, 1)
                with dve.Fori(0, N_EXP) as e:
                    for half in range(2):
                        dve.wait_ge(silu_done, 2 * e + half + 1)
                        dve.wait_ge(used[2 * half + 1], e + 2)
                        dve.tensor_tensor(hid[:, half * BANK:(half + 1) * BANK], act_a[:, half * BANK:(half + 1) * BANK],
                                          gu[:, 2 * half + 1, :], ALU.mult).then_inc(hid_done, 1)
                    dve.wait_ge(used[5], e + 2)
                    dve.wait_ge(y_free, e + 1)
                    dve.tensor_scalar(y[:], dn[:].rearrange("p b n -> p (b n)"), g.gval[:, ds(e, 1)], None,
                                      ALU.mult).then_inc(y_done, 1)


def moe_out(nc, g):
    io = g.io
    with Phase(nc, "fin") as ph:
        g2, fn = ph.sb("g2", [P, D]), ph.sb("fn", [P, D])
        x = ph.sb("x", [P, LT, D])
        y = ph.sb("y", [P, LT, D])
        junk = ph.sb("junk", [P, 2, D])
        st = ph.sb("st", [P, LT, 4])
        loaded = ph.sem("loaded")
        x_in = [ph.sem(f"x_in{n}") for n in range(LT)]
        names = ("x2_done", "squared", "var_done", "root_done", "out_done", "dve_step", "stored")
        x2_done, squared, var_done, root_done, out_done, dve_step, stored = (ph.sem(n) for n in names)
        with nc.Block() as block:
            @block.sync
            def _(sp):
                sp.dma_start(g2[:], spread(g.modrow[0, 5 * D:6 * D])).then_inc(loaded, 16)
                for n in range(LT):
                    sp.dma_start(x[:, n, :], g.x1[n * P:(n + 1) * P, :]).then_inc(x_in[n], 16)
                    sp.dma_start(y[:, n, :], g.moe[n * P:(n + 1) * P, :]).then_inc(x_in[n], 16)
                    if n == 0:
                        sp.dma_start(fn[:], spread(io["final_norm"])).then_inc(loaded, 16)
                for n in range(LT):
                    sp.wait_ge(out_done, n + 1)
                    sp.dma_start(g.xa[n * P:(n + 1) * P, :], y[:, n, :]).then_inc(stored, 16)
                sp.wait_ge(stored, 16 * LT)

            @block.scalar
            def _(act):
                for n in range(LT):
                    act.wait_ge(x2_done, n + 1)
                    if n >= 2:
                        act.wait_ge(squared, n - 1)
                    act.activation(junk[:, n % 2], x[:, n, :], ACT.Square, accum_out=st[:, n, 0:1]).then_inc(squared, 1)
                    act.wait_ge(var_done, n + 1)
                    act.activation(st[:, n, 2:3], st[:, n, 1:2], ACT.Sqrt).then_inc(root_done, 1)

            @block.vector
            def _(dve):
                step = Steps(dve, dve_step)
                dve.wait_ge(loaded, 32)

                dve.wait_ge(x_in[0], 32)
                step(dve.tensor_tensor(y[:, 0, :], y[:, 0, :], g2[:], ALU.mult))
                dve.tensor_tensor(x[:, 0, :], x[:, 0, :], y[:, 0, :], ALU.add).then_inc(x2_done, 1)
                for n in range(LT):
                    if n + 1 < LT:
                        dve.wait_ge(x_in[n + 1], 32)
                        step(dve.tensor_tensor(y[:, n + 1, :], y[:, n + 1, :], g2[:], ALU.mult))
                    dve.wait_ge(squared, n + 1)
                    dve.tensor_scalar(st[:, n, 1:2], st[:, n, 0:1], 1.0 / D, EPS, ALU.mult, ALU.add).then_inc(var_done, 1)
                    if n + 1 < LT:
                        dve.tensor_tensor(x[:, n + 1, :], x[:, n + 1, :], y[:, n + 1, :], ALU.add).then_inc(x2_done, 1)
                    dve.wait_ge(root_done, n + 1)
                    step(dve.reciprocal(st[:, n, 3:4], st[:, n, 2:3]))
                    dve.scalar_tensor_tensor(y[:, n, :], x[:, n, :], st[:, n, 3:4], fn[:], ALU.mult,
                                             ALU.mult).then_inc(out_done, 1)


def over_tiles(eng, segs, body):
    base = 0
    for col, pairs, chunks in segs:
        for j in range(2):
            body(base + j, j, chunks, col + j * P)
        if pairs > 1:
            with eng.Fori(0, pairs - 1) as i:
                for j in range(2):
                    t = 2 * i + 2 + j
                    body(base + t, j, chunks, col + t * P)
        base += 2 * pairs


def parts_of(nc, g, l, last):
    io = g.io
    KH = KD // 2
    with Phase(nc, f"pr{l}") as ph:
        raw = ph.sb("raw", [P, 2, KH, P])
        wh, wl = ph.sb("wh", [P, 2, KH, P], FR), ph.sb("wl", [P, 2, KH, P], FR)
        ps = ph.ps("ps", [P, 2, 3, BANK])
        w_in = [ph.sem(f"w_in{h}") for h in range(2)]
        high, low, used, read_out = (ph.sem(n) for n in ("high", "low", "used", "read_out"))
        segs = [(0, 1, LAT_CHUNKS), (2 * P, 1, ALL_CHUNKS), (4 * P, 9, LAT_CHUNKS)] if last else [(0, 11, ALL_CHUNKS)]
        with nc.Block() as block:
            @block.sync
            def _(sp):
                view = io["w_in_2"][l].rearrange("(h k p) n -> h p k n", p=P, h=2)

                def load(t, j, chunks, col):
                    for h in range(2):
                        wait_count(sp, low, 2 * t + h - 1)
                        sp.dma_start(raw[:, h], view[h][:, :, ds(col, P)]).then_inc(w_in[h], 16)
                over_tiles(sp, segs, load)

            @block.tensor
            def _(pe):
                def multiply(t, j, chunks, col):
                    wait_count(pe, read_out, t - 1)
                    for h in range(2):
                        pe.wait_ge(low, 2 * t + h + 1)
                        for c, (c0, cn) in enumerate(chunks):
                            cols = slice(c0, c0 + cn)
                            for k in range(KH):
                                hi, lo = g.hT[:, h * KH + k, cols], g.hT_low[:, h * KH + k, cols]
                                out = ps[:, j, c, 0:cn]
                                nc.tensor.matmul(out, wh[:, h, k, :], hi, start=h == 0 and k == 0, stop=False)
                                nc.tensor.matmul(out, wh[:, h, k, :], lo, start=False, stop=False)
                                mm = nc.tensor.matmul(out, wl[:, h, k, :], hi, start=False,
                                                      stop=h == 1 and k == KH - 1)
                        mm.then_inc(used, 1)
                over_tiles(pe, segs, multiply)

            @block.scalar
            def _(act):
                prev = []

                def read(t, j, chunks):
                    if len(chunks) == 3:
                        act.activation(g.parts[:, ds(t, 1), 0:N_CTX].rearrange("p o n -> p (o n)"),
                                       ps[:, j, 2, 0:N_CTX], ACT.Copy)
                    act.activation(g.parts[:, ds(t, 1), N_CTX:].rearrange("p o n -> p (o n)"),
                                   ps[:, j, 0:2, :].rearrange("p c n -> p (c n)"), ACT.Copy).then_inc(read_out, 1)

                def step(t, j, chunks, col):
                    for h in range(2):
                        act.wait_ge(w_in[h], 16 * (t + 1))
                        wait_count(act, used, 2 * t + h - 1)
                        act.activation(wh[:, h], raw[:, h], ACT.Copy).then_inc(high, 1)
                    if prev:
                        read(t - 1, 1 - j, prev[0])
                    prev[:] = [chunks]
                over_tiles(act, segs, step)
                tiles = sum(2 * n for _, n, _ in segs)
                act.wait_ge(used, 2 * tiles)
                read(tiles - 1, 1, prev[0])

            @block.vector
            def _(dve):
                def step(t, j, chunks, col):
                    for h in range(2):
                        dve.wait_ge(high, 2 * t + h + 1)
                        dve.tensor_tensor(wl[:, h], raw[:, h], wh[:, h].bitcast(F32), ALU.subtract).then_inc(low, 1)
                over_tiles(dve, segs, step)


def queries_keys(nc, g, l, last):
    io = g.io
    with Phase(nc, f"qk{l}") as ph:
        sq = ph.sb("sq", [P, 3, N_ALL])
        rs = ph.sb("rs", [P, 3, N_ALL])
        cos, sin = ph.sb("cos", [P, N_LAT]), ph.sb("sin", [P, N_LAT])
        ps = ph.ps("ps", [P, 2, BANK])
        cs_in, squared, root_done, normed, summed = (ph.sem(n) for n in ("cs_in", "squared", "root_done", "normed", "summed"))
        full = [ph.sem(f"full{b}") for b in range(2)]
        free = [ph.sem(f"free{b}") for b in range(2)]
        dve_step = ph.sem("dve_step")
        jobs = [(t, c) for t in (T_Q, T_Q + 1, T_K) for c in (ALL_CHUNKS if t == T_K or not last else LAT_CHUNKS)]
        turns = [(t, c) for t in (T_Q, T_Q + 1, T_K) for c in LAT_CHUNKS]
        lo = [N_CTX if last else 0, N_CTX if last else 0, 0]
        with nc.Block() as block:
            @block.sync
            def _(sp):
                sp.dma_start(cos[:], io["t_cos"]).then_inc(cs_in, 16)
                sp.dma_start(sin[:], io["t_sin"]).then_inc(cs_in, 16)

            @block.scalar
            def _(act):
                for t in range(3):
                    act.activation(sq[:, t, lo[t]:], g.parts[:, t, lo[t]:], ACT.Square).then_inc(squared, 1)
                for b in range(2):
                    act.wait_ge(free[b], (len(jobs) + 1 - b) // 2)
                for t in range(3):
                    act.activation(rs[:, t, lo[t]:], rs[:, t, lo[t]:], ACT.Sqrt).then_inc(root_done, 1)

            @block.tensor
            def _(pe):
                for n, (t, (c0, cn)) in enumerate(jobs):
                    pe.wait_ge(squared, t + 1)
                    if n >= 2:
                        pe.wait_ge(free[n % 2], n // 2)
                    accumulate(nc, ps[:, n % 2, 0:cn], [(g.block64[:], sq[:, t, c0:c0 + cn])]).then_inc(full[n % 2], 1)
                for n, (t, (c0, cn)) in enumerate(turns, len(jobs)):
                    pe.wait_ge(normed, t + 1)
                    pe.wait_ge(free[n % 2], n // 2)
                    accumulate(nc, ps[:, n % 2, 0:cn], [(g.rot[:], g.parts[:, t, c0:c0 + cn])]).then_inc(full[n % 2], 1)

            @block.vector
            def _(dve):
                step = Steps(dve, dve_step)
                for n, (t, (c0, cn)) in enumerate(jobs):
                    dve.wait_ge(full[n % 2], n // 2 + 1)
                    dve.tensor_scalar(rs[:, t, c0:c0 + cn], ps[:, n % 2, 0:cn], 1.0 / HD, EPS, ALU.mult,
                                      ALU.add).then_inc(free[n % 2], 1)
                for t in range(3):
                    gain = g.pb[:, (PB_QG if t < 2 else PB_KG) + l:(PB_QG if t < 2 else PB_KG) + l + 1]
                    dve.wait_ge(root_done, t + 1)
                    step(dve.reciprocal(rs[:, t, lo[t]:], rs[:, t, lo[t]:]))
                    dve.scalar_tensor_tensor(g.parts[:, t, lo[t]:], g.parts[:, t, lo[t]:], gain, rs[:, t, lo[t]:],
                                             ALU.mult, ALU.mult).then_inc(normed, 1)
                dve.wait_ge(cs_in, 32)
                for n, (t, (c0, cn)) in enumerate(turns, len(jobs)):
                    a = c0 - N_CTX
                    dve.wait_ge(full[n % 2], n // 2 + 1)
                    dve.tensor_tensor(sq[:, t, c0:c0 + cn], ps[:, n % 2, 0:cn], sin[:, a:a + cn],
                                      ALU.mult).then_inc(free[n % 2], 1)
                    step(dve.tensor_tensor(rs[:, t, c0:c0 + cn], g.parts[:, t, c0:c0 + cn], cos[:, a:a + cn], ALU.mult))
                    dve.wait_ge(free[n % 2], n // 2 + 1)
                    step(dve.tensor_tensor(g.parts[:, t, c0:c0 + cn], rs[:, t, c0:c0 + cn], sq[:, t, c0:c0 + cn], ALU.add))


def attention_2(nc, g, l, last):
    with Phase(nc, f"at{l}") as ph:
        raw = ph.sb("raw", [P, N_ALL])
        kh, klo = ph.sb("kh", [P, N_ALL], FR), ph.sb("klo", [HD, N_ALL], FR)
        q = ph.sb("q", [P, 2, N_ALL], FR)
        v = ph.sb("v", [P, NT, P])
        p = ph.sb("p", [P, 2, N_ALL])
        pT = ph.sb("pT", [P, 2, NT, P])
        st = ph.sb("st", [P, 2, 4])
        sc = ph.ps("sc", [P, 2, 3, BANK])
        tb = ph.ps("tb", [P, 2, BANK])
        full = [ph.sem(f"full{b}") for b in range(2)]
        free = [ph.sem(f"free{b}") for b in range(2)]
        names = ("scored", "maxed", "bias_ready", "exped", "inv_ready", "p_ready", "raw_in", "high", "low", "z_done",
                 "y_done")
        scored, maxed, bias_ready, exped, inv_ready, p_ready, raw_in, high, low, z_done, y_done = (
            ph.sem(n) for n in names)
        items = []
        for h in range(H2):
            items += [(h, N_CTX + t * P, N_ALL) for t in range(LT)]
            if not last:
                items += [(h, t * P, N_CTX) for t in range(CT)]
        per_head = len(items) // H2
        groups = lambda keys: [(a, min(4, keys // P - a)) for a in range(0, keys // P, 4)]
        V_USES = 3
        first_use = [V_USES + sum(len(groups(k)) for _, _, k in items[:n]) for n in range(len(items) + 1)]
        lo = N_CTX if last else 0
        loads = [("k", 0), ("q", 0), ("q", 1), ("q", 2), ("k", 1), ("q", 3)]
        need = (2, 3, 5, 6)
        splits_at = {2: [2], per_head + 2: [3], 2 * per_head - 2: [4], 2 * per_head + 2: [5]}

        def half(h):
            return slice((h % 2) * HD, (h % 2) * HD + HD)

        with nc.Block() as block:
            @block.sync
            def _(sp):
                for i, (what, h) in enumerate(loads):
                    if i:
                        sp.wait_ge(low, i)
                    for side in range(2):
                        src = g.parts[h * HD:(h + 1) * HD, T_K, :] if what == "k" else \
                            g.parts[half(h), T_Q + h // 2, lo:]
                        sp.dma_start(raw[side * HD:(side + 1) * HD, 0 if what == "k" else lo:], src).then_inc(raw_in, 16)

            @block.tensor
            def _(pe):
                def turn(n, srcs, more=None):
                    b = n % 2
                    if n >= 2:
                        pe.wait_ge(free[b], n // 2)
                    for k, src in enumerate(srcs):
                        mm = pe.transpose(tb[:, b, k * P:(k + 1) * P], src, g.ident[:])
                    if more is not None:
                        mm = output(b, more)
                    mm.then_inc(full[b], 1)

                def output(b, n):
                    h, _, keys = items[n]
                    return accumulate(nc, tb[half(h), b, 2 * P:3 * P], [
                        (v[:, k, (h // 2) * HD:(h // 2 + 1) * HD], pT[:, n % 2, k, :]) for k in range(keys // P)])

                def scores(n):
                    h, q0, keys = items[n]
                    if n % per_head == 0:
                        pe.wait_ge(low, need[h])
                    if n >= 2:
                        pe.wait_ge(exped, n - 1)
                    for c0 in range(0, keys, BANK):
                        cols = slice(c0, min(c0 + BANK, keys))
                        mm = accumulate(nc, sc[:, n % 2, c0 // BANK, 0:cols.stop - c0], [
                            (q[:, h % 2, q0:q0 + P], kh[:, cols]), (q[0:HD, h % 2, q0:q0 + P], klo[:, cols])])
                    mm.then_inc(scored, 1)

                for c, (t0, tn) in enumerate(groups(N_ALL)):
                    turn(c, [g.parts[:, T_V, (t0 + k) * P:(t0 + k + 1) * P] for k in range(tn)])
                scores(0)
                scores(1)
                for n, (h, q0, keys) in enumerate(items):
                    if n + 2 < len(items):
                        scores(n + 2)
                    pe.wait_ge(p_ready, n + 1)
                    gs = groups(keys)
                    for c, (t0, tn) in enumerate(gs):
                        more = n - 1 if c == len(gs) - 1 and n else None
                        if more is not None:
                            m = first_use[n] - 1
                            pe.wait_ge(free[m % 2], m // 2 + 1)
                            if first_use[n] - first_use[n - 1] > 1:
                                pe.wait_ge(free[1 - m % 2], (m - 1) // 2 + 1)
                        turn(first_use[n] + c, [p[:, n % 2, (t0 + k) * P:(t0 + k + 1) * P] for k in range(tn)], more)
                end = first_use[-1]
                for m in (end - 1, end - 2):
                    pe.wait_ge(free[m % 2], m // 2 + 1)
                output(end % 2, len(items) - 1).then_inc(full[end % 2], 1)

            @block.scalar
            def _(act):
                def exp(n):
                    keys = items[n][2]
                    act.wait_ge(bias_ready, n + 1)
                    act.activation(p[:, n % 2, 0:keys], sc[:, n % 2].rearrange("p b n -> p (b n)")[:, 0:keys], ACT.Exp,
                                   bias=st[:, n % 2, 1:2], scale=ATT2_SCALE,
                                   accum_out=st[:, n % 2, 2:3]).then_inc(exped, 1)

                def split_high(i):
                    what, h = loads[i]
                    act.wait_ge(raw_in, 32 * (i + 1))
                    if i == 4:
                        act.wait_ge(scored, 2 * per_head)
                    elif h >= 2:
                        act.wait_ge(scored, (h - 1) * per_head)
                    if what == "k":
                        act.activation(kh[:], raw[:], ACT.Copy).then_inc(high, 1)
                    else:
                        act.activation(q[:, h % 2, lo:], raw[:, lo:], ACT.Copy).then_inc(high, 1)

                def copy_output(b, n):
                    h, q0, _ = items[n]
                    return act.activation(g.hT[half(h), 2 + h // 2, q0:q0 + P], tb[half(h), b, 2 * P:3 * P], ACT.Copy)

                def copy_turned(m, dst, w, output_of=None):
                    act.wait_ge(full[m % 2], m // 2 + 1)
                    ins = act.activation(dst, tb[:, m % 2, 0:w], ACT.Copy)
                    if output_of is not None:
                        ins = copy_output(m % 2, output_of)
                    ins.then_inc(free[m % 2], 1)

                split_high(0)
                split_high(1)
                for c, (t0, tn) in enumerate(groups(N_ALL)):
                    copy_turned(c, v[:, t0:t0 + tn, :].rearrange("p t d -> p (t d)"), tn * P)
                exp(0)
                for n in range(len(items)):
                    for i in splits_at.get(n, ()):
                        split_high(i)
                    if n + 1 < len(items):
                        exp(n + 1)
                    gs = groups(items[n][2])
                    for c, (t0, tn) in enumerate(gs):
                        copy_turned(first_use[n] + c, pT[:, n % 2, t0:t0 + tn, :].rearrange("p t d -> p (t d)"), tn * P,
                                    n - 1 if c == len(gs) - 1 and n else None)
                end = first_use[-1]
                act.wait_ge(full[end % 2], end // 2 + 1)
                copy_output(end % 2, len(items) - 1).then_inc(y_done, 1)
                for t in (T_ZA, T_ZA + 1):
                    act.activation(g.parts[:, t, lo:], g.parts[:, t, lo:], ACT.Silu).then_inc(z_done, 1)

            @block.vector
            def _(dve):
                def split_low(i):
                    what, h = loads[i]
                    dve.wait_ge(high, i + 1)
                    if what == "k":
                        dve.tensor_tensor(klo[:], raw[0:HD, :], kh[0:HD, :].bitcast(F32), ALU.subtract).then_inc(low, 1)
                    else:
                        dve.tensor_tensor(q[HD:, h % 2, lo:], raw[HD:, lo:], q[HD:, h % 2, lo:].bitcast(F32),
                                          ALU.subtract).then_inc(low, 1)

                def maximum(n):
                    keys = items[n][2]
                    dve.wait_ge(scored, n + 1)
                    dve.tensor_reduce(st[:, n % 2, 0:1], sc[:, n % 2].rearrange("p b n -> p (b n)")[:, 0:keys],
                                      AX.X, ALU.max).then_inc(maxed, 1)
                    dve.wait_ge(maxed, n + 1)
                    dve.tensor_scalar(st[:, n % 2, 1:2], st[:, n % 2, 0:1], -ATT2_SCALE, None,
                                      ALU.mult).then_inc(bias_ready, 1)

                split_low(0)
                split_low(1)
                maximum(0)
                for n, (h, q0, keys) in enumerate(items):
                    for i in splits_at.get(n, ()):
                        split_low(i)
                    if n + 1 < len(items):
                        maximum(n + 1)
                    dve.wait_ge(exped, n + 1)
                    dve.reciprocal(st[:, n % 2, 3:4], st[:, n % 2, 2:3]).then_inc(inv_ready, 1)
                    dve.wait_ge(inv_ready, n + 1)
                    dve.tensor_scalar(p[:, n % 2, 0:keys], p[:, n % 2, 0:keys], st[:, n % 2, 3:4], None,
                                      ALU.mult).then_inc(p_ready, 1)
                dve.wait_ge(y_done, 1)
                for t in range(2):
                    dve.wait_ge(z_done, t + 1)
                    dve.tensor_tensor(g.hT[:, 2 + t, lo:], g.hT[:, 2 + t, lo:], g.parts[:, T_ZA + t, lo:], ALU.mult)


def fourier(nc, g, l, name):
    io = g.io
    c0, n_tok = (0, N_CTX) if name == "ctx" else (N_CTX, N_LAT)
    nt, width = n_tok // P, min(n_tok, BANK)
    halves = n_tok // width
    with Phase(nc, f"f{name}{l}") as ph:
        u = ph.sb("u", [P, nt, 2 * P])
        dft = ph.sb("dft", [P, 2, 2, n_tok])
        small = ph.sb("small", [P, 2, P])
        wf = ph.sb("wf", [P, 2, 2 * P])
        w2 = ph.sb("w2", [P, 2, 2, 2 * P])
        ab = ph.sb("ab", [P, 2, 2, n_tok])
        bank = ph.ps("bank", [P, 2, 2, 2, BANK])
        flat = bank[:].rearrange("p f s h n -> p (f s h) n")
        loaded, u_full, u_free, w_full, w_free = (ph.sem(n) for n in ("loaded", "u_full", "u_free", "w_full", "w_free"))
        d_in = [ph.sem(f"d_in{j}") for j in range(2)]
        d_used, copied, out_full, out_read, z_done = (ph.sem(n) for n in ("d_used", "copied", "out_full", "out_read",
                                                                          "z_done"))
        with nc.Block() as block:
            @block.sync
            def _(sp):
                sp.dma_start(small[:], io["t_dftd_" + name].rearrange("s p n -> p s n")).then_inc(loaded, 16)
                sp.dma_start(wf[:], io["w_fourier_2"][l].rearrange("(k p) n -> p k n", p=P)).then_inc(loaded, 16)
                for t in range(nt):
                    if t >= 2:
                        sp.wait_ge(d_used, t - 1)
                    sp.dma_start(dft[:, t % 2], io["t_dft_" + name][:, t * P:(t + 1) * P, :].rearrange("s p n -> p s n")
                                 ).then_inc(d_in[t % 2], 16)

            @block.tensor
            def _(pe):
                for t in range(0, nt, 2):
                    b = (t // 2) % 2
                    if t >= 4:
                        pe.wait_ge(u_free, t // 2 - 1)
                    for k in range(4):
                        a, f = divmod(k, 2)
                        mm = pe.transpose(flat[:, b, k * P:(k + 1) * P],
                                          g.parts[:, T_UF + f, c0 + (t + a) * P:c0 + (t + a + 1) * P], g.ident[:])
                    mm.then_inc(u_full, 1)
                pe.wait_ge(loaded, 32)
                for s in range(2):
                    for k in range(2):
                        mm = accumulate(nc, flat[:, 2 + s, k * 2 * P:(k + 1) * 2 * P], [(small[:, s, :], wf[:, k, :])])
                mm.then_inc(w_full, 1)
                pe.wait_ge(u_free, nt // 2)
                pe.wait_ge(w_free, 1)
                for t in range(nt):
                    pe.wait_ge(d_in[t % 2], 16 * (t // 2 + 1))
                    for f in range(2):
                        for s in range(2):
                            for h in range(halves):
                                mm = nc.tensor.matmul(bank[:, f, s, h, 0:width], u[:, t, f * P:(f + 1) * P],
                                                      dft[:, t % 2, s, h * width:(h + 1) * width],
                                                      start=t == 0, stop=t == nt - 1)
                    mm.then_inc(d_used, 1)
                pe.wait_ge(copied, 4)
                for j in range(2):
                    for h in range(halves):
                        accumulate(nc, bank[:, j, 0, h, 0:width], [
                            (w2[:, s, f, j * P:(j + 1) * P], ab[:, f, s, h * width:(h + 1) * width])
                            for s in range(2) for f in range(2)]).then_inc(out_full, 1)

            @block.scalar
            def _(act):
                for t in (T_ZF, T_ZF + 1):
                    act.activation(g.parts[:, t, c0:c0 + n_tok], g.parts[:, t, c0:c0 + n_tok], ACT.Silu).then_inc(z_done, 1)

            @block.vector
            def _(dve):
                for t in range(0, nt, 2):
                    dve.wait_ge(u_full, t // 2 + 1)
                    dve.tensor_copy(u[:, t:t + 2, :].rearrange("p t n -> p (t n)"),
                                    flat[:, (t // 2) % 2, :]).then_inc(u_free, 1)
                dve.wait_ge(w_full, 1)
                dve.tensor_copy(w2[:].rearrange("p s k n -> p s (k n)"), flat[:, 2:4, :]).then_inc(w_free, 1)
                dve.wait_ge(d_used, nt)
                for f in range(2):
                    for s in range(2):
                        dve.tensor_copy(ab[:, f, s, :].rearrange("p (h n) -> p h n", h=halves),
                                        bank[:, f, s, 0:halves, 0:width]).then_inc(copied, 1)
                dve.wait_ge(z_done, 2)
                for j in range(2):
                    for h in range(halves):
                        a = c0 + h * width
                        dve.wait_ge(out_full, j * halves + h + 1)
                        dve.tensor_tensor(g.hT[:, j, a:a + width], bank[:, j, 0, h, 0:width],
                                          g.parts[:, T_ZF + j, a:a + width], ALU.mult).then_inc(out_read, 1)


def conv_pool(nc, g, l, streams):
    io = g.io
    CP, PP = 1, 8
    with Phase(nc, f"cp{l}") as ph:
        tc = ph.sb("tc", [P, N_ALL + 3 * CP])
        yc = ph.sb("yc", [P, N_ALL])
        up = ph.sb("up", [P, N_ALL + 3 * PP])
        s = [ph.sb(f"s{i}", [P, N_ALL + 3 * PP]) for i in range(2)]
        dd = ph.sb("dd", [P, 2, N_ALL])
        rc = ph.sb("rc", [P, 2, N_ALL])
        pw = ph.sb("pw", [P, 2, P])
        ps = ph.ps("ps", [P, 2, BANK])
        zeroed, loaded, z_done, d_done, y_done, up_ready = (ph.sem(n) for n in (
            "zeroed", "loaded", "z_done", "d_done", "y_done", "up_ready"))
        full, dve_step, pool_step, up_used = ph.sem("full"), ph.sem("dve_step"), ph.sem("pool_step"), ph.sem("up_used")
        at_c = {0: CP, N_CTX: 2 * CP + N_CTX}
        at_p = {0: PP, N_CTX: 2 * PP + N_CTX}
        lo = streams[0][1]
        width = N_ALL + 3 * PP
        chunks = [c for c in ALL_CHUNKS if c[0] >= lo]
        jobs = [(j, c) for j in range(2) for c in chunks]
        with nc.Block() as block:
            @block.sync
            def _(sp):
                for name, c0, n in streams:
                    sp.dma_start(rc[:, :, c0:c0 + n], io["t_rcnt_" + name].rearrange("j p n -> p j n")).then_inc(loaded, 16)
                sp.wait_ge(zeroed, 3)
                for j in range(2):
                    for h in range(2):
                        sp.dma_start(pw[h * HD:(h + 1) * HD, j, h * HD:(h + 1) * HD],
                                     io["pool_w_2"][l, 2 * j + h]).then_inc(loaded, 16)
                sp.dma_start(g.wo, io["w_out_2"][l].rearrange("(k p) n -> p k n", p=P)).then_inc(g.wo_in, 16)

            @block.gpsimd
            def _(pool):
                pool.memset(tc[:], 0.0).then_inc(zeroed, 1)
                pool.memset(up[:], 0.0).then_inc(zeroed, 1)
                pool.memset(pw[:], 0.0).then_inc(zeroed, 1)

            @block.scalar
            def _(act):
                for t in (T_ZC, T_ZC + 1, T_ZP, T_ZP + 1):
                    act.activation(g.parts[:, t, lo:], g.parts[:, t, lo:], ACT.Silu).then_inc(z_done, 1)
                act.wait_ge(zeroed, 3)
                for j in range(2):
                    act.wait_ge(up_used, j)
                    for _, c0, n in streams:
                        ins = act.activation(up[:, at_p[c0]:at_p[c0] + n], g.parts[:, T_UP + j, c0:c0 + n], ACT.Copy)
                    ins.then_inc(up_ready, 1)

            @block.vector
            def _(dve):
                step = Steps(dve, dve_step)
                dve.wait_ge(loaded, 16 * (len(streams) + 4))
                for j in range(2):
                    dve.wait_ge(up_ready, j + 1)
                    src, w = up, 1
                    for q in range(2 * j + 2):
                        dst = s[q % 2]
                        ins = dve.tensor_tensor(dst[:, 0:width - 2 * w + 1], src[:, 0:width - 2 * w + 1],
                                                src[:, w:width - w + 1], ALU.add)
                        if q == 0:
                            ins.then_inc(up_used, 1)
                            dve.wait_ge(up_used, j + 1)
                        else:
                            step(ins)
                        src, w = dst, 2 * w
                        h = q - 2 * j
                        if h >= 0:
                            r = slice(h * HD, (h + 1) * HD)
                            for _, c0, n in streams:
                                a = at_p[c0] - w // 2
                                step(dve.tensor_tensor(dd[r, j, c0:c0 + n], src[r, a:a + n], rc[r, j, c0:c0 + n], ALU.mult))
                    dve.tensor_tensor(dd[:, j, lo:], dd[:, j, lo:], g.parts[:, T_UP + j, lo:],
                                      ALU.subtract).then_inc(d_done, 1)
                dve.wait_ge(z_done, 4)
                for j in range(2):
                    taps = [g.pb[:, PB_CW + l * 6 + tap * 2 + j:PB_CW + l * 6 + tap * 2 + j + 1] for tap in range(3)]
                    bias = g.pb[:, PB_CB + l * 2 + j:PB_CB + l * 2 + j + 1]
                    for _, c0, n in streams:
                        a = at_c[c0]
                        step(dve.tensor_tensor(tc[:, a:a + n], g.parts[:, T_C + j, c0:c0 + n], g.parts[:, T_H + j, c0:c0 + n],
                                               ALU.mult))
                    for _, c0, n in streams:
                        a = at_c[c0] - 1
                        step(dve.tensor_scalar(yc[:, c0:c0 + n], tc[:, a:a + n], taps[0], bias, ALU.mult, ALU.add))
                        for tap in (1, 2):
                            step(dve.scalar_tensor_tensor(yc[:, c0:c0 + n], tc[:, a + tap:a + tap + n], taps[tap],
                                                          yc[:, c0:c0 + n], ALU.mult, ALU.add))
                    step(dve.tensor_tensor(yc[:, lo:], yc[:, lo:], g.parts[:, T_B + j, lo:], ALU.mult))
                    step(dve.tensor_tensor(g.hT[:, 4 + j, lo:], yc[:, lo:], g.parts[:, T_ZC + j, lo:], ALU.mult))
                for n, (j, (c0, cn)) in enumerate(jobs):
                    dve.wait_ge(full, n + 1)
                    dve.scalar_tensor_tensor(g.hT[:, 6 + j, c0:c0 + cn], ps[:, n % 2, 0:cn],
                                             g.pb[:, PB_PS + l * 2 + j:PB_PS + l * 2 + j + 1],
                                             g.parts[:, T_ZP + j, c0:c0 + cn], ALU.mult, ALU.mult).then_inc(y_done, 1)

            @block.tensor
            def _(pe):
                pe.wait_ge(loaded, 16 * (len(streams) + 4))
                for n, (j, (c0, cn)) in enumerate(jobs):
                    pe.wait_ge(d_done, j + 1)
                    if n >= 2:
                        pe.wait_ge(y_done, n - 1)
                    accumulate(nc, ps[:, n % 2, 0:cn], [(pw[:, j, :], dd[:, j, c0:c0 + cn])]).then_inc(full, 1)


def project_out(nc, g, l, jobs):
    io = g.io
    with Phase(nc, f"po{l}") as ph:
        w = g.wo
        gate = ph.sb("gate", [P, 2, D])
        x = ph.sb("x", [P, 2, D])
        y = ph.sb("y", [P, 2, D])
        acc = ph.ps("acc", [P, 2, 2, BANK])
        loaded = ph.sem("loaded")
        x_in = [ph.sem(f"x_in{j}") for j in range(2)]
        stored = [ph.sem(f"stored{j}") for j in range(2)]
        multiplied, y_done, out_done = ph.sem("multiplied"), ph.sem("y_done"), ph.sem("out_done")
        tiles = [(src[t * P:(t + 1) * P, :], dst[t * P:(t + 1) * P, :], s, col + t * P)
                 for src, dst, s, col, n in jobs for t in range(n)]
        with nc.Block() as block:
            @block.sync
            def _(sp):
                for s in range(2):
                    a = (48 + l * 24 + 16) * P
                    sp.dma_start(gate[:, s, :], spread(g.modrow[s, a:a + D])).then_inc(loaded, 16)
                for n, (src, _, _, _) in enumerate(tiles):
                    if n >= 2:
                        sp.wait_ge(out_done, n - 1)
                    sp.dma_start(x[:, n % 2, :], src).then_inc(x_in[n % 2], 16)

            @block.gpsimd
            def _(pool):
                for n, (_, dst, _, _) in enumerate(tiles):
                    pool.wait_ge(out_done, n + 1)
                    pool.dma_start(dst, y[:, n % 2, :]).then_inc(stored[n % 2], 16)
                for j in range(2):
                    pool.wait_ge(stored[j], 8 * len(tiles))

            @block.tensor
            def _(pe):
                pe.wait_ge(g.wo_in, 16)
                for n, (_, _, _, col) in enumerate(tiles):
                    if n >= 2:
                        pe.wait_ge(y_done, n - 1)
                    for c in range(2):
                        mm = accumulate(nc, acc[:, n % 2, c, :], [
                            (g.hT[:, k, col:col + P], w[:, k, c * BANK:(c + 1) * BANK]) for k in range(KD)])
                    mm.then_inc(multiplied, 1)

            @block.vector
            def _(dve):
                dve.wait_ge(loaded, 32)
                for n, (_, _, s, _) in enumerate(tiles):
                    j = n % 2
                    dve.wait_ge(multiplied, n + 1)
                    if n >= 2:
                        dve.wait_ge(stored[j], 16 * (n // 2))
                    dve.tensor_tensor(y[:, j, :], acc[:, j].rearrange("p c n -> p (c n)"), gate[:, s, :],
                                      ALU.mult).then_inc(y_done, 1)
                    dve.wait_ge(x_in[j], 16 * (n // 2 + 1))
                    dve.wait_ge(y_done, n + 1)
                    dve.tensor_tensor(y[:, j, :], y[:, j, :], x[:, j, :], ALU.add).then_inc(out_done, 1)


def layer(nc, g, l, sb):
    last = l == 1
    x, xc = (g.xb, g.xcb) if last else (g.xa, g.io["ctx_2"])
    streams = [("lat", N_CTX, N_LAT)] if last else [("ctx", 0, N_CTX), ("lat", N_CTX, N_LAT)]
    with ExitStack() as outer:
        g.parts = sb("parts", [P, D_IN2 // P, N_ALL], outer, tag=f"l{l}")
        flat = g.parts[:].rearrange("p t n -> p (t n)")
        with ExitStack() as projecting:
            high, g.hT_low = (sb(n, [P, KD, N_ALL], projecting, dt=FR, tag=f"l{l}") for n in ("h_high", "h_low"))
            g.hT = high
            normed_transposed(nc, g, f"n2{l}", [(xc, CT // 2, 1, 0), (x, LT // 2, 0, N_CTX)],
                              g.pb[:, PB_NORM + l * KD:PB_NORM + (l + 1) * KD], g.mod2, l * 24, l * 24 + KD,
                              g.hT, g.hT_low, flat)
            parts_of(nc, g, l, last)
        g.hT = sb("o", [P, KD, N_ALL], outer, tag=f"l{l}")
        queries_keys(nc, g, l, last)
        attention_2(nc, g, l, last)
        for name, _, _ in streams:
            fourier(nc, g, l, name)
        with Phase(nc, f"wo{l}") as wo:
            g.wo, g.wo_in = flat[:, 0:KD * D].rearrange("p (k n) -> p k n", n=D), wo.sem("wo_in")
            conv_pool(nc, g, l, streams)
            if last:
                project_out(nc, g, l, [(x, g.out.rearrange("b n d -> (b n) d"), 0, N_CTX, LT)])
            else:
                project_out(nc, g, l, [(xc, g.xcb, 1, 0, CT), (x, g.xb, 0, N_CTX, LT)])


class Shared:
    pass


def program(nc, io, out):
    g = Shared()
    g.io, g.out = io, out
    with ExitStack() as whole:
        def sb(name, shape, stack=whole, dt=F32, tag="g"):
            return stack.enter_context(nc.sbuf_tensor(f"{tag}_{name}", shape, dt))

        def dram(name, shape, dt=F32):
            return nc.dram_tensor("g_" + name, shape, dt).ap()

        g.ident, g.rev, g.ones, g.block64, g.rot = (sb(n, [P, P]) for n in ("ident", "rev", "ones", "block64", "rot"))
        g.causal = sb("causal", [P, 2, P])
        g.pa = sb("pa", [P, P])
        g.pb = sb("pb", [P, P])
        g.mod1 = sb("mod1", [P, 2, 48])
        g.mod2 = sb("mod2", [P, 2, 48])
        g.modrow = dram("modrow", [2, 96 * P])
        g.y_dram = dram("y_dram", [HEADS, P, N_LAT])
        g.xm_dram = dram("xm_dram", [KD, P, W_PAD])
        g.xc_dram = dram("xc_dram", [KD, P, N_ALL])
        g.bd_dram = dram("bd_dram", [KD, P, 3, P])
        g.col_dram = dram("col_dram", [ML_HEADS, P, NT, 6, 2])
        g.m_dram = dram("m_dram", [KD, P, N_LAT])
        g.x1 = dram("x1", [N_LAT, D])
        g.h2 = dram("h2", [N_LAT, D])
        g.moe = dram("moe", [N_LAT, D])
        g.xa = dram("xa", [N_LAT, D])
        g.xb = dram("xb", [N_LAT, D])
        g.xcb = dram("xcb", [N_CTX, D])
        modulation(nc, g)
        with ExitStack() as first:
            g.hT = sb("hT", [P, KD, N_ALL], first)
            normed_transposed(nc, g, "n1", [(io["ctx"], CT // 2, 1, 0), (io["x"], LT // 2, 0, N_CTX)],
                              g.pa[:, PA_NORM1:PA_NORM1 + KD], g.mod1, 0, KD, g.hT)
            with ExitStack() as att:
                g.ql = sb("ql", [P, QL, N_LAT], att)
                g.kl = sb("kl", [P, KL, N_ALL], att)
                g.kpe_hi = sb("kpe_hi", [P, N_ALL], att, FR)
                g.kpe_lo = sb("kpe_lo", [ROPE, N_ALL], att, FR)
                g.cos = sb("cos", [P, N_LAT], att)
                g.sin = sb("sin", [P, N_LAT], att)
                latents(nc, g)
                g.yT = sb("yT", [P, HEADS, N_LAT], att)
                attention(nc, g)
                gate_attention(nc, g)
            with ExitStack() as ml:
                g.gts = sb("gts", [P, NT, 16], ml)
                g.cols = sb("cols", [P, NT, 6, 4, 2], ml)
                with ExitStack() as inn:
                    g.xm = sb("xm", [P, KD, W_PAD], inn)
                    g.xc = sb("xc", [P, KD, N_ALL], inn)
                    g.dense = sb("dense", [P, 3, KD, 4], inn)
                    g.block4 = sb("block4", [P, P], inn)
                    g.wg = sb("wg", [P, 3 * KD, 16], inn)
                    g.bg = sb("bg", [P, 16], inn)
                    inner(nc, g)
                    gates(nc, g)
                gate_rows(nc, g)
            g.hs = sb("hs", [P, LT, D], first)
            mlstm(nc, g)
            readout(nc, g)
        with ExitStack() as moe:
            g.affT = sb("affT", [N_EXP, N_LAT], moe)
            g.gval = sb("gval", [P, N_EXP], moe)
            g.gidx = sb("gidx", [P, N_EXP], moe, U32)
            merge(nc, g)
            with Phase(nc, "wts") as wts:
                g.we = wts.sb("we", [P, 6, KD, BANK])
                g.we_in = [wts.sem(f"we_in{s}") for s in range(6)]
                route(nc, g)
                experts(nc, g)
        moe_out(nc, g)
        for l in range(2):
            layer(nc, g, l, sb)


_IN = ["x", "c", "ctx", "c_ctx", "w_mod", "b_mod", "norm1", "w_in", "q_norm", "w_uq", "kv_norm", "w_ukv", "conv_w",
       "conv_b", "w_qblk", "w_kblk", "w_vblk", "w_gate", "b_gate", "ml_norm", "ml_skip", "w_out", "norm2", "w_router",
       "w_e_gate", "w_e_up", "w_e_down", "final_norm", "c_2", "ctx_2", "c_ctx_2", "w_mod_2", "b_mod_2", "norm_g_2",
       "w_in_2", "q_gain_2", "k_gain_2", "w_fourier_2", "conv_w_2", "conv_b_2", "pool_w_2", "pool_scale_2", "w_out_2"]
_FLAT = {"c", "b_mod", "norm1", "q_norm", "kv_norm", "conv_w", "conv_b", "b_gate", "ml_norm", "ml_skip", "norm2",
         "c_2", "b_mod_2", "norm_g_2", "conv_w_2", "conv_b_2", "pool_scale_2"}
_DROP = {"x", "ctx", "w_mod", "w_in", "w_uq", "w_ukv", "w_qblk", "w_kblk", "w_vblk", "w_gate", "w_out", "w_router",
         "w_e_gate", "w_e_up", "w_e_down", "ctx_2"}


def kernel(**inputs):
    import concourse.bacc as bacc
    from concourse.bass_utils import run_bass_kernel_spmd

    nc = bacc.Bacc("TRN2", target_bir_lowering=False, num_devices=1)
    arrays, io = {}, {}

    def give(name, a):
        arrays[f"in_{name}"] = a
        io[name] = nc.dram_tensor(f"in_{name}", a.shape, mybir.dt.from_np(a.dtype), kind="ExternalInput").ap()

    for name in _IN:
        a = np.ascontiguousarray(inputs[name])
        give(name, a.reshape(-1) if name in _FLAT else a.reshape(a.shape[1:]) if name in _DROP else a)
    for name, a in tables().items():
        give("t_" + name, a)
    out = nc.dram_tensor("out", (1, N_LAT, D), F32, kind="ExternalOutput").ap()
    program(nc, io, out)
    r = run_bass_kernel_spmd(nc, [arrays], core_ids=[0])
    return r.results[0]["out"]
```
